# Optimizing a Trainium2 kernel written in Bass

```python
import jax, jax.numpy as jnp
from jax import lax
import numpy as np

D_MODEL = 1024
BATCH = 1
SEQ = 512
DEPTH = 2
DEC_BATCH = 8
DEC_SEQ = 4
PAST_LEN = 2048
PAGE_SIZE = 128

NSA_HEADS = 8
NSA_KV_HEADS = 2
NSA_GROUP = NSA_HEADS // NSA_KV_HEADS
NSA_HD = 64
CMP_LEN = 32
CMP_STRIDE = 16
CMP_HIDDEN = 128
SEL_LEN = 64
N_SEL = 8
WINDOW = 512
Q_BLOCK = 128
ROPE_DIMS = NSA_HD // 4
ROPE_THETA = 500000.0
ML_HEADS = 4
ML_HD = 128
ML_W = ML_HEADS * ML_HD
ML_CHUNK = 64
CONV_W = 4
XA_HEADS = 4
XA_HD = 64
N_MEM = 256
D_FF = 4 * D_MODEL
EPS = 1e-6
NSA_Q_W = NSA_HEADS * NSA_HD
NSA_KV_W = 6 * NSA_KV_HEADS * NSA_HD
NSA_G_W = 3 * NSA_HEADS
COL_SPLITS = (NSA_Q_W, NSA_KV_W, NSA_G_W, 2 * ML_W, ML_W, ML_W, 2 * ML_HEADS)
IN_W = sum(COL_SPLITS)
MIX_W = NSA_Q_W + ML_W

kernel_name = 'nsa_mlstm_hymba_decode_step'

def rms_norm(x, g):
    xf = x.astype(jnp.float32)
    y = xf * lax.rsqrt(jnp.mean(xf * xf, axis=-1, keepdims=True) + EPS)
    return (y * g.astype(jnp.float32)).astype(x.dtype)

def rope(x, pos):
    half = ROPE_DIMS // 2
    freqs = ROPE_THETA ** (-jnp.arange(half, dtype=jnp.float32) / half)
    ang = pos.astype(jnp.float32)[:, None] * freqs
    shape = (ang.shape[0],) + (1,) * (x.ndim - 3) + (half,)
    cos, sin = jnp.cos(ang).reshape(shape), jnp.sin(ang).reshape(shape)
    xf = x.astype(jnp.float32)
    x1, x2 = xf[..., :half], xf[..., half:ROPE_DIMS]
    out = jnp.concatenate([x1 * cos - x2 * sin, x2 * cos + x1 * sin, xf[..., ROPE_DIMS:]], axis=-1)
    return out.astype(x.dtype)

def masked_softmax(s, mask):
    s = jnp.where(mask, s.astype(jnp.float32), -jnp.inf)
    m = jnp.max(s, axis=-1, keepdims=True)
    m = jnp.where(jnp.isfinite(m), m, 0.0)
    e = jnp.exp(s - m)
    den = jnp.sum(e, axis=-1, keepdims=True)
    return e / jnp.where(den > 0, den, 1.0)

def split_cols(z):
    idx = np.cumsum(COL_SPLITS)[:-1].tolist()
    return jnp.split(z, idx, axis=-1)

def nsa_prepare(z_q, z_kv, z_g, pos, qn_g, kn_g):
    B, T = z_q.shape[:2]
    q = rope(rms_norm(z_q.reshape(B, T, NSA_HEADS, NSA_HD), qn_g), pos)
    kv = z_kv.reshape(B, T, 3, 2, NSA_KV_HEADS, NSA_HD)
    k = rope(rms_norm(kv[:, :, :, 0], kn_g[:, None, :]), pos)
    kvp = jnp.stack([k, kv[:, :, :, 1]], axis=3)
    gates = jax.nn.sigmoid(z_g.reshape(B, T, NSA_HEADS, 3).astype(jnp.float32))
    return q, kvp, gates

def compress(x, pos_emb, w1, w2):
    B, T, G, D = x.shape
    nc = (T - CMP_LEN) // CMP_STRIDE + 1
    r = CMP_LEN // CMP_STRIDE
    sub = x[:, :(nc + r - 1) * CMP_STRIDE].reshape(B, nc + r - 1, CMP_STRIDE, G, D)
    blocks = jnp.concatenate([sub[:, j:j + nc] for j in range(r)], axis=2)
    blocks = blocks + pos_emb[:, None, :]
    flat = blocks.transpose(0, 1, 3, 2, 4).reshape(B, nc, G, CMP_LEN * D)
    return jax.nn.silu(flat @ w1) @ w2

def sel_blocks(x):
    B, T, G, D = x.shape
    ns = -(-T // SEL_LEN)
    x = jnp.pad(x, ((0, 0), (0, ns * SEL_LEN - T), (0, 0), (0, 0)))
    return x.reshape(B, ns, SEL_LEN, G, D).transpose(0, 3, 1, 2, 4)

def nsa_attend(q, q_pos, gates, kc, vc, c_end, kb, vb, kw, vw, w_pos):
    B, Tq = q.shape[:2]
    G, HG, D = NSA_KV_HEADS, NSA_GROUP, NSA_HD
    scale = D ** -0.5
    qg = q.reshape(B, Tq, G, HG, D)
    s_c = jnp.einsum('btghd,bcgd->btghc', qg, kc) * scale
    m_c = (c_end[None, :] <= q_pos[:, None])[None, :, None, None, :]
    p_c = masked_softmax(s_c, m_c)
    o_c = jnp.einsum('btghc,bcgd->btghd', p_c.astype(vc.dtype), vc)
    NC, NS = kc.shape[1], kb.shape[2]
    ci = jnp.arange(NC)[:, None] * CMP_STRIDE
    sj = jnp.arange(NS)[None, :]
    cover = ((ci < (sj + 1) * SEL_LEN) & (ci + CMP_LEN > sj * SEL_LEN)).astype(jnp.float32)
    imp = jnp.einsum('btghc,cs->btgs', p_c, cover)
    cur = (q_pos // SEL_LEN)[:, None]
    forced = ((sj == cur) | (sj == 0))[None, :, None, :]
    future = (sj > cur)[None, :, None, :]
    imp = jnp.where(forced, jnp.inf, jnp.where(future, -jnp.inf, imp))
    n_top = min(N_SEL, NS)
    top_v, top_i = lax.top_k(imp, n_top)
    gather = jax.vmap(jax.vmap(lambda blk, ix: blk[ix]))
    idx = top_i.transpose(0, 2, 1, 3)
    ks = gather(kb, idx).reshape(B, G, Tq, n_top * SEL_LEN, D)
    vs = gather(vb, idx).reshape(B, G, Tq, n_top * SEL_LEN, D)
    kpos = (top_i[..., None] * SEL_LEN + jnp.arange(SEL_LEN)).reshape(B, Tq, G, n_top * SEL_LEN)
    valid = jnp.repeat(top_v > -jnp.inf, SEL_LEN, axis=-1)
    m_s = (valid & (kpos <= q_pos[None, :, None, None]))[:, :, :, None, :]
    s_s = jnp.einsum('btghd,bgtkd->btghk', qg, ks) * scale
    p_s = masked_softmax(s_s, m_s)
    o_s = jnp.einsum('btghk,bgtkd->btghd', p_s.astype(vs.dtype), vs)
    dpos = q_pos[:, None] - w_pos[None, :]
    m_w = ((dpos >= 0) & (dpos <= WINDOW) & (w_pos[None, :] >= 0))[None, :, None, None, :]
    s_w = jnp.einsum('btghd,bwgd->btghw', qg, kw) * scale
    p_w = masked_softmax(s_w, m_w)
    o_w = jnp.einsum('btghw,bwgd->btghd', p_w.astype(vw.dtype), vw)
    g = gates.reshape(B, Tq, G, HG, 3)
    o = g[..., 0:1] * o_c + g[..., 1:2] * o_s + g[..., 2:3] * o_w
    return o.reshape(B, Tq, G * HG * D).astype(q.dtype)

def nsa_prompt(q, kvp, gates, cmp_pos, cmp_w1, cmp_w2):
    B, T = q.shape[:2]
    kc = compress(kvp[:, :, 0, 0], cmp_pos[0], cmp_w1[0], cmp_w2[0])
    vc = compress(kvp[:, :, 0, 1], cmp_pos[1], cmp_w1[1], cmp_w2[1])
    c_end = jnp.arange(kc.shape[1], dtype=jnp.int32) * CMP_STRIDE + CMP_LEN - 1
    kb, vb = sel_blocks(kvp[:, :, 1, 0]), sel_blocks(kvp[:, :, 1, 1])
    pad = ((0, 0), (WINDOW, 0), (0, 0), (0, 0))
    kw, vw = jnp.pad(kvp[:, :, 2, 0], pad), jnp.pad(kvp[:, :, 2, 1], pad)
    span = WINDOW + Q_BLOCK

    def block(i):
        q0 = i * Q_BLOCK
        sl = lambda a, n: lax.dynamic_slice_in_dim(a, q0, n, axis=1)
        q_pos = q0 + jnp.arange(Q_BLOCK, dtype=jnp.int32)
        w_pos = q0 - WINDOW + jnp.arange(span, dtype=jnp.int32)
        return nsa_attend(sl(q, Q_BLOCK), q_pos, sl(gates, Q_BLOCK), kc, vc, c_end, kb, vb,
                          sl(kw, span), sl(vw, span), w_pos)

    o = lax.map(block, jnp.arange(T // Q_BLOCK, dtype=jnp.int32))
    return jnp.moveaxis(o, 0, 1).reshape(B, T, -1)

def nsa_sample(q, kvp, gates, pos, past_rows, win_buf, cmp_pos, cmp_w1, cmp_w2):
    DB, DS = q.shape[:2]
    new_rows = kvp[:, :, :2].reshape(DB, DS, 4, NSA_KV_HEADS, NSA_HD)
    full = jnp.concatenate([past_rows, new_rows], axis=1)
    kc = compress(full[:, :, 0], cmp_pos[0], cmp_w1[0], cmp_w2[0])
    vc = compress(full[:, :, 1], cmp_pos[1], cmp_w1[1], cmp_w2[1])
    c_end = jnp.arange(kc.shape[1], dtype=jnp.int32) * CMP_STRIDE + CMP_LEN - 1
    kb, vb = sel_blocks(full[:, :, 2]), sel_blocks(full[:, :, 3])
    WB = win_buf.shape[1]
    wfull = jnp.concatenate([win_buf, kvp[:, :, 2]], axis=1)
    w_pos = pos[0] - WB + jnp.arange(WB + DS, dtype=jnp.int32)
    o = nsa_attend(q, pos, gates, kc, vc, c_end, kb, vb, wfull[:, :, 0], wfull[:, :, 1], w_pos)
    return o, new_rows, wfull[:, -WB:]

def causal_conv(x, buf, w, b):
    T = x.shape[1]
    xp = jnp.concatenate([buf, x], axis=1)
    y = sum(xp[:, j:j + T] * w[j] for j in range(CONV_W)) + b
    return y, xp[:, -(CONV_W - 1):]

def mlstm_prepare(z_qk, z_v, z_if, conv_buf, conv_w, conv_b, gate_b):
    B, T = z_qk.shape[:2]
    qk, new_buf = causal_conv(z_qk, conv_buf, conv_w, conv_b)
    qk = jax.nn.silu(qk).astype(jnp.float32)
    heads = lambda a: a.reshape(B, T, ML_HEADS, ML_HD).transpose(0, 2, 1, 3)
    q = heads(qk[..., :ML_W])
    k = heads(qk[..., ML_W:]) * (ML_HD ** -0.5)
    v = heads(z_v.astype(jnp.float32))
    g = (z_if.astype(jnp.float32) + gate_b.astype(jnp.float32)).transpose(0, 2, 1)
    li = g[:, :ML_HEADS]
    lf = jax.nn.log_sigmoid(g[:, ML_HEADS:])
    return (q, k, v, li, lf), new_buf

def mlstm_chunk(state, inp):
    C, n, m = state
    q, k, v, li, lf = inp
    L = q.shape[2]
    b = jnp.cumsum(lf, axis=-1)
    causal = jnp.tril(jnp.ones((L, L), dtype=bool))
    Dm = jnp.where(causal, b[..., :, None] - b[..., None, :] + li[..., None, :], -jnp.inf)
    inter = b + m[..., None]
    m_t = jnp.maximum(inter, jnp.max(Dm, axis=-1))
    W = jnp.exp(Dm - m_t[..., None])
    a = jnp.exp(inter - m_t)
    Wqk = W * jnp.einsum('bhtd,bhsd->bhts', q, k)
    num = a[..., None] * jnp.einsum('bhvk,bhtk->bhtv', C, q) + jnp.einsum('bhts,bhsv->bhtv', Wqk, v)
    den = a * jnp.einsum('bhk,bhtk->bht', n, q) + jnp.sum(Wqk, axis=-1)
    h = num / jnp.maximum(jnp.abs(den), jnp.exp(-m_t))[..., None]
    m_new = m_t[..., -1]
    wgt = jnp.exp(b[..., -1:] - b + li - m_new[..., None])
    decay = jnp.exp(b[..., -1] + m - m_new)
    C_new = decay[..., None, None] * C + jnp.einsum('bhs,bhsv,bhsk->bhvk', wgt, v, k)
    n_new = decay[..., None] * n + jnp.einsum('bhs,bhsk->bhk', wgt, k)
    return (C_new, n_new, m_new), h

def mlstm_sequence(inp, state):
    T = inp[0].shape[2]
    nch = T // ML_CHUNK

    def chunks(a):
        a = a.reshape(a.shape[:2] + (nch, ML_CHUNK) + a.shape[3:])
        return jnp.moveaxis(a, 2, 0)

    state, h = lax.scan(mlstm_chunk, state, tuple(chunks(a) for a in inp))
    h = jnp.moveaxis(h, 0, 2)
    return state, h.reshape(h.shape[:2] + (T, ML_HD))

def mlstm_output(h, z_o, hn_g):
    B, NH, T, DV = h.shape
    h = rms_norm(h.transpose(0, 2, 1, 3), hn_g).reshape(B, T, NH * DV)
    return (h * jax.nn.sigmoid(z_o.astype(jnp.float32))).astype(z_o.dtype)

def memory_kv(mem, g, wkv, kn_g):
    B, M, _ = mem.shape
    z = (rms_norm(mem, g) @ wkv).reshape(B, M, 2, XA_HEADS, XA_HD)
    return jnp.stack([rms_norm(z[:, :, 0], kn_g), z[:, :, 1]], axis=2)

def cross_attn(xn, mkv, wq, qn_g, wo):
    B, T, _ = xn.shape
    q = rms_norm((xn @ wq).reshape(B, T, XA_HEADS, XA_HD), qn_g)
    s = jnp.einsum('bthd,bmhd->bhtm', q, mkv[:, :, 0]).astype(jnp.float32) * (XA_HD ** -0.5)
    p = jax.nn.softmax(s, axis=-1).astype(xn.dtype)
    o = jnp.einsum('bhtm,bmhd->bthd', p, mkv[:, :, 1])
    return o.reshape(B, T, XA_HEADS * XA_HD) @ wo

def sq_relu_mlp(xn, w1, w2):
    return jnp.square(jax.nn.relu(xn @ w1)) @ w2

def setup_inputs(seed: int = 0) -> dict:
    key = jax.random.key(seed)
    ks = iter(jax.random.split(key, 48))
    f32 = jnp.float32

    def nrm(shape, scale):
        return jax.random.normal(next(ks), shape, f32) * scale

    n_pages = PAST_LEN // PAGE_SIZE
    n_pool = (DEC_BATCH * n_pages * 5) // 4
    wbuf = min(WINDOW, PAST_LEN)
    G, D = NSA_KV_HEADS, NSA_HD
    x_prompt = nrm((BATCH, SEQ, D_MODEL), 1.0)
    x_sample = nrm((DEC_BATCH, DEC_SEQ, D_MODEL), 1.0)
    mem_prompt = nrm((BATCH, N_MEM, D_MODEL), 1.0)
    cache_nsa_kv = nrm((n_pool, PAGE_SIZE, DEPTH, 4, G, D), 1.0)
    cache_win_kv = nrm((DEPTH, DEC_BATCH, wbuf, 2, G, D), 1.0)
    cache_mem_kv = nrm((DEPTH, DEC_BATCH, N_MEM, 2, XA_HEADS, XA_HD), 1.0)
    state_mlstm_C = nrm((DEPTH, DEC_BATCH, ML_HEADS, ML_HD, ML_HD), 0.1)
    state_mlstm_n = nrm((DEPTH, DEC_BATCH, ML_HEADS, ML_HD), 0.1)
    state_mlstm_m = nrm((DEPTH, DEC_BATCH, ML_HEADS), 0.5)
    state_conv = nrm((DEPTH, DEC_BATCH, CONV_W - 1, 2 * ML_W), 1.0)
    perm = jax.random.permutation(next(ks), n_pool)
    page_table = perm[:DEC_BATCH * n_pages].reshape(DEC_BATCH, n_pages).astype(jnp.int32)
    ml_gate_b = jnp.concatenate([nrm((DEPTH, ML_HEADS), 0.1), 3.0 + nrm((DEPTH, ML_HEADS), 0.5)], axis=-1)
    return {
        'x_prompt': x_prompt,
        'x_sample': x_sample,
        'mem_prompt': mem_prompt,
        'cache_nsa_kv': cache_nsa_kv,
        'cache_win_kv': cache_win_kv,
        'cache_mem_kv': cache_mem_kv,
        'state_mlstm_C': state_mlstm_C,
        'state_mlstm_n': state_mlstm_n,
        'state_mlstm_m': state_mlstm_m,
        'state_conv': state_conv,
        'page_table': page_table,
        'norm_mix_g': 1.0 + nrm((DEPTH, D_MODEL), 0.05),
        'w_in': nrm((DEPTH, D_MODEL, IN_W), D_MODEL ** -0.5),
        'nsa_qn_g': 1.0 + nrm((DEPTH, NSA_HD), 0.05),
        'nsa_kn_g': 1.0 + nrm((DEPTH, 3, NSA_HD), 0.05),
        'cmp_pos': nrm((DEPTH, 2, CMP_LEN, NSA_HD), 0.1),
        'cmp_w1': nrm((DEPTH, 2, CMP_LEN * NSA_HD, CMP_HIDDEN), (CMP_LEN * NSA_HD) ** -0.5),
        'cmp_w2': nrm((DEPTH, 2, CMP_HIDDEN, NSA_HD), CMP_HIDDEN ** -0.5),
        'ml_conv_w': nrm((DEPTH, CONV_W, 2 * ML_W), CONV_W ** -0.5),
        'ml_conv_b': nrm((DEPTH, 2 * ML_W), 0.02),
        'ml_gate_b': ml_gate_b,
        'ml_hn_g': 1.0 + nrm((DEPTH, ML_HD), 0.05),
        'w_out': nrm((DEPTH, MIX_W, D_MODEL), MIX_W ** -0.5),
        'norm_xa_g': 1.0 + nrm((DEPTH, D_MODEL), 0.05),
        'norm_mem_g': 1.0 + nrm((DEPTH, D_MODEL), 0.05),
        'xa_wq': nrm((DEPTH, D_MODEL, XA_HEADS * XA_HD), D_MODEL ** -0.5),
        'xa_wkv': nrm((DEPTH, D_MODEL, 2 * XA_HEADS * XA_HD), D_MODEL ** -0.5),
        'xa_qn_g': 1.0 + nrm((DEPTH, XA_HD), 0.05),
        'xa_kn_g': 1.0 + nrm((DEPTH, XA_HD), 0.05),
        'xa_wo': nrm((DEPTH, XA_HEADS * XA_HD, D_MODEL), (XA_HEADS * XA_HD) ** -0.5),
        'norm_mlp_g': 1.0 + nrm((DEPTH, D_MODEL), 0.05),
        'mlp_w1': nrm((DEPTH, D_MODEL, D_FF), D_MODEL ** -0.5),
        'mlp_w2': nrm((DEPTH, D_FF, D_MODEL), D_FF ** -0.5),
    }

def reference(x_prompt, x_sample, mem_prompt, cache_nsa_kv, cache_win_kv, cache_mem_kv,
              state_mlstm_C, state_mlstm_n, state_mlstm_m, state_conv, page_table,
              norm_mix_g, w_in, nsa_qn_g, nsa_kn_g, cmp_pos, cmp_w1, cmp_w2,
              ml_conv_w, ml_conv_b, ml_gate_b, ml_hn_g, w_out,
              norm_xa_g, norm_mem_g, xa_wq, xa_wkv, xa_qn_g, xa_kn_g, xa_wo,
              norm_mlp_g, mlp_w1, mlp_w2):
    f32 = jnp.float32
    B, T, _ = x_prompt.shape
    DB, DS, _ = x_sample.shape
    P = page_table.shape[1] * cache_nsa_kv.shape[1]
    pos_p = jnp.arange(T, dtype=jnp.int32)
    pos_s = P + jnp.arange(DS, dtype=jnp.int32)
    wkeep = min(WINDOW, T)
    xp, xs = x_prompt, x_sample
    nsa_p, nsa_s, win_p, win_s = [], [], [], []
    C_p, C_s, n_p, n_s, m_p, m_s = [], [], [], [], [], []
    cv_p, cv_s, mem_p = [], [], []
    for l in range(DEPTH):
        zq_p, zkv_p, zg_p, zqk_p, zv_p, zo_p, zif_p = split_cols(rms_norm(xp, norm_mix_g[l]) @ w_in[l])
        zq_s, zkv_s, zg_s, zqk_s, zv_s, zo_s, zif_s = split_cols(rms_norm(xs, norm_mix_g[l]) @ w_in[l])
        q, kvp, gt = nsa_prepare(zq_p, zkv_p, zg_p, pos_p, nsa_qn_g[l], nsa_kn_g[l])
        a_p = nsa_prompt(q, kvp, gt, cmp_pos[l], cmp_w1[l], cmp_w2[l])
        nsa_p.append(kvp[:, :, :2].reshape(B, T, 4, NSA_KV_HEADS, NSA_HD))
        win_p.append(kvp[:, T - wkeep:, 2])
        q, kvp, gt = nsa_prepare(zq_s, zkv_s, zg_s, pos_s, nsa_qn_g[l], nsa_kn_g[l])
        past = cache_nsa_kv[page_table, :, l].reshape(DB, P, 4, NSA_KV_HEADS, NSA_HD)
        a_s, rows_s, wbuf_s = nsa_sample(q, kvp, gt, pos_s, past, cache_win_kv[l], cmp_pos[l], cmp_w1[l], cmp_w2[l])
        nsa_s.append(rows_s)
        win_s.append(wbuf_s)
        inp, buf_p = mlstm_prepare(zqk_p, zv_p, zif_p, jnp.zeros((B, CONV_W - 1, 2 * ML_W), xp.dtype),
                                   ml_conv_w[l], ml_conv_b[l], ml_gate_b[l])
        st0 = (jnp.zeros((B, ML_HEADS, ML_HD, ML_HD), f32), jnp.zeros((B, ML_HEADS, ML_HD), f32),
               jnp.zeros((B, ML_HEADS), f32))
        (Cn, nn, mn), h = mlstm_sequence(inp, st0)
        b_p = mlstm_output(h, zo_p, ml_hn_g[l])
        C_p.append(Cn); n_p.append(nn); m_p.append(mn); cv_p.append(buf_p)
        inp, buf_s = mlstm_prepare(zqk_s, zv_s, zif_s, state_conv[l], ml_conv_w[l], ml_conv_b[l], ml_gate_b[l])
        st = (state_mlstm_C[l].astype(f32), state_mlstm_n[l].astype(f32), state_mlstm_m[l].astype(f32))
        (Cn, nn, mn), h = mlstm_chunk(st, inp)
        b_s = mlstm_output(h, zo_s, ml_hn_g[l])
        C_s.append(Cn); n_s.append(nn); m_s.append(mn); cv_s.append(buf_s)
        xp = xp + jnp.concatenate([a_p, b_p], axis=-1) @ w_out[l]
        xs = xs + jnp.concatenate([a_s, b_s], axis=-1) @ w_out[l]
        mkv_p = memory_kv(mem_prompt, norm_mem_g[l], xa_wkv[l], xa_kn_g[l])
        mem_p.append(mkv_p)
        xp = xp + cross_attn(rms_norm(xp, norm_xa_g[l]), mkv_p, xa_wq[l], xa_qn_g[l], xa_wo[l])
        xs = xs + cross_attn(rms_norm(xs, norm_xa_g[l]), cache_mem_kv[l], xa_wq[l], xa_qn_g[l], xa_wo[l])
        xp = xp + sq_relu_mlp(rms_norm(xp, norm_mlp_g[l]), mlp_w1[l], mlp_w2[l])
        xs = xs + sq_relu_mlp(rms_norm(xs, norm_mlp_g[l]), mlp_w1[l], mlp_w2[l])
    dt = xp.dtype
    return (xp, xs,
            jnp.stack(nsa_p, axis=2), jnp.stack(nsa_s, axis=2),
            jnp.stack(win_p), jnp.stack(win_s),
            jnp.stack(C_p).astype(dt), jnp.stack(C_s).astype(dt),
            jnp.stack(n_p).astype(dt), jnp.stack(n_s).astype(dt),
            jnp.stack(m_p).astype(dt), jnp.stack(m_s).astype(dt),
            jnp.stack(cv_p), jnp.stack(cv_s),
            jnp.stack(mem_p))


_drawn_inputs = setup_inputs


def setup_inputs(seed=0):
    import zlib

    import numpy as np

    out = dict(_drawn_inputs(seed))
    spreads = {}
    factors = {'nsa_qn_g': 6.984, 'norm_xa_g': 8.0, 'xa_qn_g': 8.0}
    for name, (base, spread) in spreads.items():
        noise = np.random.default_rng([zlib.crc32(name.encode()), seed]).standard_normal(out[name].shape)
        drawn = base * np.exp(spread * noise) if base else spread * noise
        out[name] = __import__('jax').numpy.asarray(drawn.astype(out[name].dtype))
    for name, factor in factors.items():
        out[name] = (out[name] * factor).astype(out[name].dtype)
    return out
```

```python
from contextlib import ExitStack

import numpy as np

import concourse.bass as bass
from concourse import mybir

F32 = mybir.dt.float32
I32 = mybir.dt.int32
ALU = mybir.AluOpType
ACT = mybir.ActivationFunctionType
AX = mybir.AxisListType

P = 128
D = 1024
KT = D // P
SEQ, DB, DS = 512, 8, 4
NS = DB * DS
TP = SEQ // P
TT = TP + 1
TOK = SEQ + NS
DEPTH = 2
PAST, PAGE = 2048, 128
NPG = PAST // PAGE
POOL = DB * NPG * 5 // 4
HEADS, G, HG, HD = 8, 2, 4, 64
CMP_LEN, STRIDE, HID = 32, 16, 128
J = CMP_LEN // 2
NC_P = (SEQ - CMP_LEN) // STRIDE + 1
NC_S = (PAST + DS - CMP_LEN) // STRIDE + 1
SELB = 64
WIN = 512
MH, MD = 4, 128
XH = 4
MEM = 256
MT = MEM // P
FF = 4 * D
EPS = 1e-6
NEG = -1.0e30
BIG = 1.0e30

ZQ, ZK, ZV, ZO, ZG, ZI = 0, 512, 1280, 1792, 2304, 2328
ZW = 2336
NZ = 512

PRM = {}
_at = 0
for _n, _w in (("qn", 64), ("kn", 192), ("hn", 128), ("xq", 64), ("xk", 64), ("cw", 32), ("cb", 8),
               ("bi", 1), ("bf", 1), ("w2", 128), ("pos", 32)):
    PRM[_n] = (_at, _at + _w)
    _at += _w
NPRM = _at

CST = {}
_at = 0
for _n, _w in (("id", 128), ("causal", 128), ("tri", 128), ("cos", 40), ("sin", 40), ("cma", 4 * NC_P),
               ("cmm", 4 * NC_P), ("new", 64), ("low", 4), ("ms", 32), ("ohb", 8), ("grp", 128), ("one", 1),
               ("xnew", 4)):
    CST[_n] = (_at, _at + _w)
    _at += _w
NCST = _at

CHUNKS = [(f"in{i}", NZ * KT) for i in range(4)] + [("in4", (ZW - 4 * NZ) * KT), ("qk0", 4096), ("qk1", 4096),
          ("cmpw", 4096), ("w_out0", 4096), ("w_out1", 4096), ("wkv", 4096), ("wqo", 4096)] \
    + [(f"w1_{i}", 4096) for i in range(8)] + [(f"w2_{i}", 4096) for i in range(8)]
CH_AT = {}
_at = 0
for _n, _w in CHUNKS:
    CH_AT[_n] = (_at, _w)
    _at += P * _w
WTOT = _at

ORDER = ["in0", "in1", "in2", "in3", "in4", "qk0", "qk1", "cmpw"] + [f"cmp{b}" for b in range(DB)] + ["cst"]
for _g in range(2):
    ORDER += [f"kT{2 * _g}", f"kT{2 * _g + 1}", f"win{_g}", f"v{2 * _g}", f"v{2 * _g + 1}"]
ORDER += ["w_out0", "w_out1", "wkv", "wqo", "mc0", "mc1"] + [f"w1_{i}" for i in range(8)] + [f"w2_{i}" for i in range(8)]
SLOT = {}
_free = [0, 1, 2, 3]
for _i, _n in enumerate(ORDER):
    if _n == "cmpw":
        SLOT[_n] = 3
        _rot = 0
    elif _n.startswith("cmp") or _n == "cst":
        SLOT[_n] = _rot % 3
        _rot += 1
    elif _i < ORDER.index("cmpw"):
        SLOT[_n] = _i % 4
    else:
        SLOT[_n] = (_i + 1) % 4
STAGE_OF = {}
for _n in ORDER:
    STAGE_OF[_n] = ("in" if _n[:2] in ("in", "qk") else "pcmp" if _n == "cmpw" else "compress" if _n.startswith("cmp") else
                    "mls" if _n == "cst" else "samp0" if _n in ("kT0", "kT1", "win0", "v0", "v1") else
                    "samp1" if _n in ("kT2", "kT3", "win1", "v2", "v3") else
                    "out" if _n.startswith("w_out") else "wkv" if _n == "wkv" else "wo" if _n == "wqo" else
                    "xs" if _n.startswith("mc") else "mlp1" if _n.startswith("w1") else "mlp2")
STAGES = ["norm1", "in", "post", "compress", "gates", "mlp_", "mls", "mfin", "prep", "pcmp", "att", "samp0", "samp1", "sfin",
          "mix", "out", "memld", "memn", "wkv", "memk", "memT", "norm2", "wq", "xprep", "xqT", "xatt", "xs", "xT", "wo",
          "norm3", "mlp1", "mlp2"]


def load_plan():
    before, last, at, issue = {}, {}, 0, {s: [] for s in STAGES}
    for n in ORDER:
        s = SLOT[n]
        before[n] = last.get(s)
        if s in last:
            at = max(at, STAGES.index(STAGE_OF[last[s]]))
        issue[STAGES[at]].append(n)
        last[s] = n
    return before, issue


def build(nc, din, dout):
    before, issue = load_plan()
    with ExitStack() as ctx:
        sb = lambda name, shape, dt=F32: ctx.enter_context(nc.sbuf_tensor(name, shape, dt))
        whole = lambda name: ctx.enter_context(nc.semaphore(name))
        part = {"held": ExitStack(), "sems": []}

        def sem(name):
            s = part["held"].enter_context(nc.semaphore(name))
            part["sems"].append(s)
            return s

        def clear(more=()):
            with nc.Block() as block:
                @block.gpsimd
                def _(pool):
                    for s in part["sems"] + list(more):
                        pool.sem_clear(s)
            part["held"].close()
            part["held"], part["sems"] = ExitStack(), []

        x = sb("x", [P, TT, D])
        hT = sb("hT", [P, KT, TT * P])
        ring = sb("ring", [P, 4, 4096])
        arena = sb("arena", [P, TT * ZW + 2 * KT * TOK])
        hn = sb("hn", [P, 2, D])
        gain = sb("gain", [P, D])
        prm = sb("prm", [P, NPRM])
        cst = sb("cst", [P, NCST])
        stat = sb("stat", [P, 160])
        cols = sb("cols", [P, 96])
        pages = sb("pages", [1, DB * NPG], I32)
        ps = ctx.enter_context(nc.psum_tensor("ps", [P, 8, 512], F32))

        z = arena[:, 0:TT * ZW].rearrange("p (t w) -> p t w", t=TT)
        _o = TT * ZW
        zqkT = arena[:, _o:_o + KT * TOK].rearrange("p (c t) -> p c t", c=KT)
        qkT = arena[:, _o + KT * TOK:_o + 2 * KT * TOK].rearrange("p (c t) -> p c t", c=KT)
        hTf = hT[:, :, :].rearrange("p k t -> p (k t)")
        ropf = arena[:, _o:_o + KT * TOK]
        qkf = arena[:, _o + KT * TOK:_o + 2 * KT * TOK]

        def pr(n, rows=P):
            return prm[0:rows, PRM[n][0]:PRM[n][1]]

        def cs(n, rows=P):
            return cst[0:rows, CST[n][0]:CST[n][1]]

        ident = cs("id")
        loaded = [whole(f"slot_loaded{i}") for i in range(4)]
        dmas_in_slot = [0] * 4
        loaded_at = {}
        for n in ORDER:
            k = 2 * NPG if n[:2] == "kT" or (n[0] == "v") else NPG if n[:3] == "cmp" and n != "cmpw" else \
                8 if n[:3] == "win" else 1
            dmas_in_slot[SLOT[n]] += 16 * k
            loaded_at[n] = dmas_in_slot[SLOT[n]]

        def slot(n):
            return ring[:, SLOT[n], :]

        def arrived(eng, n):
            eng.wait_ge(loaded[SLOT[n]], loaded_at[n])

        def chain(eng, name):
            s, count = sem(name), [0]

            def link(ins):
                count[0] += 1
                ins.then_inc(s, 1)
                eng.wait_ge(s, count[0])
            return link

        def fill(sp, stage, l, read={}):
            for n in issue.get(stage, ()):
                s = SLOT[n]
                if before[n] and STAGE_OF[before[n]] == stage:
                    sp.wait_ge(*read[before[n]])
                dst = ring[:, s, :]
                if n in CH_AT:
                    at, w = CH_AT[n]
                    src = din["wst"][bass.ds(l, 1), at:at + P * w].rearrange("a (p w) -> (a p) w", p=P)
                    sp.dma_start(dst[:, 0:w], src).then_inc(loaded[s], 16)
                elif n == "cst":
                    sp.dma_start(dst, din["cT"][bass.ds(l, 1)].rearrange("a p w -> (a p) w")).then_inc(loaded[s], 16)
                elif n[:2] == "mc":
                    g = int(n[2:])
                    src = din["mkv"][bass.ds(l * 2 + g, 1)].rearrange("a p w -> (a p) w")
                    sp.dma_start(dst, src).then_inc(loaded[s], 16)
                elif n[:3] == "win":
                    g = int(n[3:])
                    for b in range(4):
                        src = din["winT"][bass.ds(l * DB + 4 * g + b, 1)].rearrange("a p w -> (a p) w")
                        sp.dma_start(dst[:, 512 * b:512 * b + 512], src).then_inc(loaded[s], 16)
                        src = din["win"][bass.ds(l * DB + 4 * g + b, 1), :, 128:256]
                        src = src.rearrange("a (t p) c -> p (a t) c", p=P)
                        sp.dma_start(dst[:, 2048 + 512 * b:2560 + 512 * b].rearrange("p (t c) -> p t c", t=4),
                                     src).then_inc(loaded[s], 16)
                else:
                    name, first, w = (("cx", NPG * int(n[3:]), 256) if n[:3] == "cmp" else
                                      ("kx", 2 * NPG * int(n[2:]), 128) if n[:2] == "kT" else
                                      ("vx", 2 * NPG * int(n[1:]), 128))
                    with sp.Fori(0, 4096 // w) as i:
                        page = sp.value_load(pages[0:1, bass.ds(i + first, 1)], min_val=0, max_val=POOL - 1)
                        src = din[name][bass.ds(page + l * POOL, 1)].rearrange("a p w -> (a p) w")
                        sp.dma_start(dst[:, bass.ds(i * w, w)], src).then_inc(loaded[s], 16)

        def norm_stage(stage, l, src, tiles, gain_i):
            g_ld, ssq, msq, rt, hn_ok, tp, ea, ed = [sem(f"{stage}_{n}") for n in
                ("gain_loaded", "squares", "mean", "root", "rows_ready", "turned", "copied_a", "copied_d")]
            with nc.Block() as block:
                @block.sync
                def _(sp):
                    g = din["gains"][bass.ds(l * 4 + gain_i, 1)].rearrange("a p w -> (a p) w")
                    sp.dma_start(gain[:, :], g).then_inc(g_ld, 16)
                    fill(sp, stage, l)

                @block.scalar
                def _(act):
                    link = chain(act, f"{stage}_act")
                    for t in range(tiles):
                        link(nc.scalar.activation(hn[:, 0, :], src[:, t, :], ACT.Square, accum_out=stat[:, t:t + 1]))
                    nc.scalar.activation(stat[:, 8:8 + tiles], stat[:, 0:tiles], ACT.Copy).then_inc(ssq, 1)
                    act.wait_ge(msq, 1)
                    nc.scalar.activation(stat[:, 24:24 + tiles], stat[:, 16:16 + tiles], ACT.Sqrt).then_inc(rt, 1)
                    for t in range(tiles):
                        act.wait_ge(tp, 2 * t + 1)
                        b = 2 * (t % 4)
                        nc.scalar.copy(hT[:, 0:4, t * P:t * P + P], ps[:, b, :].rearrange("p (k t) -> p k t", k=4))\
                            .then_inc(ea, 1)

                @block.vector
                def _(dve):
                    link = chain(dve, f"{stage}_dve")
                    dve.wait_ge(ssq, 1)
                    nc.vector.tensor_scalar(stat[:, 16:16 + tiles], stat[:, 8:8 + tiles], 1.0 / D, EPS, ALU.mult,
                                            ALU.add).then_inc(msq, 1)
                    dve.wait_ge(rt, 1)
                    link(nc.vector.reciprocal(stat[:, 32:32 + tiles], stat[:, 24:24 + tiles]))
                    dve.wait_ge(g_ld, 16)

                    def rows(t):
                        if t >= 2:
                            dve.wait_ge(tp, 2 * t - 2)
                        nc.vector.scalar_tensor_tensor(out=hn[:, t % 2, :], in0=src[:, t, :],
                                                       scalar=stat[:, 32 + t:33 + t], in1=gain[:, :],
                                                       op0=ALU.mult, op1=ALU.mult).then_inc(hn_ok, 1)
                    rows(0)
                    for t in range(tiles):
                        if t + 1 < tiles:
                            rows(t + 1)
                        dve.wait_ge(tp, 2 * t + 2)
                        b = 2 * (t % 4) + 1
                        nc.vector.tensor_copy(hT[:, 4:8, t * P:t * P + P], ps[:, b, :].rearrange("p (k t) -> p k t", k=4))\
                            .then_inc(ed, 1)

                @block.tensor
                def _(pe):
                    for t in range(tiles):
                        pe.wait_ge(hn_ok, t + 1)
                        if t >= 4:
                            pe.wait_ge(ea, t - 3)
                            pe.wait_ge(ed, t - 3)
                        for k in range(8):
                            ins = nc.tensor.transpose(ps[:, 2 * (t % 4) + k // 4, (k % 4) * P:(k % 4) * P + P],
                                                      hn[:, t % 2, k * P:k * P + P], ident)
                            if k % 4 == 3:
                                ins.then_inc(tp, 1)

        def gemm_stage(stage, l, units):
            prod, ev = sem(f"{stage}_products"), {e: sem(f"{stage}_evicted_{e}") for e in "ad"}
            nth, cnt = [], {"a": 0, "d": 0}
            for u in units:
                cnt[u[2]] += 1
                nth.append(cnt[u[2]])
            with nc.Block() as block:
                @block.sync
                def _(sp):
                    fill(sp, stage, l, {u[4]: (prod, i + 1) for i, u in enumerate(units) if u[4]})

                @block.tensor
                def _(pe):
                    for i, (load, mms, e, _, _) in enumerate(units):
                        if load:
                            arrived(pe, load)
                        if i >= 8:
                            pe.wait_ge(ev[units[i - 8][2]], nth[i - 8])
                        for m, (out, a, b) in enumerate(mms):
                            ins = nc.tensor.matmul(out(ps[:, i % 8, :]), a, b, start=(m == 0), stop=(m == len(mms) - 1))
                        ins.then_inc(prod, 1)

                @block.scalar
                def _(act):
                    link = chain(act, f"{stage}_act")
                    for i, u in enumerate(units):
                        if u[2] == "a":
                            act.wait_ge(prod, i + 1)
                            u[3](link, nc.scalar, ps[:, i % 8, :]).then_inc(ev["a"], 1)

                @block.vector
                def _(dve):
                    link = chain(dve, f"{stage}_dve")
                    for i, u in enumerate(units):
                        if u[2] == "d":
                            dve.wait_ge(prod, i + 1)
                            u[3](link, nc.vector, ps[:, i % 8, :]).then_inc(ev["d"], 1)

        def copy_to(dst, n):
            def f(link, eng, bank):
                src = bank[:, 0:n]
                return nc.scalar.copy(dst, src) if eng is nc.scalar else nc.vector.tensor_copy(dst, src)
            return f

        def add_to(dst, n):
            return lambda link, eng, bank: nc.vector.tensor_tensor(dst, bank[:, 0:n], dst, ALU.add)

        def head_norm(link, heads, nh_total, act_go, dve_go, width):
            for v, _, c, scratch in heads:
                t, h = v.shape[1], v.shape[2]
                link(nc.vector.tensor_tensor(scratch, v, v, ALU.mult))
                link(nc.vector.tensor_reduce(stat[:, c:c + t * h].rearrange("p (t h) -> p t h", t=t), scratch,
                                             AX.X, ALU.add))
            nc.vector.tensor_scalar(stat[:, 0:nh_total], stat[:, 0:nh_total], 1.0 / width, EPS, ALU.mult,
                                    ALU.add).then_inc(dve_go, 1)
            nc.vector.wait_ge(act_go, 1)
            link(nc.vector.reciprocal(stat[:, 80:80 + nh_total], stat[:, 80:80 + nh_total]))
            for v, g, c, _ in heads:
                t, h, w = v.shape[1], v.shape[2], v.shape[3]
                r = stat[:, 80 + c:80 + c + t * h].rearrange("p (t h o) -> p t h o", t=t, o=1)
                link(nc.vector.tensor_tensor(v, v, r.to_broadcast([P, t, h, w]), ALU.mult))
                gg = g.rearrange("p (a b w) -> p a b w", a=1, b=1).to_broadcast([P, t, h, w])
                link(nc.vector.tensor_tensor(v, v, gg, ALU.mult))


        def input_projection(l):
            units = []
            for c in range(5):
                w = min(NZ, ZW - NZ * c)
                wt = slot(f"in{c}")[:, 0:w * KT].rearrange("p (k n) -> p k n", k=KT)
                for t in range(TT):
                    mms = [(lambda bank, w=w: bank[:, 0:w], hT[:, k, t * P:t * P + P], wt[:, k, :]) for k in range(KT)]
                    units.append((f"in{c}" if t == 0 else None, mms, "ad"[(c + t) % 2],
                                  copy_to(z[:, t, NZ * c:NZ * c + w], w), f"in{c}" if t == TT - 1 else None))
            for c in range(KT):
                name, q = f"qk{c // 4}", c % 4
                wt = slot(name).rearrange("p (k n) -> p k n", k=KT)
                for part, (a, w) in enumerate(((0, SEQ), (SEQ, NS))):
                    mms = [(lambda bank, w=w: bank[:, 0:w], wt[:, k, q * P:q * P + P], hT[:, k, a:a + w]) for k in range(KT)]
                    units.append((name if q == 0 and part == 0 else None, mms, "ad"[c % 2],
                                  copy_to(zqkT[:, c, a:a + w], w), name if q == 3 and part == 1 else None))
            gemm_stage("in", l, units)

        def post_stage(l):
            go, root, cv_ld, y0, y1, silu, dn, st_o = [sem(f"post_{n}") for n in
                ("squares", "root", "state_loaded", "conv_begun", "conv_done", "silu_done", "rows_done", "stored")]
            sq = hTf[:, 0:2560]
            tail = hTf[:, 2560:3008].rearrange("p (c b u) -> p c b u", c=KT, b=DB)
            held = hTf[:, 3008:3200]
            q = z[:, :, ZQ:ZQ + 512].rearrange("p t (h d) -> p t h d", h=HEADS)
            ks = [z[:, :, ZK + 256 * r:ZK + 256 * r + 128].rearrange("p t (h d) -> p t h d", h=G) for r in range(3)]
            heads = [(q, pr("qn"), 0, sq.rearrange("p (t h d) -> p t h d", t=TT, h=HEADS))]
            heads += [(ks[r], prm[:, PRM["kn"][0] + 64 * r:PRM["kn"][0] + 64 * r + 64], 40 + 10 * r,
                       sq[:, 0:640].rearrange("p (t h d) -> p t h d", t=TT, h=G)) for r in range(3)]
            with nc.Block() as block:
                @block.sync
                def _(sp):
                    src = din["convT"][bass.ds(l, 1)].rearrange("a p w -> (a p) w")
                    sp.dma_start(held, src).then_inc(cv_ld, 16)
                    fill(sp, "post", l)
                    sp.dma_start(dout["convT"][bass.ds(l, 1)].rearrange("a p c t -> (a p) c t"),
                                   zqkT[:, :, SEQ - 3:TOK]).then_inc(st_o, 16)
                    for b in range(DB):
                        sp.dma_start(dout["win_s"][bass.ds(l * DB + b, 1), 0:WIN - DS],
                                       din["win"][bass.ds(l * DB + b, 1), DS:WIN]).then_inc(st_o, 16)
                    sp.wait_ge(dn, 1)
                    sp.dma_start(dout["nsa_p"][bass.ds(l, 1)].rearrange("a p t c -> (a p) t c"),
                                   z[:, 0:TP, ZK:ZK + 512]).then_inc(st_o, 16)
                    sp.dma_start(dout["nsa_s"][bass.ds(l, 1)].rearrange("a r c -> (a r) c"),
                                   z[0:NS, TP, ZK:ZK + 512]).then_inc(st_o, 16)
                    sp.dma_start(dout["win_p"][bass.ds(l, 1)].rearrange("a p t c -> (a p) t c"),
                                   z[:, 0:TP, ZK + 512:ZK + 768]).then_inc(st_o, 16)
                    for b in range(DB):
                        sp.dma_start(dout["win_s"][bass.ds(l * DB + b, 1), WIN - DS:WIN].rearrange("a r c -> (a r) c"),
                                       z[4 * b:4 * b + 4, TP, ZK + 512:ZK + 768]).then_inc(st_o, 16)
                    sp.wait_ge(st_o, 16 * (4 + 2 * DB))

                @block.scalar
                def _(act):
                    link = chain(act, "post_act")
                    for c in range(KT):
                        w3 = PRM["cw"][0] + 4 * c + 3
                        nc.scalar.activation(qkT[:, c, 0:SEQ], zqkT[:, c, 0:SEQ], ACT.Identity,
                                             bias=prm[:, PRM["cb"][0] + c:PRM["cb"][0] + c + 1],
                                             scale=prm[:, w3:w3 + 1]).then_inc(y0, 1)
                    act.wait_ge(go, 1)
                    nc.scalar.activation(stat[:, 80:150], stat[:, 0:70], ACT.Sqrt).then_inc(root, 1)
                    link(nc.scalar.activation(z[:, :, ZO:ZI], z[:, :, ZO:ZI], ACT.Sigmoid))
                    for c in range(KT):
                        act.wait_ge(y1, c + 1)
                        nc.scalar.activation(qkT[:, c, :], qkT[:, c, :], ACT.Silu).then_inc(silu, 1)
                    act.wait_ge(silu, KT)

                @block.vector
                def _(dve):
                    link = chain(dve, "post_dve")
                    head_norm(link, heads, 70, root, go, HD)
                    cos = cs("cos").rearrange("p (t o f) -> p t o f", t=TT, o=1)
                    sin = cs("sin").rearrange("p (t o f) -> p t o f", t=TT, o=1)
                    for v, h in [(q, HEADS)] + [(k, G) for k in ks]:
                        a, b = v[:, :, :, 0:8], v[:, :, :, 8:16]
                        t = [sq[:, 320 * i:320 * i + TT * h * 8].rearrange("p (t h f) -> p t h f", t=TT, h=h) for i in range(4)]
                        cb, sb_ = cos.to_broadcast([P, TT, h, 8]), sin.to_broadcast([P, TT, h, 8])
                        link(nc.vector.tensor_tensor(t[0], a, cb, ALU.mult))
                        link(nc.vector.tensor_tensor(t[1], b, sb_, ALU.mult))
                        link(nc.vector.tensor_tensor(t[2], b, cb, ALU.mult))
                        link(nc.vector.tensor_tensor(t[3], a, sb_, ALU.mult))
                        link(nc.vector.tensor_tensor(a, t[0], t[1], ALU.subtract))
                        link(nc.vector.tensor_tensor(b, t[2], t[3], ALU.add))
                    nc.vector.tensor_copy(stat[:, 0:1], stat[:, 1:2]).then_inc(dn, 1)
                    dve.wait_ge(cv_ld, 16)
                    link(nc.vector.tensor_copy(tail[:, :, :, 0:3], held.rearrange("p (c b u) -> p c b u", c=KT, b=DB)))
                    link(nc.vector.tensor_copy(tail[:, :, :, 3:7],
                                               zqkT[:, :, SEQ:TOK].rearrange("p c (b u) -> p c b u", b=DB)))
                    for c in range(KT):
                        cw = PRM["cw"][0] + 4 * c
                        dve.wait_ge(y0, c + 1)
                        y = qkT[:, c, SEQ:TOK].rearrange("p (b u) -> p b u", b=DB)
                        for j in range(1, 4):
                            link(nc.vector.scalar_tensor_tensor(
                                out=qkT[:, c, j:SEQ], in0=zqkT[:, c, 0:SEQ - j], scalar=prm[:, cw + 3 - j:cw + 4 - j],
                                in1=qkT[:, c, j:SEQ], op0=ALU.mult, op1=ALU.add))
                        link(nc.vector.tensor_scalar(y, tail[:, c, :, 3:7], prm[:, cw + 3:cw + 4],
                                                     prm[:, PRM["cb"][0] + c:PRM["cb"][0] + c + 1], ALU.mult, ALU.add))
                        for j in range(3):
                            ins = nc.vector.scalar_tensor_tensor(out=y, in0=tail[:, c, :, j:j + 4],
                                                                 scalar=prm[:, cw + j:cw + j + 1], in1=y,
                                                                 op0=ALU.mult, op1=ALU.add)
                            if j < 2:
                                link(ins)
                        ins.then_inc(y1, 1)
                    dve.wait_ge(y1, KT)

        kc_s = hn[:, 0, :].rearrange("p (b c) -> p b c", b=DB)
        vc_s = hn[:, 1, :].rearrange("p (b c) -> p b c", b=DB)

        def compress_stage(stage, l, jobs, frees=None):
            prod, hid_ok, hid_used, pr2, ev2, bi, bi_ok = [sem(f"{stage}_{n}") for n in
                ("products", "hidden_ready", "hidden_read", "outputs", "evicted", "position_bias", "bias_ready")]
            w1 = slot("cmpw").rearrange("p (k j n) -> p k j n", k=2, j=J)
            pos = pr("pos").rearrange("p (k j) -> p k j", k=2)
            w2 = pr("w2").rearrange("p (k d) -> p k d", k=2)
            hid = hTf[:, 0:1024].rearrange("p (s c) -> p s c", s=2)
            with nc.Block() as block:
                @block.sync
                def _(sp):
                    fill(sp, stage, l, {j[0]: (prod, 2 * i + 2) for i, j in enumerate(jobs)} | {frees: (pr2, len(jobs))})

                @block.tensor
                def _(pe):
                    arrived(pe, "cmpw")
                    for k in range(2):
                        for j in range(J):
                            ins = nc.tensor.matmul(ps[:, 7, k:k + 1], w1[:, k, j, :], pos[:, k, j:j + 1],
                                                   start=(j == 0), stop=(j == J - 1))
                    ins.then_inc(bi, 1)

                    def second(i):
                        n = jobs[i][2]
                        o = 4 + i % 2
                        pe.wait_ge(hid_ok, 2 * i + 2)
                        if i >= 2:
                            pe.wait_ge(ev2, 2 * (i - 1))
                        h = hid[:, i % 2, 0:4 * n].rearrange("p (k g c) -> p k g c", k=2, g=G)
                        for g in range(G):
                            nc.tensor.matmul(ps[64 * g:64 * g + 64, o, 0:n], w2[:, 0, :], h[:, 0, g, :],
                                             start=True, stop=True)
                        for g in range(G):
                            ins = nc.tensor.matmul(ps[0:n, o, 128 + 64 * g:192 + 64 * g], h[:, 1, g, :], w2[:, 1, :],
                                                   start=True, stop=True)
                        ins.then_inc(pr2, 1)
                    for i, (load, tok, n, _, _) in enumerate(jobs):
                        if load:
                            arrived(pe, load)
                        if i >= 2:
                            pe.wait_ge(hid_ok, 2 * i - 2)
                        for k in range(2):
                            for j in range(J):
                                v = tok.rearrange("p q (k g) -> p k g q", k=2)[:, k, :, j:j + 8 * (n - 1) + 1:8]
                                ins = nc.tensor.matmul(ps[:, 2 * (i % 2) + k, 0:G * n], w1[:, k, j, :], v,
                                                       start=(j == 0), stop=(j == J - 1))
                            ins.then_inc(prod, 1)
                        if i:
                            second(i - 1)
                    second(len(jobs) - 1)

                @block.scalar
                def _(act):
                    act.wait_ge(bi_ok, 1)
                    for i, (_, _, n, _, _) in enumerate(jobs):
                        for k in range(2):
                            act.wait_ge(prod, 2 * i + k + 1)
                            if i >= 2 and k == 0:
                                act.wait_ge(pr2, i - 1)
                            nc.scalar.activation(hid[:, i % 2, 2 * k * n:2 * (k + 1) * n], ps[:, 2 * (i % 2) + k, 0:G * n],
                                                 ACT.Silu, bias=stat[:, 158 + k:159 + k]).then_inc(hid_ok, 1)

                @block.vector
                def _(dve):
                    dve.wait_ge(bi, 1)
                    nc.vector.tensor_copy(stat[:, 158:160], ps[:, 7, 0:2]).then_inc(bi_ok, 1)
                    for i, (_, _, n, kc, vc) in enumerate(jobs):
                        dve.wait_ge(pr2, i + 1)
                        nc.vector.tensor_copy(kc, ps[:, 4 + i % 2, 0:n]).then_inc(ev2, 1)
                        nc.vector.tensor_copy(vc, ps[0:n, 4 + i % 2, 128:256]).then_inc(ev2, 1)

        def sample_compress(l):
            compress_stage("compress", l, [
                (f"cmp{b}", slot(f"cmp{b}").rearrange("p (q w) -> p q w", w=4), NC_S, kc_s[:, b, 0:NC_S],
                 vc_s[0:NC_S, b, :]) for b in range(DB)])

        grow = gain[0:MH, 0:TOK]
        decay = gain[0:MH, TOK:TOK + DB]
        gcol = cols[:, 0:20].rearrange("p (t h) -> p t h", t=TT)
        emcol = cols[:, 20:40].rearrange("p (t h) -> p t h", t=TT)
        wscol, ascol = cols[0:NS, 40:44], cols[0:NS, 44:48]
        wpcol = cols[:, 48:64].rearrange("p (h t) -> p h t", h=MH)

        def gates_stage(l):
            tp, ev, ex, exd, rows_ok, tp2, ev2, m_ld, m_st = [sem(f"gates_{n}") for n in
                ("turned", "rows_in", "to_act", "from_act", "rows_ready", "columns", "columns_out", "m_loaded", "m_stored")]
            R = lambda i: hTf[0:MH, i * TOK:i * TOK + TOK]
            li, lf, ab, F, g, m, wg, av, zero = [R(i) for i in range(9)]
            m0 = cols[0:MH, 64:64 + DB]
            s4 = lambda r: r[:, SEQ:TOK].rearrange("p (b u) -> p b u", b=DB)
            with nc.Block() as block:
                @block.sync
                def _(sp):
                    sp.dma_start(m0, din["mT"][bass.ds(l, 1)].rearrange("a p w -> (a p) w")).then_inc(m_ld, 16)
                    fill(sp, "gates", l)
                    sp.wait_ge(rows_ok, 1)
                    sp.dma_start(dout["mT"][bass.ds(l, 1)].rearrange("a p w -> (a p) w"), m).then_inc(m_st, 16)
                    sp.wait_ge(m_st, 16)

                @block.tensor
                def _(pe):
                    for half in range(2):
                        for t in range(TT):
                            b = 2 * half + t // 4
                            ins = nc.tensor.transpose(ps[0:MH, b, (t % 4) * P:(t % 4) * P + P],
                                                      z[:, t, ZI + MH * half:ZI + MH * half + MH], ident)
                    ins.then_inc(tp, 1)
                    pe.wait_ge(rows_ok, 1)
                    i4 = ident[0:MH, 0:MH]
                    for n, r in enumerate((g, m)):
                        for t in range(TT):
                            w = P if t < TP else NS
                            nc.tensor.transpose(ps[0:w, 4, 20 * n + 4 * t:20 * n + 4 * t + 4], r[:, t * P:t * P + w], i4)
                    for n, r in enumerate((wg, av)):
                        ins = nc.tensor.transpose(ps[0:NS, 4, 40 + 4 * n:44 + 4 * n], r[:, SEQ:TOK], i4)
                    ins.then_inc(tp2, 1)

                @block.scalar
                def _(act):
                    link = chain(act, "gates_act")
                    act.wait_ge(ex, 1)
                    link(nc.scalar.activation(ab, lf, ACT.Abs))
                    link(nc.scalar.activation(ab, ab, ACT.Exp, scale=-1.0))
                    nc.scalar.activation(ab, ab, ACT.Ln, bias=1.0).then_inc(exd, 1)
                    act.wait_ge(ex, 2)
                    link(nc.scalar.activation(decay, decay, ACT.Exp))
                    link(nc.scalar.activation(wg[:, SEQ:TOK], wg[:, SEQ:TOK], ACT.Exp))
                    nc.scalar.activation(av[:, SEQ:TOK], av[:, SEQ:TOK], ACT.Exp).then_inc(exd, 1)
                    act.wait_ge(ev2, 2)
                    link(nc.scalar.activation(cols[:, 20:36], cols[:, 20:36], ACT.Exp, scale=-1.0))
                    link(nc.scalar.activation(cols[0:NS, 36:40], cols[0:NS, 36:40], ACT.Exp, scale=-1.0))

                @block.vector
                def _(dve):
                    link = chain(dve, "gates_dve")
                    link(nc.vector.memset(zero, 0.0))
                    link(nc.vector.memset(cols[:, 16:20], 0.0))
                    link(nc.vector.memset(cols[:, 36:40], 0.0))
                    dve.wait_ge(tp, 1)
                    for half, (r, b) in enumerate(((li, "bi"), (lf, "bf"))):
                        link(nc.vector.tensor_scalar(r[:, 0:SEQ], ps[0:MH, 2 * half, :], pr(b, MH), None, ALU.add))
                        link(nc.vector.tensor_scalar(r[:, SEQ:TOK], ps[0:MH, 2 * half + 1, 0:NS], pr(b, MH), None, ALU.add))
                    nc.vector.tensor_copy(m, li).then_inc(ex, 1)
                    dve.wait_ge(exd, 1)
                    link(nc.vector.scalar_tensor_tensor(out=lf, in0=lf, scalar=0.0, in1=ab, op0=ALU.min, op1=ALU.subtract))
                    link(nc.vector.tensor_tensor_scan(F[:, 0:SEQ], lf[:, 0:SEQ], zero[:, 0:SEQ], 0.0, ALU.add, ALU.add))
                    link(nc.vector.tensor_copy(s4(F)[:, :, 0:1], s4(lf)[:, :, 0:1]))
                    for u in range(1, DS):
                        link(nc.vector.tensor_tensor(s4(F)[:, :, u:u + 1], s4(F)[:, :, u - 1:u], s4(lf)[:, :, u:u + 1], ALU.add))
                    link(nc.vector.tensor_tensor(g, li, F, ALU.subtract))
                    link(nc.vector.tensor_tensor_scan(grow[:, 0:SEQ], g[:, 0:SEQ], g[:, 0:SEQ], 0.0, ALU.max, ALU.max))
                    dve.wait_ge(m_ld, 16)
                    m3 = m0.rearrange("p (b o) -> p b o", o=1)
                    for u in range(DS):
                        prev = m3 if u == 0 else s4(grow)[:, :, u - 1:u]
                        link(nc.vector.tensor_tensor(s4(grow)[:, :, u:u + 1], prev, s4(g)[:, :, u:u + 1], ALU.max))
                    link(nc.vector.tensor_tensor(m, F, grow, ALU.add))
                    last = s4(grow)[:, :, DS - 1:DS]
                    link(nc.vector.tensor_tensor(decay.rearrange("p (b o) -> p b o", o=1), m3, last, ALU.subtract))
                    link(nc.vector.tensor_tensor(s4(wg), s4(g), last.to_broadcast([MH, DB, DS]), ALU.subtract))
                    nc.vector.tensor_tensor(s4(av), m3.to_broadcast([MH, DB, DS]), s4(grow), ALU.subtract).then_inc(ex, 1)
                    dve.wait_ge(exd, 2)
                    nc.vector.tensor_copy(zero[:, 0:1], g[:, 0:1]).then_inc(rows_ok, 1)
                    dve.wait_ge(tp2, 1)
                    for n in range(2):
                        link(nc.vector.tensor_copy(cols[:, 20 * n:20 * n + 16], ps[:, 4, 20 * n:20 * n + 16]))
                        nc.vector.tensor_copy(cols[0:NS, 20 * n + 16:20 * n + 20], ps[0:NS, 4, 20 * n + 16:20 * n + 20]).then_inc(ev2, 1)
                    link(nc.vector.tensor_copy(cols[0:NS, 40:48], ps[0:NS, 4, 40:48]))

        KSC = float(MD) ** -0.5
        hh = ropf[:, 0:TT * 512].rearrange("p (t w) -> p t w", t=TT)

        def prompt_mlstm(l):
            gb, s_ok, kt, num, c_ok, w_ok, e_ok, p_ok, kw_ok, h_ok, cc_ok, stc = [sem(f"mlp_{n}") for n in
                ("g_rows", "scores", "keys_turned", "numerators", "state", "exponents", "weights", "probs", "keys_weighted",
                 "hidden", "state_copied", "state_stored")]
            Pb = lambda h: hTf[:, 2048 * (h % 2):2048 * (h % 2) + 2048].rearrange("p (s t) -> p s t", s=TP)
            W = lambda u: hTf[:, 4096 + 512 * (u % 2):4608 + 512 * (u % 2)]
            kw = ropf[:, 2560:3072].rearrange("p (s d) -> p s d", s=TP)
            CT = ropf[:, 3584:3584 + MH * 129].rearrange("p (h v) -> p h v", h=MH)
            one = cs("one")
            with nc.Block() as block:
                @block.sync
                def _(sp):
                    fill(sp, "mlp_", l)
                    sp.wait_ge(cc_ok, MH)
                    sp.dma_start(dout["cT_p"][bass.ds(l, 1)].rearrange("a p h v -> (a p) h v"), CT).then_inc(stc, 16)
                    sp.wait_ge(stc, 16)

                @block.tensor
                def _(pe):
                    for h in range(MH):
                        if h >= 2:
                            pe.wait_ge(kw_ok, 2 * (h - 1))
                        nc.tensor.matmul(ps[:, h % 2, :], ident[0:MH, h:h + 1].to_broadcast([MH, P]), grow[:, 0:SEQ],
                                         start=True, stop=True).then_inc(gb, 1)
                        for st in range(TP):
                            u = TP * h + st
                            if u >= 2:
                                pe.wait_ge(p_ok, u - 1)
                            nc.tensor.matmul(ps[:, 2 + u % 2, st * P:SEQ], qkT[:, MH + h, st * P:st * P + P],
                                             qkT[:, h, st * P:SEQ], start=True, stop=True).then_inc(s_ok, 1)
                        if h:
                            pe.wait_ge(kw_ok, 2 * h)
                        for st in range(TP):
                            ins = nc.tensor.transpose(ps[:, 4, st * P:st * P + P], qkT[:, MH + h, st * P:st * P + P], ident)
                        ins.then_inc(kt, 1)
                        pe.wait_ge(p_ok, TP * h + TP)
                        for t in range(TP):
                            u = TP * h + t
                            if u >= 2:
                                pe.wait_ge(h_ok, u - 1)
                            o = ps[:, 5 + (TP * h + t) % 2, 0:129]
                            for st in range(t + 1):
                                nc.tensor.matmul(o[:, 0:128], Pb(h)[:, st, t * P:t * P + P],
                                                 z[:, st, ZV + MD * h:ZV + MD * h + MD], start=(st == 0), stop=(st == t))
                            for st in range(t + 1):
                                ins = nc.tensor.matmul(o[:, 128:129], Pb(h)[:, st, t * P:t * P + P], one,
                                                       start=(st == 0), stop=(st == t))
                            ins.then_inc(num, 1)
                        pe.wait_ge(kw_ok, 2 * h + 2)
                        if h:
                            pe.wait_ge(cc_ok, h)
                        for st in range(TP):
                            nc.tensor.matmul(ps[:, 7, 0:128], kw[:, st, :], z[:, st, ZV + MD * h:ZV + MD * h + MD],
                                             start=(st == 0), stop=(st == TP - 1))
                        for st in range(TP):
                            ins = nc.tensor.matmul(ps[:, 7, 128:129], kw[:, st, :], one, start=(st == 0), stop=(st == TP - 1))
                        ins.then_inc(c_ok, 1)

                @block.scalar
                def _(act):
                    for h in range(MH):
                        for st in range(TP):
                            u = TP * h + st
                            act.wait_ge(w_ok, 5 * h + st + 1)
                            w = W(u)[:, st * P:SEQ]
                            nc.scalar.activation(w, w, ACT.Exp, scale=-1.0).then_inc(e_ok, 1)
                        act.wait_ge(w_ok, 5 * h + 5)
                        nc.scalar.activation(wpcol[:, h, :], wpcol[:, h, :], ACT.Exp).then_inc(e_ok, 1)

                @block.vector
                def _(dve):
                    link = chain(dve, "mlp_dve")
                    tri = cs("tri")
                    for h in range(MH):
                        dve.wait_ge(gb, h + 1)
                        B = ps[:, h % 2, :]

                        def weights(st):
                            u = TP * h + st
                            nc.vector.tensor_scalar(W(u)[:, st * P:SEQ], B[:, st * P:SEQ], gcol[:, st, h:h + 1], 0.0,
                                                    ALU.subtract, ALU.max).then_inc(w_ok, 1)
                        weights(0)
                        weights(1)
                        for st in range(TP):
                            u = TP * h + st
                            dve.wait_ge(e_ok, 5 * h + st + 1)
                            dve.wait_ge(s_ok, u + 1)
                            pb = Pb(h)[:, st, st * P:SEQ]
                            link(nc.vector.scalar_tensor_tensor(out=pb, in0=ps[:, 2 + u % 2, st * P:SEQ], scalar=KSC,
                                                                in1=W(u)[:, st * P:SEQ], op0=ALU.mult, op1=ALU.mult))
                            d = Pb(h)[:, st, st * P:st * P + P]
                            nc.vector.tensor_tensor(d, d, tri, ALU.mult).then_inc(p_ok, 1)
                            if st + 2 < TP:
                                weights(st + 2)
                        nc.vector.tensor_scalar(wpcol[:, h, :], gcol[:, 0:TP, h], B[:, SEQ - 1:SEQ], None,
                                                ALU.subtract).then_inc(w_ok, 1)
                        dve.wait_ge(e_ok, 5 * h + 5)
                        dve.wait_ge(kt, h + 1)
                        if h:
                            dve.wait_ge(c_ok, h)
                        for st in range(TP):
                            ins = nc.vector.tensor_scalar(kw[:, st, :], ps[:, 4, st * P:st * P + P], wpcol[:, h, st:st + 1],
                                                          KSC, ALU.mult, ALU.mult)
                            link(ins) if st < TP - 2 else ins.then_inc(kw_ok, 1)
                        for t in range(TP):
                            dve.wait_ge(num, TP * h + t + 1)
                            o = ps[:, 5 + (TP * h + t) % 2, 0:129]
                            link(nc.vector.tensor_scalar(stat[:, 0:1], o[:, 128:129], -1.0, emcol[:, t, h:h + 1],
                                                         ALU.mult, ALU.max))
                            link(nc.vector.tensor_scalar(stat[:, 0:1], o[:, 128:129], stat[:, 0:1], None, ALU.max))
                            link(nc.vector.reciprocal(stat[:, 1:2], stat[:, 0:1]))
                            nc.vector.tensor_scalar(hh[:, t, MD * h:MD * h + MD], o[:, 0:128], stat[:, 1:2], None,
                                                    ALU.mult).then_inc(h_ok, 1)
                        dve.wait_ge(c_ok, h + 1)
                        nc.vector.tensor_copy(CT[:, h, :], ps[:, 7, 0:129]).then_inc(cc_ok, 1)

        def sample_mlstm(l):
            gb, kt, it, ia, cu, cu_used, nu, dv, ex, stc, n_ld, cs_st = [sem(f"mls_{n}") for n in
                ("g_rows", "keys_turned", "from_state", "from_chunk", "updates", "updates_read", "n_update", "to_pe", "exp",
                 "stored", "n_loaded", "c_done")]
            C = slot("cst").rearrange("p (h b v) -> p h b v", h=MH, b=DB)
            nT = ropf[:, 2560:2592].rearrange("p (h b) -> p h b", h=MH)
            kw, pT, tmp, decB, qm = (ropf[0:NS, 2592:2720], ropf[0:NS, 2720:2752], ropf[0:NS, 2752:2881],
                                     ropf[:, 2884:2916].rearrange("p (h b) -> p h b", h=MH),
                                     hTf[:, 0:1024].rearrange("p (h b t) -> p h b t", h=MH, b=DB))
            kwm = hTf[0:NS, 1024:2048].rearrange("p (b d) -> p b d", b=DB)
            W = hTf[0:NS, 2048:2080]
            one, oh, ms = cs("one", NS), cs("ohb", NS), cs("ms", NS)
            with nc.Block() as block:
                @block.sync
                def _(sp):
                    sp.dma_start(nT, din["nT"][bass.ds(l, 1)].rearrange("a p (h b) -> (a p) h b", h=MH)).then_inc(n_ld, 16)
                    sp.wait_ge(cs_st, MH)
                    sp.dma_start(dout["cT_s"][bass.ds(l, 1)].rearrange("a p w -> (a p) w"), slot("cst")).then_inc(stc, 16)
                    sp.dma_start(dout["nT"][bass.ds(l, 1)].rearrange("a p (h b) -> (a p) h b", h=MH), nT).then_inc(stc, 16)
                    sp.wait_ge(stc, 32)
                    fill(sp, "mls", l, {"cst": (stc, 32)})

                @block.tensor
                def _(pe):
                    arrived(pe, "cst")
                    pe.wait_ge(n_ld, 16)
                    pe.wait_ge(dv, 1)
                    v = z[0:NS, TP, :]
                    for h in range(MH):
                        vh = v[:, ZV + MD * h:ZV + MD * h + MD]
                        nc.tensor.matmul(ps[0:NS, 1, 32:64], ident[0:MH, h:h + 1].to_broadcast([MH, NS]), grow[:, SEQ:TOK],
                                         start=True, stop=True)
                        nc.tensor.matmul(ps[:, 1, 64:72], ident[0:MH, h:h + 1].to_broadcast([MH, P]), decay,
                                         start=True, stop=True)
                        nc.tensor.matmul(ps[0:NS, 1, 0:32], qkT[:, MH + h, SEQ:TOK], qkT[:, h, SEQ:TOK],
                                         start=True, stop=True).then_inc(gb, 1)
                        nc.tensor.transpose(ps[0:NS, 2, 0:128], qkT[:, MH + h, SEQ:TOK], ident).then_inc(kt, 1)
                        for b in range(DB):
                            nc.tensor.matmul(ps[0:NS, 0, 0:128], qm[:, h, b, :], C[:, h, b, :], start=(b == 0), stop=(b == DB - 1))
                        for b in range(DB):
                            ins = nc.tensor.matmul(ps[0:NS, 0, 128:129], qm[:, h, b, :], nT[:, h, b:b + 1],
                                                   start=(b == 0), stop=(b == DB - 1))
                        ins.then_inc(it, 1)
                        pe.wait_ge(dv, 3 * h + 2)
                        nc.tensor.matmul(ps[0:NS, 3, 0:128], pT, vh, start=True, stop=True)
                        nc.tensor.matmul(ps[0:NS, 3, 128:129], pT, one, start=True, stop=True).then_inc(ia, 1)
                        pe.wait_ge(dv, 3 * h + 3)
                        for b in range(DB):
                            ins = nc.tensor.matmul(ps[:, 5 + b // 4, (b % 4) * P:(b % 4) * P + P], kwm[:, b, :], vh,
                                                   start=True, stop=True)
                        ins.then_inc(cu, 1)
                        nc.tensor.matmul(ps[:, 7, 0:DB], kw, oh, start=True, stop=True).then_inc(nu, 1)
                        pe.wait_ge(dv, 3 * h + 4)

                @block.scalar
                def _(act):
                    for h in range(MH):
                        act.wait_ge(ex, 2 * h + 1)
                        nc.scalar.activation(W, W, ACT.Exp, scale=-1.0).then_inc(ex, 1)

                @block.vector
                def _(dve):
                    link = chain(dve, "mls_dve")
                    dve.wait_ge(n_ld, 16)
                    arrived(dve, "cst")
                    link(nc.vector.memset(qm, 0.0))
                    for b in range(DB):
                        ins = nc.vector.tensor_copy(qm[:, :, b, 4 * b:4 * b + 4], qkT[:, 0:MH, SEQ + 4 * b:SEQ + 4 * b + 4])
                        link(ins) if b < DB - 1 else ins.then_inc(dv, 1)
                    for h in range(MH):
                        dve.wait_ge(gb, h + 1)
                        nc.vector.tensor_scalar(W, ps[0:NS, 1, 32:64], gcol[0:NS, TP, h:h + 1], 0.0, ALU.subtract,
                                                ALU.max).then_inc(ex, 1)
                        link(nc.vector.tensor_copy(decB[:, h, :], ps[:, 1, 64:72]))
                        dve.wait_ge(ex, 2 * h + 2)
                        link(nc.vector.scalar_tensor_tensor(out=pT, in0=ps[0:NS, 1, 0:32], scalar=KSC, in1=W,
                                                            op0=ALU.mult, op1=ALU.mult))
                        nc.vector.tensor_tensor(pT, pT, ms, ALU.mult).then_inc(dv, 1)
                        dve.wait_ge(kt, h + 1)
                        link(nc.vector.tensor_scalar(kw, ps[0:NS, 2, 0:128], wscol[:, h:h + 1], KSC, ALU.mult, ALU.mult))
                        nc.vector.tensor_tensor(
                            kwm, kw.rearrange("p (o d) -> p o d", o=1).to_broadcast([NS, DB, MD]),
                            oh.rearrange("p (b o) -> p b o", o=1).to_broadcast([NS, DB, MD]), ALU.mult).then_inc(dv, 1)
                        dve.wait_ge(it, h + 1)
                        link(nc.vector.tensor_scalar(tmp, ps[0:NS, 0, 0:129], ascol[:, h:h + 1], None, ALU.mult))
                        dve.wait_ge(ia, h + 1)
                        link(nc.vector.tensor_tensor(tmp, ps[0:NS, 3, 0:129], tmp, ALU.add))
                        link(nc.vector.tensor_scalar(stat[0:NS, 0:1], tmp[:, 128:129], -1.0, emcol[0:NS, TP, h:h + 1],
                                                     ALU.mult, ALU.max))
                        link(nc.vector.tensor_scalar(stat[0:NS, 0:1], tmp[:, 128:129], stat[0:NS, 0:1], None, ALU.max))
                        link(nc.vector.reciprocal(stat[0:NS, 1:2], stat[0:NS, 0:1]))
                        if h == 0:
                            link(nc.vector.memset(hh[:, TP, :], 0.0))
                        link(nc.vector.tensor_scalar(hh[0:NS, TP, MD * h:MD * h + MD], tmp[:, 0:128], stat[0:NS, 1:2], None,
                                                     ALU.mult))
                        dve.wait_ge(cu, h + 1)
                        for b in range(DB):
                            link(nc.vector.scalar_tensor_tensor(out=C[:, h, b, :], in0=C[:, h, b, :],
                                                                scalar=decB[:, h, b:b + 1],
                                                                in1=ps[:, 5 + b // 4, (b % 4) * P:(b % 4) * P + P],
                                                                op0=ALU.mult, op1=ALU.add))
                        dve.wait_ge(nu, h + 1)
                        link(nc.vector.tensor_tensor(nT[:, h, :], nT[:, h, :], decB[:, h, :], ALU.mult))
                        link(nc.vector.tensor_tensor(nT[:, h, :], ps[:, 7, 0:DB], nT[:, h, :], ALU.add))
                        nc.vector.tensor_copy(stat[0:1, 2:3], stat[0:1, 1:2]).then_inc(dv, 1)
                        dve.wait_ge(dv, 3 * h + 4)
                        nc.vector.tensor_copy(stat[0:1, 3:4], stat[0:1, 2:3]).then_inc(cs_st, 1)

        def finish_mlstm(l):
            go, root = sem("mfin_squares"), sem("mfin_root")
            v = hh.rearrange("p t (h d) -> p t h d", h=MH)
            sq = hTf[:, 0:2560]
            with nc.Block() as block:
                @block.sync
                def _(sp):
                    fill(sp, "mfin", l)

                @block.scalar
                def _(act):
                    act.wait_ge(go, 1)
                    nc.scalar.activation(stat[:, 80:100], stat[:, 0:20], ACT.Sqrt).then_inc(root, 1)

                @block.vector
                def _(dve):
                    link = chain(dve, "mfin_dve")
                    head_norm(link, [(v, pr("hn"), 0, sq.rearrange("p (t h d) -> p t h d", t=TT, h=MH))], 20, root, go, MD)
                    o = z[:, :, ZO:ZO + 512]
                    link(nc.vector.tensor_tensor(o, o, hh, ALU.mult))

        kselT, kwinT = ropf[:, 0:TOK], ropf[:, TOK:2 * TOK]
        qT = ropf[:, 2 * TOK:2 * TOK + HG * TOK].rearrange("p (h t) -> p h t", h=HG)
        xp = qkf[:, 0:SEQ // 2 * 4]
        kc_p = qkf[:, 1024:1024 + NC_P]
        vc_p = qkf[0:NC_P, 1056:1056 + P]
        QSC = float(HD) ** -0.5

        def prep_stage(l):
            tp, ea, ed = sem("prep_turned"), sem("prep_copied_a"), sem("prep_copied_d")
            pairs = xp.rearrange("p (q k g) -> p k g q", k=2, g=G)
            with nc.Block() as block:
                @block.sync
                def _(sp):
                    fill(sp, "prep", l)

                @block.tensor
                def _(pe):
                    for t in range(TT):
                        if t >= 4:
                            pe.wait_ge(ea, t - 3)
                            pe.wait_ge(ed, t - 3)
                        b = 2 * (t % 4)
                        for hg in range(HG):
                            nc.tensor.transpose(ps[:, b, hg * P:hg * P + P], z[:, t, ZQ + hg * P:ZQ + hg * P + P], ident)
                        for n, c in enumerate((ZK + 256, ZK + 512, ZK, ZK + 128)):
                            if t < TP or n < 2:
                                ins = nc.tensor.transpose(ps[:, b + 1, n * P:n * P + P], z[:, t, c:c + P], ident)
                        ins.then_inc(tp, 1)

                @block.scalar
                def _(act):
                    for t in range(TT):
                        w = P if t < TP else NS
                        act.wait_ge(tp, t + 1)
                        nc.scalar.activation(qT[:, :, t * P:t * P + w],
                                             ps[:, 2 * (t % 4), :].rearrange("p (h t) -> p h t", h=HG)[:, :, 0:w],
                                             ACT.Copy, scale=QSC).then_inc(ea, 1)

                @block.vector
                def _(dve):
                    link = chain(dve, "prep_dve")
                    for t in range(TT):
                        w = P if t < TP else NS
                        dve.wait_ge(tp, t + 1)
                        s = ps[:, 2 * (t % 4) + 1, :]
                        if t < TP:
                            for k in range(2):
                                for g in range(G):
                                    for par in range(2):
                                        a = 256 + 128 * k + par
                                        link(nc.vector.tensor_copy(pairs[64 * par:64 * par + 64, k, g, 64 * t:64 * t + 64],
                                                                   s[64 * g:64 * g + 64, a:a + 127:2]))
                        link(nc.vector.tensor_copy(kselT[:, t * P:t * P + w], s[:, 0:w]))
                        nc.vector.tensor_copy(kwinT[:, t * P:t * P + w], s[:, 128:128 + w]).then_inc(ed, 1)

        def prompt_compress(l):
            compress_stage("pcmp", l, [(None, xp.rearrange("p (q w) -> p q w", w=4), NC_P, kc_p, vc_p)], frees="cmpw")

        def tile_attention(stage, l, units, free=None):
            s_ok, mx, e_ok, pt, ptc, o_ok, o_used, cf = [sem(f"{stage}_{n}") for n in
                ("scores", "maxima", "exponentials", "probs_turned", "probs_copied", "outputs", "outputs_read", "factors")]
            Pb = lambda u: hTf[:, 512 * (u % 4):512 * (u % 4) + 512]
            PT = lambda u: hTf[:, 2048 + 512 * (u % 4):2560 + 512 * (u % 4)]
            st = lambda u, c: stat[:, 8 * (u % 8) + c:8 * (u % 8) + c + 1]
            causal = cs("causal")
            N = len(units)
            with nc.Block() as block:
                @block.sync
                def _(sp):
                    fill(sp, stage, l)

                @block.tensor
                def _(pe):
                    def scores(u):
                        q, k, n = units[u][0:3]
                        if u >= 3:
                            pe.wait_ge(e_ok, u - 2)
                        nc.tensor.matmul(ps[:, u % 3, 0:n], q, k, start=True, stop=True).then_inc(s_ok, 1)

                    def turn(u):
                        n = units[u][2]
                        pe.wait_ge(e_ok, u + 1)
                        if u >= 3:
                            pe.wait_ge(ptc, u - 2)
                        for i in range(n // P):
                            ins = nc.tensor.transpose(ps[:, 3 + u % 3, i * P:i * P + P], Pb(u)[:, i * P:i * P + P], ident)
                        ins.then_inc(pt, 1)

                    def values(u):
                        n, vs, w = units[u][2], units[u][4], units[u][5]
                        pe.wait_ge(ptc, u + 1)
                        if u >= 2:
                            pe.wait_ge(o_used, u - 1)
                        for i in range(n // P):
                            ins = nc.tensor.matmul(ps[:, 6 + u % 2, 0:w], PT(u)[:, i * P:i * P + P], vs[i],
                                                   start=(i == 0), stop=(i == n // P - 1))
                        ins.then_inc(o_ok, 1)
                    for u in range(N + 3):
                        if u < N:
                            scores(u)
                        if 2 <= u < N + 2:
                            turn(u - 2)
                        if u >= 3:
                            values(u - 3)

                @block.scalar
                def _(act):
                    def copied(u):
                        act.wait_ge(pt, u + 1)
                        n = units[u][2]
                        if u >= 4:
                            act.wait_ge(o_ok, u - 3)
                        nc.scalar.copy(PT(u)[:, 0:n], ps[:, 3 + u % 3, 0:n]).then_inc(ptc, 1)
                    for u in range(N + 2):
                        if u < N:
                            n = units[u][2]
                            act.wait_ge(mx, u + 1)
                            if u >= 4:
                                act.wait_ge(pt, u - 3)
                            nc.scalar.activation(Pb(u)[:, 0:n], ps[:, u % 3, 0:n], ACT.Exp, bias=st(u, 0),
                                                 accum_out=st(u, 1)).then_inc(e_ok, 1)
                        if u >= 2:
                            copied(u - 2)

                @block.vector
                def _(dve):
                    link = chain(dve, f"{stage}_dve")

                    def output(u):
                        _, _, n, _, _, w, gate, out, adds = units[u]
                        dve.wait_ge(e_ok, u + 1)
                        link(nc.vector.reciprocal(st(u, 2), st(u, 1)))
                        f = st(u, 2)
                        if gate is not None:
                            link(nc.vector.tensor_tensor(st(u, 3), st(u, 2), gate, ALU.mult))
                            f = st(u, 3)
                        dve.wait_ge(o_ok, u + 1)
                        src = ps[:, 6 + u % 2, 0:w]
                        if adds:
                            nc.vector.scalar_tensor_tensor(out=out, in0=src, scalar=f, in1=out, op0=ALU.mult,
                                                           op1=ALU.add).then_inc(o_used, 1)
                        else:
                            nc.vector.tensor_scalar(out, src, f, None, ALU.mult).then_inc(o_used, 1)
                    for u in range(N + 3):
                        if u < N:
                            n, diag = units[u][2], units[u][3]
                            dve.wait_ge(s_ok, u + 1)
                            if diag:
                                link(nc.vector.tensor_tensor(ps[:, u % 3, n - P:n], ps[:, u % 3, n - P:n], causal, ALU.add))
                            nc.vector.tensor_reduce(st(u, 0), ps[:, u % 3, 0:n], AX.X, ALU.max, negate=True).then_inc(mx, 1)
                        if u >= 3:
                            if adds_need(units, u - 3):
                                dve.wait_ge(o_used, u - 3)
                            output(u - 3)
                    dve.wait_ge(o_used, N)

        def adds_need(units, u):
            return u > 0 and units[u][8]

        def prompt_attention(l):
            s_ok, r_ok, e_ok, pt, ptc, o_ok, ouse = [sem(f"pc_{n}") for n in
                ("scores", "rows", "exponentials", "turned", "copied", "outputs", "outputs_read")]
            n = NC_P
            e = hTf[:, 0:HEADS * n].rearrange("p (h c) -> p h c", h=HEADS)
            eT = hTf[0:n, 1024:2048].rearrange("p (h t) -> p h t", h=HEADS)
            zg = z[:, :, ZG:ZG + 24].rearrange("p t (h r) -> p t h r", r=3)
            with nc.Block() as block:
                @block.sync
                def _(sp):
                    fill(sp, "att", l)

                @block.tensor
                def _(pe):
                    for t in range(TP):
                        if t:
                            pe.wait_ge(e_ok, t)
                        for h in range(HEADS):
                            g, hg = h % G, h // G
                            ins = nc.tensor.matmul(ps[:, 4 * g, n * hg:n * hg + n], qT[64 * g:64 * g + 64, hg, t * P:t * P + P],
                                                   kc_p[64 * g:64 * g + 64, :], start=True, stop=True)
                        ins.then_inc(s_ok, 1)
                        pe.wait_ge(r_ok, t + 1)
                        for h in range(HEADS):
                            ins = nc.tensor.transpose(ps[0:n, 1 + h // 4, (h % 4) * P:(h % 4) * P + P], e[:, h, :], ident)
                        ins.then_inc(pt, 1)
                        pe.wait_ge(ptc, t + 1)
                        for h in range(HEADS):
                            ins = nc.tensor.matmul(ps[:, 3, 64 * h:64 * h + 64], eT[:, h, :],
                                                   vc_p[:, 64 * (h % G):64 * (h % G) + 64], start=True, stop=True)
                        ins.then_inc(o_ok, 1)

                @block.scalar
                def _(act):
                    for t in range(TP):
                        act.wait_ge(s_ok, 2 * t + 2)
                        nc.scalar.activation(e, e, ACT.Exp).then_inc(e_ok, 1)

                @block.vector
                def _(dve):
                    link = chain(dve, "pc_dve")
                    bc = lambda a: a.rearrange("p (h o) -> p h o", o=1).to_broadcast([P, HEADS, n])
                    for t in range(TP):
                        dve.wait_ge(s_ok, 2 * t + 1)
                        ma = cs("cma")[:, n * t:n * t + n].rearrange("p (o c) -> p o c", o=1).to_broadcast([P, HG, n])
                        mm = cs("cmm")[:, n * t:n * t + n].rearrange("p (o c) -> p o c", o=1).to_broadcast([P, HEADS, n])
                        for g in range(G):
                            src = ps[:, 4 * g, 0:HG * n].rearrange("p (h c) -> p h c", h=HG)
                            link(nc.vector.tensor_tensor(e[:, g:HEADS:G, :], src, ma, ALU.add))
                        link(nc.vector.tensor_reduce(stat[:, 0:8], e, AX.X, ALU.max))
                        nc.vector.tensor_tensor(e, e, bc(stat[:, 0:8]), ALU.subtract).then_inc(s_ok, 1)
                        dve.wait_ge(e_ok, t + 1)
                        link(nc.vector.tensor_tensor(e, e, mm, ALU.mult))
                        link(nc.vector.tensor_reduce(stat[:, 8:16], e, AX.X, ALU.add))
                        link(nc.vector.tensor_scalar(stat[:, 8:16], stat[:, 8:16], 1e-30, None, ALU.max))
                        link(nc.vector.reciprocal(stat[:, 16:24], stat[:, 8:16]))
                        link(nc.vector.tensor_tensor(stat[:, 24:32], stat[:, 16:24], zg[:, t, :, 0], ALU.mult))
                        nc.vector.tensor_tensor(e, e, bc(stat[:, 24:32]), ALU.mult).then_inc(r_ok, 1)
                        dve.wait_ge(pt, t + 1)
                        link(nc.vector.tensor_copy(eT[:, 0:4, :], ps[0:n, 1, :].rearrange("p (h t) -> p h t", h=4)))
                        nc.vector.tensor_copy(eT[:, 4:8, :], ps[0:n, 2, :].rearrange("p (h t) -> p h t", h=4)).then_inc(ptc, 1)
                        dve.wait_ge(o_ok, t + 1)
                        link(nc.vector.tensor_copy(z[:, t, ZQ:ZQ + 512], ps[:, 3, :]))
            units = []
            for t in range(TP):
                for r, kT in ((1, kselT), (2, kwinT)):
                    for h in range(HEADS):
                        g, hg = h % G, h // G
                        vc = ZK + 256 * r + 128 + 64 * g
                        units.append((qT[64 * g:64 * g + 64, hg, t * P:t * P + P], kT[64 * g:64 * g + 64, 0:t * P + P],
                                      t * P + P, True, [z[:, i, vc:vc + 64] for i in range(t + 1)], 64, zg[:, t, h, r:r + 1],
                                      z[:, t, ZQ + 64 * h:ZQ + 64 * h + 64], True))
            tile_attention("att2", l, units)

        s_sel, s_win, s_cmp = qkf[:, 0:PAST + NS], qkf[:, 2080:2080 + WIN + NS], qkf[:, 2624:2752]
        imp, rep, top, impc = qkf[:, 2752:2785], qkf[:, 2786:2819], qkf[:, 2820:2828], qkf[:, 2828:2956]
        oT = qkf[:, 3000:3384].rearrange("p (r h t) -> p r h t", r=3, h=HG)
        qblk = qkf[:, 3400:3656].rearrange("p (b r) -> p b r", b=DB)
        pT = hTf[:, 0:23 * P].rearrange("p (i r) -> p i r", i=23)

        def sample_attention(l, hb):
            stage = f"samp{hb}"
            q_ok, sc, sw, ss, cp, pc_ok, im, mx, ex, pn, pt, ca, cd, wv, ov = [sem(f"{stage}_{n}") for n in
                ("queries", "cmp_scores", "win_scores", "sel_scores", "scores_copied", "cmp_probs", "importance", "maxima",
                 "exponentials", "probs_ready", "turned", "copied_a", "copied_d", "win_outputs", "outputs")]
            kl, vl = [f"kT{2 * hb + i}" for i in range(2)], [f"v{2 * hb + i}" for i in range(2)]
            wl = f"win{hb}"
            tiles = [(s_cmp[:, 0:NC_S], NC_S)] + [(s_win[:, i * P:i * P + P], P) for i in range(4)] + [(s_win[:, WIN:], NS)]
            tiles += [(s_sel[:, i * P:i * P + P], P) for i in range(16)] + [(s_sel[:, PAST:], NS)]
            with nc.Block() as block:
                @block.sync
                def _(sp):
                    fill(sp, stage, l, {kl[0]: (ss, 1), kl[1]: (ss, 2), wl: (wv, 1), vl[0]: (ov, 1), vl[1]: (ov, 2)})

                @block.tensor
                def _(pe):
                    pe.wait_ge(q_ok, 1)
                    for b4 in range(4):
                        b = 4 * hb + b4
                        r = slice(32 * b4, 32 * b4 + 32)
                        q = qblk[:, b, :]
                        nc.tensor.matmul(ps[r, 0, 0:NC_S], q, kc_s[:, b, 0:NC_S], start=True, stop=True)
                        nc.tensor.matmul(ps[r, 0, 128:160], q, kwinT[:, SEQ:TOK], start=True, stop=True)
                        ins = nc.tensor.matmul(ps[r, 0, 160:192], q, kselT[:, SEQ:TOK], start=True, stop=True)
                    ins.then_inc(sc, 1)
                    for i in range(2):
                        arrived(pe, kl[i])
                        keys = slot(kl[i]).rearrange("p (b k) -> p b k", b=2)
                        for b4 in range(2 * i, 2 * i + 2):
                            for c in range(4):
                                ins = nc.tensor.matmul(ps[32 * b4:32 * b4 + 32, 2 + c, :], qblk[:, 4 * hb + b4, :],
                                                       keys[:, b4 % 2, c * 512:c * 512 + 512], start=True, stop=True)
                        ins.then_inc(ss, 1)
                    arrived(pe, wl)
                    for b4 in range(4):
                        ins = nc.tensor.matmul(ps[32 * b4:32 * b4 + 32, 1, :], qblk[:, 4 * hb + b4, :],
                                               slot(wl)[:, 512 * b4:512 * b4 + 512], start=True, stop=True)
                    ins.then_inc(sw, 1)
                    pe.wait_ge(pc_ok, 1)
                    nc.tensor.matmul(ps[:, 6, 0:NC_S], cs("grp"), s_cmp[:, 0:NC_S], start=True, stop=True).then_inc(im, 1)
                    for i, (src, n) in enumerate(tiles):
                        if i == 1:
                            pe.wait_ge(pn, 1)
                        if i == 6:
                            pe.wait_ge(pn, 2)
                        if i % 4 == 0:
                            if i == 0:
                                pe.wait_ge(cp, 1)
                            if i >= 8:
                                pe.wait_ge(ca if (i // 4) % 2 == 0 else cd, (i // 4 - 2) // 2 + 1)
                        ins = nc.tensor.transpose(ps[0:n, (0, 6)[i // 4 % 2], (i % 4) * P:(i % 4) * P + P], src, ident)
                        if i % 4 == 3 or i == 22:
                            ins.then_inc(pt, 1)
                    pe.wait_ge(ca, 3)
                    pe.wait_ge(cd, 3)
                    win_v = slot(wl)[:, 2048:4096].rearrange("p (b t c) -> p b t c", b=4, t=4)
                    for b4 in range(4):
                        r = slice(32 * b4, 32 * b4 + 32)
                        nc.tensor.matmul(ps[:, 7, r], vc_s[0:NC_S, 4 * hb + b4, :], pT[0:NC_S, 0, r], start=True, stop=True)
                        for i in range(4):
                            nc.tensor.matmul(ps[:, 7, 128 + 32 * b4:160 + 32 * b4], win_v[:, b4, i, :], pT[:, 1 + i, r],
                                             start=(i == 0), stop=False)
                        ins = nc.tensor.matmul(ps[:, 7, 128 + 32 * b4:160 + 32 * b4], z[0:NS, TP, ZK + 640:ZK + 768],
                                               pT[0:NS, 5, r], start=False, stop=True)
                    ins.then_inc(wv, 1)
                    for j in range(2):
                        arrived(pe, vl[j])
                        vals = slot(vl[j]).rearrange("p (b i c) -> p b i c", b=2, i=NPG)
                        for b4 in range(2 * j, 2 * j + 2):
                            r = slice(32 * b4, 32 * b4 + 32)
                            o = ps[:, 7, 256 + 32 * b4:288 + 32 * b4]
                            nc.tensor.matmul(o, z[0:NS, TP, ZK + 384:ZK + 512], pT[0:NS, 22, r], start=True, stop=False)
                            for i in range(NPG):
                                ins = nc.tensor.matmul(o, vals[:, b4 % 2, i, :], pT[:, 6 + i, r], start=False, stop=(i == NPG - 1))
                        ins.then_inc(ov, 1)

                @block.scalar
                def _(act):
                    link = chain(act, f"{stage}_act")
                    for i, (s, a) in enumerate(((s_cmp[:, 0:NC_S], 0), (s_win, 4), (s_sel, 8))):
                        act.wait_ge(mx, i + 1)
                        nc.scalar.activation(s, s, ACT.Exp, bias=stat[:, a:a + 1], accum_out=stat[:, a + 1:a + 2]).then_inc(ex, 1)
                    for q in (0, 2, 4):
                        act.wait_ge(pt, q + 1)
                        if q == 0:
                            link(nc.scalar.copy(pT[0:NC_S, 0, :], ps[0:NC_S, 0, 0:P]))
                            ins = nc.scalar.copy(pT[:, 1:4, :], ps[:, 0, P:512].rearrange("p (i r) -> p i r", i=3))
                        else:
                            ins = nc.scalar.copy(pT[:, 4 * q:4 * q + 4, :], ps[:, 0, :].rearrange("p (i r) -> p i r", i=4))
                        ins.then_inc(ca, 1)

                @block.vector
                def _(dve):
                    link = chain(dve, f"{stage}_dve")
                    if hb == 0:
                        link(nc.vector.memset(qblk, 0.0))
                        for g in range(G):
                            for hg in range(HG):
                                p = slice(64 * g, 64 * g + 64)
                                c = 16 * g + 4 * hg
                                link(nc.vector.tensor_copy(qblk[p, :, c:c + 4],
                                                           qT[p, hg, SEQ:TOK].rearrange("p (b t) -> p b t", b=DB)))
                    nc.vector.memset(impc[:, 127:128], 0.0).then_inc(q_ok, 1)
                    dve.wait_ge(q_ok, 1)
                    new = cs("new")[:, 32 * hb:32 * hb + 32]
                    dve.wait_ge(sc, 1)
                    link(nc.vector.tensor_copy(s_cmp[:, 0:NC_S], ps[:, 0, 0:NC_S]))
                    link(nc.vector.tensor_reduce(stat[:, 0:1], s_cmp[:, 0:NC_S], AX.X, ALU.max, negate=True))
                    link(nc.vector.tensor_tensor(s_win[:, WIN:], ps[:, 0, 128:160], new, ALU.add))
                    link(nc.vector.tensor_tensor(s_sel[:, PAST:], ps[:, 0, 160:192], new, ALU.add))
                    nc.vector.tensor_copy(stat[:, 2:3], stat[:, 0:1]).then_inc(cp, 1)
                    dve.wait_ge(cp, 1)
                    nc.vector.tensor_copy(stat[:, 3:4], stat[:, 2:3]).then_inc(mx, 1)
                    dve.wait_ge(ex, 1)
                    link(nc.vector.reciprocal(stat[:, 2:3], stat[:, 1:2]))
                    nc.vector.tensor_scalar(s_cmp[:, 0:NC_S], s_cmp[:, 0:NC_S], stat[:, 2:3], None, ALU.mult).then_inc(pc_ok, 1)
                    dve.wait_ge(sw, 1)
                    link(nc.vector.tensor_copy(s_win[:, 4:WIN], ps[:, 1, 4:WIN]))
                    link(nc.vector.tensor_tensor(s_win[:, 0:4], ps[:, 1, 0:4], cs("low"), ALU.add))
                    nc.vector.tensor_reduce(stat[:, 4:5], s_win, AX.X, ALU.max, negate=True).then_inc(mx, 1)
                    dve.wait_ge(im, 1)
                    link(nc.vector.tensor_copy(impc[:, 0:NC_S], ps[:, 6, 0:NC_S]))
                    link(nc.vector.tensor_reduce(imp[:, 0:32], impc.rearrange("p (s u) -> p s u", u=4), AX.X, ALU.add))
                    link(nc.vector.tensor_tensor(imp[:, 1:32], imp[:, 1:32], impc[:, 3:124:4], ALU.add))
                    link(nc.vector.memset(imp[:, 0:1], BIG))
                    link(nc.vector.memset(imp[:, 32:33], BIG))
                    link(nc.vector.max(top, imp))
                    link(nc.vector.match_replace(rep, top, imp, 3.0 * BIG))
                    link(nc.vector.tensor_scalar(rep, rep, 2.0 * BIG, None, ALU.is_ge))
                    link(nc.vector.tensor_scalar(rep, rep, -1.0, BIG, ALU.add, ALU.mult))
                    dve.wait_ge(ss, 2)
                    for c in range(4):
                        link(nc.vector.tensor_tensor(
                            s_sel[:, c * 512:c * 512 + 512].rearrange("p (s k) -> p s k", s=8),
                            ps[:, 2 + c, :].rearrange("p (s k) -> p s k", s=8),
                            rep[:, 8 * c:8 * c + 8].rearrange("p (s o) -> p s o", o=1).to_broadcast([P, 8, SELB]), ALU.add))
                    nc.vector.tensor_reduce(stat[:, 8:9], s_sel, AX.X, ALU.max, negate=True).then_inc(mx, 1)
                    dve.wait_ge(ex, 2)
                    link(nc.vector.reciprocal(stat[:, 6:7], stat[:, 5:6]))
                    nc.vector.tensor_scalar(s_win, s_win, stat[:, 6:7], None, ALU.mult).then_inc(pn, 1)
                    dve.wait_ge(ex, 3)
                    link(nc.vector.reciprocal(stat[:, 10:11], stat[:, 9:10]))
                    nc.vector.tensor_scalar(s_sel, s_sel, stat[:, 10:11], None, ALU.mult).then_inc(pn, 1)
                    for q in (1, 3, 5):
                        dve.wait_ge(pt, q + 1)
                        if q == 1:
                            link(nc.vector.tensor_copy(pT[:, 4, :], ps[:, 6, 0:P]))
                            link(nc.vector.tensor_copy(pT[0:NS, 5, :], ps[0:NS, 6, P:2 * P]))
                            ins = nc.vector.tensor_copy(pT[:, 6:8, :], ps[:, 6, 256:512].rearrange("p (i r) -> p i r", i=2))
                        elif q == 3:
                            ins = nc.vector.tensor_copy(pT[:, 12:16, :], ps[:, 6, :].rearrange("p (i r) -> p i r", i=4))
                        else:
                            link(nc.vector.tensor_copy(pT[:, 20:22, :], ps[:, 6, 0:256].rearrange("p (i r) -> p i r", i=2)))
                            ins = nc.vector.tensor_copy(pT[0:NS, 22, :], ps[0:NS, 6, 256:384])
                        ins.then_inc(cd, 1)
                    dve.wait_ge(ov, 2)
                    for r, at in enumerate((0, 256, 128)):
                        for g in range(G):
                            p = slice(64 * g, 64 * g + 64)
                            for hg in range(HG):
                                link(nc.vector.tensor_copy(
                                    oT[p, r, hg, 16 * hb:16 * hb + 16].rearrange("p (b t) -> p b t", b=4),
                                    ps[p, 7, at:at + P].rearrange("p (b w) -> p b w", b=4)[:, :, 16 * g + 4 * hg:16 * g + 4 * hg + 4]))

        def sample_merge(l):
            tp = sem("sfin_turned")
            with nc.Block() as block:
                @block.sync
                def _(sp):
                    fill(sp, "sfin", l)

                @block.tensor
                def _(pe):
                    for r in range(3):
                        for hg in range(HG):
                            ins = nc.tensor.transpose(ps[0:NS, r, hg * P:hg * P + P], oT[:, r, hg, :], ident)
                    ins.then_inc(tp, 1)

                @block.vector
                def _(dve):
                    link = chain(dve, "sfin_dve")
                    dve.wait_ge(tp, 1)
                    zg = z[0:NS, TP, ZG:ZG + 24].rearrange("p (h r) -> p h r", r=3)
                    out = z[0:NS, TP, ZQ:ZQ + 512].rearrange("p (h d) -> p h d", h=HEADS)
                    tmp = hTf[0:NS, 0:512].rearrange("p (h d) -> p h d", h=HEADS)
                    for r in range(3):
                        src = ps[0:NS, r, :].rearrange("p (h d) -> p h d", h=HEADS)
                        gt = zg[:, :, r:r + 1].to_broadcast([NS, HEADS, HD])
                        if r == 0:
                            link(nc.vector.tensor_tensor(out, src, gt, ALU.mult))
                        else:
                            link(nc.vector.tensor_tensor(tmp, src, gt, ALU.mult))
                            link(nc.vector.tensor_tensor(out, out, tmp, ALU.add))

        def turn_stage(stage, l, tiles, srcs, dst, scale=1.0):
            tp = sem(f"{stage}_turned")
            ev = [sem(f"{stage}_copied_{j}") for j in range(2)]
            n = len(srcs(0))
            nb = -(-n // 4)
            with nc.Block() as block:
                @block.sync
                def _(sp):
                    fill(sp, stage, l)

                @block.tensor
                def _(pe):
                    for t in range(tiles):
                        if t >= 4:
                            for j in range(nb):
                                pe.wait_ge(ev[j], t - 3)
                        for k, src in enumerate(srcs(t)):
                            ins = nc.tensor.transpose(ps[:, 2 * (t % 4) + k // 4, (k % 4) * P:(k % 4) * P + P], src, ident)
                        ins.then_inc(tp, 1)

                def evict(eng, engine_copy, j):
                    for t in range(tiles):
                        eng.wait_ge(tp, t + 1)
                        if j < nb:
                            m = min(4, n - 4 * j)
                            engine_copy(dst[:, 4 * j:4 * j + m, t * P:t * P + P],
                                        ps[:, 2 * (t % 4) + j, 0:m * P].rearrange("p (k t) -> p k t", k=m)).then_inc(ev[j], 1)

                @block.scalar
                def _(act):
                    evict(act, nc.scalar.copy, 1)

                @block.vector
                def _(dve):
                    evict(dve, lambda o, i: nc.vector.tensor_scalar(o, i, scale, None, ALU.mult), 0)

        A = lambda a, n: arena[:, a:a + n]
        memx = A(0, 2048).rearrange("p (t w) -> p t w", t=MT)
        zm = A(2048, 1024).rearrange("p (t w) -> p t w", t=MT)
        kmT = A(3072, 512).rearrange("p (e m) -> p e m", e=2)
        zx = A(3584, 1280).rearrange("p (t w) -> p t w", t=TT)
        qxT = A(4864, 2 * TT * P).rearrange("p (e t) -> p e t", e=2)
        ox = A(6144, 1280).rearrange("p (t w) -> p t w", t=TT)
        oxT = A(7424, 2 * TT * P).rearrange("p (e t) -> p e t", e=2)
        xsq = A(8704, 1280)
        qxb = A(9984, 512).rearrange("p (e b r) -> p e b r", e=2, b=DB)
        sx, pxT = A(10496, 256), A(10752, 256).rearrange("p (i r) -> p i r", i=2)

        def memory_load(l):
            ld = sem("memory_loaded")
            with nc.Block() as block:
                @block.sync
                def _(sp):
                    sp.dma_start(memx, din["mem"]).then_inc(ld, 16)
                    fill(sp, "memld", l)
                    sp.wait_ge(ld, 16)

        def memory_kv(l):
            wt = slot("wkv").rearrange("p (k n) -> p k n", k=KT)
            gemm_stage("wkv", l, [("wkv" if t == 0 else None,
                                   [(lambda bank: bank, hT[:, k, t * P:t * P + P], wt[:, k, :]) for k in range(KT)],
                                   "ad"[t], copy_to(zm[:, t, :], 512), "wkv" if t == MT - 1 else None) for t in range(MT)])

        def head_norm_stage(stage, l, view, g, scratch):
            go, root = sem(f"{stage}_squares"), sem(f"{stage}_root")
            n = view.shape[1] * view.shape[2]
            with nc.Block() as block:
                @block.sync
                def _(sp):
                    fill(sp, stage, l)

                @block.scalar
                def _(act):
                    act.wait_ge(go, 1)
                    nc.scalar.activation(stat[:, 80:80 + n], stat[:, 0:n], ACT.Sqrt).then_inc(root, 1)

                @block.vector
                def _(dve):
                    head_norm(chain(dve, f"{stage}_dve"), [(view, g, 0, scratch)], n, root, go, HD)

        def memory_store(l):
            st = sem("memory_kv_stored")
            with nc.Block() as block:
                @block.sync
                def _(sp):
                    sp.dma_start(dout["mem"][bass.ds(l, 1)].rearrange("a p t c -> (a p) t c"), zm).then_inc(st, 16)
                    sp.wait_ge(st, 16)

        def cross_samples(l):
            q_ok, s_ok, mx, ex, pn, tp, tc, o_ok, o_used = [sem(f"xs_{n}") for n in
                ("queries", "scores", "maxima", "exponentials", "probs", "turned", "copied", "outputs", "outputs_read")]
            with nc.Block() as block:
                @block.sync
                def _(sp):
                    fill(sp, "xs", l, {f"mc{hb}": (o_ok, hb + 1) for hb in range(2)})

                @block.tensor
                def _(pe):
                    pe.wait_ge(q_ok, 1)
                    for hb in range(2):
                        arrived(pe, f"mc{hb}")
                        kv = slot(f"mc{hb}").rearrange("p (b w) -> p b w", b=4)
                        for b4 in range(4):
                            for e in range(2):
                                ins = nc.tensor.matmul(ps[32 * b4:32 * b4 + 32, 0, 0:MEM], qxb[:, e, 4 * hb + b4, :],
                                                       kv[:, b4, MEM * e:MEM * e + MEM], start=(e == 0), stop=(e == 1))
                        ins.then_inc(s_ok, 1)
                        pe.wait_ge(pn, hb + 1)
                        for i in range(2):
                            ins = nc.tensor.transpose(ps[:, 1, i * P:i * P + P], sx[:, i * P:i * P + P], ident)
                        ins.then_inc(tp, 1)
                        pe.wait_ge(tc, hb + 1)
                        if hb:
                            pe.wait_ge(o_used, 1)
                        for b4 in range(4):
                            for e in range(2):
                                c = P * e + 32 * b4
                                for i in range(2):
                                    v = kv[:, b4, 2 * MEM + MEM * i + P * e:2 * MEM + MEM * i + P * e + P]
                                    ins = nc.tensor.matmul(ps[:, 2, c:c + 32], v, pxT[:, i, 32 * b4:32 * b4 + 32],
                                                           start=(i == 0), stop=(i == 1))
                        ins.then_inc(o_ok, 1)

                @block.scalar
                def _(act):
                    for hb in range(2):
                        act.wait_ge(mx, hb + 1)
                        nc.scalar.activation(sx, ps[:, 0, 0:MEM], ACT.Exp, bias=stat[:, 0:1], accum_out=stat[:, 1:2]).then_inc(ex, 1)

                @block.vector
                def _(dve):
                    link = chain(dve, "xs_dve")
                    link(nc.vector.memset(qxb, 0.0))
                    link(nc.vector.memset(oxT[:, :, SEQ:], 0.0))
                    for h in range(XH):
                        p = slice(64 * (h % 2), 64 * (h % 2) + 64)
                        ins = nc.vector.tensor_copy(qxb[p, h // 2, :, 4 * h:4 * h + 4],
                                                    qxT[p, h // 2, SEQ:TOK].rearrange("p (b t) -> p b t", b=DB))
                        link(ins) if h < XH - 1 else ins.then_inc(q_ok, 1)
                    for hb in range(2):
                        dve.wait_ge(s_ok, hb + 1)
                        nc.vector.tensor_reduce(stat[:, 0:1], ps[:, 0, 0:MEM], AX.X, ALU.max, negate=True).then_inc(mx, 1)
                        dve.wait_ge(ex, hb + 1)
                        link(nc.vector.reciprocal(stat[:, 2:3], stat[:, 1:2]))
                        nc.vector.tensor_scalar(sx, sx, stat[:, 2:3], None, ALU.mult).then_inc(pn, 1)
                        dve.wait_ge(tp, hb + 1)
                        nc.vector.tensor_copy(pxT, ps[:, 1, 0:256].rearrange("p (i r) -> p i r", i=2)).then_inc(tc, 1)
                        dve.wait_ge(o_ok, hb + 1)
                        for h in range(XH):
                            p = slice(64 * (h % 2), 64 * (h % 2) + 64)
                            src = ps[p, 2, P * (h // 2):P * (h // 2) + P].rearrange("p (b w) -> p b w", b=4)[:, :, 4 * h:4 * h + 4]
                            dst = oxT[p, h // 2, SEQ + 16 * hb:SEQ + 16 * hb + 16].rearrange("p (b t) -> p b t", b=4)
                            ins = nc.vector.tensor_copy(dst, src)
                            link(ins) if h < XH - 1 else ins.then_inc(o_used, 1)

        hf = arena[:, 0:FF // P * TOK].rearrange("p (f t) -> p f t", f=FF // P)

        def mlp_hidden(l):
            def relu2(dst, n):
                def f(link, eng, bank):
                    if eng is nc.scalar:
                        link(nc.scalar.activation(dst, bank[:, 0:n], ACT.Relu))
                        return nc.scalar.activation(dst, dst, ACT.Square)
                    link(nc.vector.tensor_scalar(dst, bank[:, 0:n], 0.0, None, ALU.max))
                    return nc.vector.tensor_tensor(dst, dst, dst, ALU.mult)
                return f
            units = []
            for f in range(FF // P):
                name, q = f"w1_{f // 4}", f % 4
                wt = slot(name).rearrange("p (k n) -> p k n", k=KT)
                for part, (a, w) in enumerate(((0, SEQ), (SEQ, NS))):
                    mms = [(lambda bank, w=w: bank[:, 0:w], wt[:, k, q * P:q * P + P], hT[:, k, a:a + w]) for k in range(KT)]
                    units.append((name if q == 0 and part == 0 else None, mms, "ad"[f % 2], relu2(hf[:, f, a:a + w], w),
                                  name if q == 3 and part == 1 else None))
            gemm_stage("mlp1", l, units)

        def mlp_out(l):
            prod, ev, rd = sem("mlp2_products"), sem("mlp2_added"), sem("mlp2_weights_read")
            bank = lambda half, t: (5 * half + t) % 8
            with nc.Block() as block:
                @block.sync
                def _(sp):
                    fill(sp, "mlp2", l, {f"w2_{4 * h + c}": (rd, 3 * h + c + 1) if c < 3 else (prod, TT * (h + 1))
                                         for h in range(2) for c in range(4)})

                @block.tensor
                def _(pe):
                    for half in range(2):
                        for c in range(4):
                            name = f"w2_{4 * half + c}"
                            arrived(pe, name)
                            wt = slot(name).rearrange("p (f n) -> p f n", f=8)
                            for t in range(TT):
                                w = P if t < TP else NS
                                if half and c == 0 and t >= 3:
                                    pe.wait_ge(ev, t - 2)
                                for f in range(8):
                                    ins = nc.tensor.matmul(ps[0:w, bank(half, t), :], hf[:, 8 * c + f, t * P:t * P + w],
                                                           wt[:, f, :], start=(c == 0 and f == 0), stop=(c == 3 and f == 7))
                                if c == 3:
                                    ins.then_inc(prod, 1)
                            if c < 3:
                                ins.then_inc(rd, 1)

                @block.vector
                def _(dve):
                    for half in range(2):
                        for t in range(TT):
                            w = P if t < TP else NS
                            dve.wait_ge(prod, 5 * half + t + 1)
                            dst = x[0:w, t, 512 * half:512 * half + 512]
                            nc.vector.tensor_tensor(dst, ps[0:w, bank(half, t), :], dst, ALU.add).then_inc(ev, 1)

        first, prm_ld, done = whole("inputs_loaded"), whole("parameters_loaded"), whole("tokens_stored")
        with nc.Block() as block:
            @block.sync
            def _(sp):
                sp.dma_start(pages[:, :], din["pages"]).then_inc(first, 16)
                sp.dma_start(cst[:, :], din["consts"]).then_inc(first, 16)
                sp.dma_start(x[:, :, :], din["x"]).then_inc(first, 16)
                sp.wait_ge(first, 48)

        def output_projection(l):
            units = []
            for c in range(2):
                wt = slot(f"w_out{c}").rearrange("p (k n) -> p k n", k=KT)
                for t in range(TT):
                    mms = [(lambda bank: bank, hT[:, k, t * P:t * P + P], wt[:, k, :]) for k in range(KT)]
                    units.append((f"w_out{c}" if t == 0 else None, mms, "d", add_to(x[:, t, 512 * c:512 * c + 512], 512),
                                  f"w_out{c}" if t == TT - 1 else None))
            gemm_stage("out", l, units)

        def cross_queries(l):
            wq = slot("wqo")[:, 0:2048].rearrange("p (k n) -> p k n", k=KT)
            gemm_stage("wq", l, [("wqo" if t == 0 else None,
                                  [(lambda bank: bank[:, 0:256], hT[:, k, t * P:t * P + P], wq[:, k, :]) for k in range(KT)],
                                  "ad"[t % 2], copy_to(zx[:, t, :], 256), None) for t in range(TT)])

        def cross_output(l):
            wo = slot("wqo")[:, 2048:4096].rearrange("p (k n) -> p k n", k=2)
            units = []
            for t in range(TT):
                for c in range(2):
                    mms = [(lambda bank: bank, oxT[:, k, t * P:t * P + P], wo[:, k, 512 * c:512 * c + 512]) for k in range(2)]
                    units.append((None, mms, "d", add_to(x[:, t, 512 * c:512 * c + 512], 512),
                                  "wqo" if (t, c) == (TT - 1, 1) else None))
            gemm_stage("wo", l, units)

        with nc.Fori(0, DEPTH) as l:
            with nc.Block() as block:
                @block.sync
                def _(sp):
                    sp.dma_start(prm[:, :], din["prm"][bass.ds(l, 1)].rearrange("a p w -> (a p) w")).then_inc(prm_ld, 16)
                    sp.wait_ge(prm_ld, 16)
            norm_stage("norm1", l, x[:, :, :], TT, 0)
            input_projection(l)
            post_stage(l)
            sample_compress(l)
            gates_stage(l)
            prompt_mlstm(l)
            sample_mlstm(l)
            finish_mlstm(l)
            prep_stage(l)
            prompt_compress(l)
            prompt_attention(l)
            sample_attention(l, 0)
            sample_attention(l, 1)
            sample_merge(l)
            turn_stage("mix", l, TT, lambda t: [z[:, t, ZQ + P * k:ZQ + P * k + P] for k in range(4)]
                       + [z[:, t, ZO + P * k:ZO + P * k + P] for k in range(4)], hT)
            output_projection(l)
            clear()
            memory_load(l)
            norm_stage("memn", l, memx, MT, 2)
            memory_kv(l)
            head_norm_stage("memk", l, zm[:, :, 0:256].rearrange("p t (h d) -> p t h d", h=XH), pr("xk"),
                            xsq[:, 0:512].rearrange("p (t h d) -> p t h d", t=MT, h=XH))
            memory_store(l)
            turn_stage("memT", l, MT, lambda t: [zm[:, t, P * e:P * e + P] for e in range(2)], kmT)
            norm_stage("norm2", l, x[:, :, :], TT, 1)
            cross_queries(l)
            head_norm_stage("xprep", l, zx.rearrange("p t (h d) -> p t h d", h=XH), pr("xq"),
                            xsq.rearrange("p (t h d) -> p t h d", t=TT, h=XH))
            turn_stage("xqT", l, TT, lambda t: [zx[:, t, P * e:P * e + P] for e in range(2)], qxT, QSC)
            tile_attention("xatt", l, [
                (qxT[64 * (h % 2):64 * (h % 2) + 64, h // 2, t * P:t * P + P], kmT[64 * (h % 2):64 * (h % 2) + 64, h // 2, :],
                 MEM, False, [zm[:, i, 256 + 64 * h:320 + 64 * h] for i in range(MT)], 64, None,
                 ox[:, t, 64 * h:64 * h + 64], False) for t in range(TP) for h in range(XH)])
            cross_samples(l)
            turn_stage("xT", l, TP, lambda t: [ox[:, t, P * e:P * e + P] for e in range(2)], oxT)
            cross_output(l)
            norm_stage("norm3", l, x[:, :, :], TT, 3)
            mlp_hidden(l)
            mlp_out(l)
            clear(loaded + [prm_ld])

        with nc.Block() as block:
            @block.sync
            def _(sp):
                sp.dma_start(dout["y"], x[:, :, :]).then_inc(done, 16)
                sp.wait_ge(done, 16)
    return nc


def constants():
    c = np.zeros((P, NCST), np.float32)
    put = lambda n, a: c.__setitem__((slice(0, a.shape[0]), slice(*CST[n])), a)
    p = np.arange(P)
    put("id", np.eye(P, dtype=np.float32))
    put("causal", np.where(p[None, :] <= p[:, None], 0.0, NEG).astype(np.float32))
    put("tri", (p[:, None] <= p[None, :]).astype(np.float32))
    half = HD // 8
    freqs = np.float32(500000.0) ** (-np.arange(half, dtype=np.float32) / np.float32(half))
    pos = np.zeros((TT, P), np.float32)
    pos[:TP] = np.arange(SEQ).reshape(TP, P)
    pos[TP, :NS] = PAST + np.arange(NS) % DS
    ang = (pos[:, :, None] * freqs.astype(np.float32)).astype(np.float32)
    put("cos", np.cos(ang).transpose(1, 0, 2).reshape(P, -1))
    put("sin", np.sin(ang).transpose(1, 0, 2).reshape(P, -1))
    end = np.arange(NC_P) * STRIDE + CMP_LEN - 1
    seen = (end[None, None, :] <= (np.arange(TP)[None, :, None] * P + p[:, None, None]))
    put("cma", np.where(seen, 0.0, NEG).reshape(P, -1))
    put("cmm", seen.astype(np.float32).reshape(P, -1))
    tok = np.arange(NS)
    b4, t = p // 32, p % DS
    new = np.stack([((tok[None, :] // DS == 4 * hb + b4[:, None]) & (tok[None, :] % DS <= t[:, None])) for hb in range(2)], 1)
    put("new", np.where(new, 0.0, NEG).reshape(P, -1))
    put("low", np.where(np.arange(4)[None, :] >= t[:, None], 0.0, NEG))
    put("ms", ((tok[:, None] // DS == tok[None, :] // DS) & (tok[:, None] <= tok[None, :])).astype(np.float32))
    put("ohb", (tok[:, None] // DS == np.arange(DB)[None, :]).astype(np.float32))
    key = (p // 16) * DS + t
    put("grp", (key[:, None] == key[None, :]).astype(np.float32))
    put("one", np.ones((P, 1), np.float32))
    return c


def lay_out(x_prompt, x_sample, mem_prompt, cache_nsa_kv, cache_win_kv, cache_mem_kv, state_mlstm_C, state_mlstm_n,
            state_mlstm_m, state_conv, page_table, norm_mix_g, w_in, nsa_qn_g, nsa_kn_g, cmp_pos, cmp_w1, cmp_w2,
            ml_conv_w, ml_conv_b, ml_gate_b, ml_hn_g, w_out, norm_xa_g, norm_mem_g, xa_wq, xa_wkv, xa_qn_g, xa_kn_g,
            xa_wo, norm_mlp_g, mlp_w1, mlp_w2):
    L = DEPTH
    a = {}
    xs = np.zeros((P, D), np.float32)
    xs[:NS] = x_sample.reshape(NS, D)
    a["x"] = np.concatenate([x_prompt.reshape(TP, P, D), xs[None]]).transpose(1, 0, 2)
    a["mem"] = mem_prompt.reshape(MT, P, D).transpose(1, 0, 2)
    a["pages"] = page_table.reshape(1, DB * NPG)
    a["consts"] = constants()
    gains = np.stack([norm_mix_g, norm_xa_g, norm_mem_g, norm_mlp_g], 1).reshape(L * 4, 1, D)
    a["gains"] = np.broadcast_to(gains, (L * 4, P, D))
    pm = np.zeros((L, P, NPRM), np.float32)

    def put(n, v, rows=P):
        pm[:, :rows, slice(*PRM[n])] = v
    put("qn", nsa_qn_g[:, None, :])
    put("kn", nsa_kn_g.reshape(L, 1, 192))
    put("hn", ml_hn_g[:, None, :])
    put("xq", xa_qn_g[:, None, :])
    put("xk", xa_kn_g[:, None, :])
    put("cw", ml_conv_w.reshape(L, 4, KT, P).transpose(0, 3, 2, 1).reshape(L, P, 32))
    put("cb", ml_conv_b.reshape(L, KT, P).transpose(0, 2, 1))
    put("bi", ml_gate_b[:, :MH, None], MH)
    put("bf", ml_gate_b[:, MH:, None], MH)
    put("w2", cmp_w2.transpose(0, 2, 1, 3).reshape(L, P, 128))
    put("pos", cmp_pos.reshape(L, 2, J, P).transpose(0, 3, 1, 2).reshape(L, P, 32))
    a["prm"] = pm
    cols = lambda w, k: w.reshape(L, k, P, -1).transpose(0, 2, 1, 3)
    q, kv, g, qk, v, o, f = np.split(w_in, np.cumsum([512, 768, 24, 1024, 512, 512]).tolist(), axis=-1)
    q = q.reshape(L, D, G, HG, HD).transpose(0, 1, 3, 2, 4).reshape(L, D, 512)
    g = g.reshape(L, D, G, HG, 3).transpose(0, 1, 3, 2, 4).reshape(L, D, 24)
    wa = w_out[:, :512].reshape(L, G, HG, HD, D).transpose(0, 2, 1, 3, 4).reshape(L, 512, D)
    w_out = np.concatenate([wa, w_out[:, 512:]], 1)
    wi = cols(np.concatenate([q, kv, v, o, g, f], -1), KT)
    wqk, wo_, w1, w2 = cols(qk, KT), cols(w_out, KT), cols(mlp_w1, KT), cols(mlp_w2, FF // P)
    ch = {f"in{i}": wi[..., NZ * i:NZ * i + NZ] for i in range(5)}
    for i in range(2):
        ch[f"qk{i}"] = wqk[..., 512 * i:512 * i + 512]
        ch[f"w_out{i}"] = wo_[..., 512 * i:512 * i + 512]
    ch["cmpw"] = cmp_w1.reshape(L, 2, J, P, HID).transpose(0, 3, 1, 2, 4)
    ch["wkv"] = cols(xa_wkv, KT)
    ch["wqo"] = np.concatenate([cols(xa_wq, KT).reshape(L, P, -1), cols(xa_wo, 2).reshape(L, P, -1)], -1)
    for i in range(8):
        ch[f"w1_{i}"] = w1[..., 512 * i:512 * i + 512]
        ch[f"w2_{i}"] = w2[:, :, 8 * (i % 4):8 * (i % 4) + 8, 512 * (i // 4):512 * (i // 4) + 512]
    a["wst"] = np.concatenate([ch[n].reshape(L, -1) for n, _ in CHUNKS], 1)
    c = cache_nsa_kv.reshape(POOL, PAGE // 2, 2, L, 4, G, HD)
    a["cx"] = c[:, :, :, :, 0:2].transpose(3, 0, 2, 6, 1, 4, 5).reshape(L * POOL, P, 256)
    c = cache_nsa_kv.reshape(POOL, PAGE, L, 4, P)
    a["kx"] = c[:, :, :, 2].transpose(2, 0, 3, 1).reshape(L * POOL, P, P)
    a["vx"] = c[:, :, :, 3].transpose(2, 0, 1, 3).reshape(L * POOL, P, P)
    w = cache_win_kv.reshape(L * DB, WIN, 2 * P)
    a["win"] = w
    a["winT"] = w[:, :, 0:P].transpose(0, 2, 1)
    m = cache_mem_kv.reshape(L, 2, 4, MEM, 2, 2, P)
    k_ = m[:, :, :, :, 0].transpose(0, 1, 5, 2, 4, 3)
    v_ = m[:, :, :, :, 1].reshape(L, 2, 4, MT, P, 2, P).transpose(0, 1, 4, 2, 3, 5, 6)
    a["mkv"] = np.concatenate([k_.reshape(L, 2, P, 4, 512), v_.reshape(L, 2, P, 4, 512)], -1).reshape(L * 2, P, 4096)
    a["cT"] = state_mlstm_C.transpose(0, 4, 2, 1, 3).reshape(L, P, 4096)
    a["nT"] = state_mlstm_n.transpose(0, 3, 2, 1).reshape(L, P, MH * DB)
    a["mT"] = state_mlstm_m.transpose(0, 2, 1)
    a["convT"] = state_conv.reshape(L, DB, 3, KT, P).transpose(0, 4, 3, 1, 2).reshape(L, P, KT * DB * 3)
    return {n: np.ascontiguousarray(v) for n, v in a.items()}


OUTS = {
    "y": (P, TT, D), "nsa_p": (DEPTH, P, TP, 512), "nsa_s": (DEPTH, NS, 512), "win_p": (DEPTH, P, TP, 256),
    "win_s": (DEPTH * DB, WIN, 256), "convT": (DEPTH, P, KT, NS + 3), "mT": (DEPTH, MH, TOK),
    "cT_p": (DEPTH, P, MH, 129), "cT_s": (DEPTH, P, 4096), "nT": (DEPTH, P, MH * DB), "mem": (DEPTH, P, MT, 512),
}


def kernel(**inputs):
    import concourse.bacc as _bacc
    from concourse.bass_utils import run_bass_kernel_spmd as _run

    arrays = lay_out(**{n: np.asarray(v) for n, v in inputs.items()})
    nc = _bacc.Bacc("TRN2", target_bir_lowering=False, num_devices=1)
    din = {n: nc.dram_tensor(f"in_{n}", v.shape, mybir.dt.from_np(v.dtype), kind="ExternalInput").ap()
           for n, v in arrays.items()}
    dout = {n: nc.dram_tensor(f"out_{n}", s, F32, kind="ExternalOutput").ap() for n, s in OUTS.items()}
    build(nc, din, dout)
    r = _run(nc, [{f"in_{n}": v for n, v in arrays.items()}], core_ids=[0])
    o = {n: np.asarray(r.results[0][f"out_{n}"]) for n in OUTS}
    L = DEPTH
    rows = o["y"].transpose(1, 0, 2)
    tok = lambda n, w: o[n].transpose(0, 2, 1, 3).reshape(L, SEQ, w)
    ct = o["cT_p"]
    cs_ = o["cT_s"].reshape(L, P, MH, DB, MD)
    cv = o["convT"]
    return (
        rows[:TP].reshape(1, SEQ, D), rows[TP, :NS].reshape(DB, DS, D),
        tok("nsa_p", 512).transpose(1, 0, 2).reshape(1, SEQ, L, 4, G, HD),
        o["nsa_s"].reshape(L, DB, DS, 4, G, HD).transpose(1, 2, 0, 3, 4, 5),
        tok("win_p", 256).reshape(L, 1, WIN, 2, G, HD),
        o["win_s"].reshape(L, DB, WIN, 2, G, HD),
        ct[..., 0:MD].transpose(0, 2, 3, 1).reshape(L, 1, MH, MD, MD),
        cs_.transpose(0, 3, 2, 4, 1),
        ct[..., MD].transpose(0, 2, 1).reshape(L, 1, MH, MD),
        o["nT"].reshape(L, MD, MH, DB).transpose(0, 3, 2, 1),
        o["mT"][:, :, SEQ - 1].reshape(L, 1, MH),
        o["mT"][:, :, SEQ + DS - 1::DS].transpose(0, 2, 1),
        cv[..., 0:3].transpose(0, 3, 2, 1).reshape(L, 1, 3, KT * P),
        cv[..., 3:].reshape(L, P, KT, DB, DS)[..., 1:].transpose(0, 3, 4, 2, 1).reshape(L, DB, 3, KT * P),
        o["mem"].transpose(0, 2, 1, 3).reshape(L, 1, MEM, 2, XH, HD),
    )
```

```python
from contextlib import ExitStack

import numpy as np

import concourse.bass as bass
from concourse import mybir

F32 = mybir.dt.float32
I32 = mybir.dt.int32
ALU = mybir.AluOpType
ACT = mybir.ActivationFunctionType
AX = mybir.AxisListType

P = 128
D = 1024
KT = D // P
SEQ, DB, DS = 512, 8, 4
NS = DB * DS
TP = SEQ // P
TT = TP + 1
TOK = SEQ + NS
DEPTH = 2
PAST, PAGE = 2048, 128
NPG = PAST // PAGE
POOL = DB * NPG * 5 // 4
HEADS, G, HG, HD = 8, 2, 4, 64
CMP_LEN, STRIDE, HID = 32, 16, 128
J = CMP_LEN // 2
NC_P = (SEQ - CMP_LEN) // STRIDE + 1
NC_S = (PAST + DS - CMP_LEN) // STRIDE + 1
SELB = 64
WIN = 512
MH, MD = 4, 128
XH = 4
MEM = 256
MT = MEM // P
FF = 4 * D
EPS = 1e-6
NEG = -1.0e30
BIG = 1.0e30

ZQ, ZK, ZV, ZO, ZG, ZI = 0, 512, 1280, 1792, 2304, 2328
ZW = 2336
NZ = 512

PRM = {}
_at = 0
for _n, _w in (("qn", 64), ("kn", 192), ("hn", 128), ("xq", 64), ("xk", 64), ("cw", 32), ("cb", 8),
               ("bi", 1), ("bf", 1), ("w2", 128), ("pos", 32)):
    PRM[_n] = (_at, _at + _w)
    _at += _w
NPRM = _at

CST = {}
_at = 0
for _n, _w in (("id", 128), ("causal", 128), ("tri", 128), ("cos", 40), ("sin", 40), ("cma", 4 * NC_P),
               ("cmm", 4 * NC_P), ("new", 64), ("low", 4), ("ms", 32), ("ohb", 8), ("grp", 128), ("one", 1),
               ("xnew", 4)):
    CST[_n] = (_at, _at + _w)
    _at += _w
NCST = _at

CHUNKS = [(f"in{i}", NZ * KT) for i in range(4)] + [("in4", (ZW - 4 * NZ) * KT), ("qk0", 4096), ("qk1", 4096),
          ("cmpw", 4096), ("w_out0", 4096), ("w_out1", 4096), ("wkv", 4096), ("wqo", 4096)] \
    + [(f"w1_{i}", 4096) for i in range(8)] + [(f"w2_{i}", 4096) for i in range(8)]
CH_AT = {}
_at = 0
for _n, _w in CHUNKS:
    CH_AT[_n] = (_at, _w)
    _at += P * _w
WTOT = _at

ORDER = ["in0", "in1", "in2", "in3", "in4", "qk0", "qk1", "cmpw"] + [f"cmp{b}" for b in range(DB)] + ["cst"]
for _g in range(2):
    ORDER += [f"k{2 * _g}", f"k{2 * _g + 1}", f"win{_g}", f"v{2 * _g}", f"v{2 * _g + 1}"]
ORDER += ["w_out0", "w_out1", "wkv", "wqo", "mc0", "mc1"] + [f"w1_{i}" for i in range(8)] + [f"w2_{i}" for i in range(8)]
FIRST_LOADS, SECOND_LOADS = ORDER[:ORDER.index("w1_0")], ORDER[ORDER.index("w1_0"):]
SLOT = {}
for _i, _n in enumerate(ORDER):
    if _n == "cmpw":
        SLOT[_n] = 3
        _rot = 0
    elif _n.startswith("cmp") or _n == "cst":
        SLOT[_n] = _rot % 3
        _rot += 1
    elif _i < ORDER.index("cmpw"):
        SLOT[_n] = _i % 4
    else:
        SLOT[_n] = (_i + 1) % 4


def slot_users():
    before, last = {}, {}
    for n in ORDER:
        before[n] = last.get(SLOT[n])
        last[SLOT[n]] = n
    return before


GATHERED = [f"cmp{b}" for b in range(1, DB, 2)] + [f"{k}{i}" for g in range(2) for k in "kv" for i in (2 * g, 2 * g + 1)]
ARRIVALS = {n: 16 * (NPG if n[:3] == "cmp" else 2) for n in GATHERED}


class Stage:

    def __init__(self):
        self.parts = {}

    def tensor(self, part):
        self.parts["pe"] = part

    def scalar(self, part):
        self.parts["act"] = part

    def vector(self, part):
        self.parts["dve"] = part


def build(nc, din, dout):
    before = slot_users()
    with ExitStack() as ctx:
        sb = lambda name, shape, dt=F32: ctx.enter_context(nc.sbuf_tensor(name, shape, dt))
        whole = lambda name: ctx.enter_context(nc.semaphore(name))
        layer_sems = []
        half = {"held": ExitStack(), "sems": []}

        def through_layer(name):
            layer_sems.append(whole(name))
            return layer_sems[-1]

        def sem(name):
            half["sems"].append(half["held"].enter_context(nc.semaphore(name)))
            return half["sems"][-1]

        x = sb("x", [P, TT, D])
        hT = sb("hT", [P, KT, TT * P])
        ring = sb("ring", [P, 4, 4096])
        arena = sb("arena", [P, TT * ZW + 2 * KT * TOK])
        hn = sb("hn", [P, 2, D])
        gain = sb("gain", [P, D])
        prm = sb("prm", [P, NPRM])
        cst = sb("cst", [P, NCST])
        stat = sb("stat", [P, 160])
        cols = sb("cols", [P, 128])
        pages = sb("pages", [1, DB * NPG], I32)
        row = sb("row", [P, DB], I32)
        gpage = sb("gpage", [P, 2 * DB], I32)
        ps = ctx.enter_context(nc.psum_tensor("ps", [P, 8, 512], F32))

        z = arena[:, 0:TT * ZW].rearrange("p (t w) -> p t w", t=TT)
        _o = TT * ZW
        zqkT = arena[:, _o:_o + KT * TOK].rearrange("p (c t) -> p c t", c=KT)
        qkT = arena[:, _o + KT * TOK:_o + 2 * KT * TOK].rearrange("p (c t) -> p c t", c=KT)
        hTf = hT[:, :, :].rearrange("p k t -> p (k t)")
        ropf = arena[:, _o:_o + KT * TOK]
        qkf = arena[:, _o + KT * TOK:_o + 2 * KT * TOK]

        def pr(n, rows=P):
            return prm[0:rows, PRM[n][0]:PRM[n][1]]

        def cs(n, rows=P):
            return cst[0:rows, CST[n][0]:CST[n][1]]

        ident = cs("id")
        loaded = [through_layer(f"slot_loaded{i}") for i in range(4)]
        gathered = whole("pages_arrived")
        idx_ok, gathers_in = through_layer("gather_rows_ready"), through_layer("gathers_arrived")
        win_moved = through_layer("window_rows_moved")
        prm_ld, m0_ld, n_ld, mem_ld = [through_layer(f"{n}_loaded") for n in ("parameters", "mlstm_m", "mlstm_n", "memory")]
        rows_normed, kv_st = through_layer("keys_values_ready"), through_layer("keys_values_stored")
        conv_st, m_st, ctp_st, cts_st, mem_st = [through_layer(f"{n}_stored") for n in
            ("conv_state", "mlstm_m", "prompt_c", "sample_c_n", "memory_kv")]
        KV_STORES, CTS_STORES = 3 + DB, MH + 1
        met = {e: through_layer(f"{e}_stages_done") for e in ("pe", "act", "dve")}
        stages, read_at = [], {}
        in_slot = [0] * 4
        loaded_at = {}
        for n in ORDER:
            if n not in GATHERED:
                in_slot[SLOT[n]] += 16 * (NPG if n[:3] == "cmp" and n != "cmpw" else 8 if n[:3] == "win" else 1)
                loaded_at[n] = in_slot[SLOT[n]]

        def slot(n):
            return ring[:, SLOT[n], :]

        def arrived(eng, n):
            if n in GATHERED:
                eng.wait_ge(gathers_in, GATHERED.index(n) + 1)
            else:
                eng.wait_ge(loaded[SLOT[n]], loaded_at[n])

        class Chain:

            def __init__(self, done):
                self.done, self.count = done, 0

            def __call__(self, eng):
                def link(ins):
                    self.count += 1
                    ins.then_inc(self.done, 1)
                    eng.wait_ge(self.done, self.count)
                return link

        act_chain, dve_chain = Chain(through_layer("act_step_done")), Chain(through_layer("dve_step_done"))
        idx_chain = Chain(whole("rows_step_done"))

        def new_stage():
            stages.append(Stage())
            return stages[-1]

        def meet(eng, name, count):
            eng.drain().then_inc(met[name], 1)
            for other in met:
                if other != name:
                    eng.wait_ge(met[other], count)

        def store_keys_values(sp, l):
            sp.wait_ge(rows_normed, 1)
            sp.dma_start(dout["nsa_p"][bass.ds(l, 1)].rearrange("a p t c -> (a p) t c"),
                         z[:, 0:TP, ZK:ZK + 512]).then_inc(kv_st, 16)
            sp.dma_start(dout["nsa_s"][bass.ds(l, 1)].rearrange("a r c -> (a r) c"),
                         z[0:NS, TP, ZK:ZK + 512]).then_inc(kv_st, 16)
            sp.dma_start(dout["win_p"][bass.ds(l, 1)].rearrange("a p t c -> (a p) t c"),
                         z[:, 0:TP, ZK + 512:ZK + 768]).then_inc(kv_st, 16)
            for b in range(DB):
                sp.dma_start(dout["win_s"][bass.ds(l * DB + b, 1), WIN - DS:WIN].rearrange("a r c -> (a r) c"),
                             z[4 * b:4 * b + 4, TP, ZK + 512:ZK + 768]).then_inc(kv_st, 16)

        def load_pages(eng, l, n, arrives):
            first_page = NPG * int(n[3:])
            with eng.Fori(0, NPG // 4) as i:
                for j in range(4):
                    page = eng.value_load(pages[0:1, bass.ds(i * 4 + (first_page + j), 1)], min_val=0, max_val=POOL - 1)
                    src = din["cx"][bass.ds(page + l * POOL, 1)].rearrange("a p w -> (a p) w")
                    eng.dma_start(slot(n)[:, bass.ds(i * 1024 + 256 * j, 256)], src).then_inc(arrives, 16)

        def fill_ring(sp, l, loads):
            for n in loads:
                if n in GATHERED:
                    continue
                if n == "cst":
                    store_keys_values(sp, l)
                if n == "win0":
                    for b in range(DB):
                        sp.dma_start(dout["win_s"][bass.ds(l * DB + b, 1), 0:WIN - DS],
                                     din["win"][bass.ds(l * DB + b, 1), DS:WIN]).then_inc(win_moved, 16)
                s = SLOT[n]
                if before[n]:
                    sp.wait_ge(*read_at[before[n]])
                dst = ring[:, s, :]
                if n in CH_AT:
                    at, w = CH_AT[n]
                    src = din["wst"][bass.ds(l, 1), at:at + P * w].rearrange("a (p w) -> (a p) w", p=P)
                    sp.dma_start(dst[:, 0:w], src).then_inc(loaded[s], 16)
                elif n == "cst":
                    sp.dma_start(dst, din["cT"][bass.ds(l, 1)].rearrange("a p w -> (a p) w")).then_inc(loaded[s], 16)
                elif n[:2] == "mc":
                    g = int(n[2:])
                    src = din["mkv"][bass.ds(l * 2 + g, 1)].rearrange("a p w -> (a p) w")
                    sp.dma_start(dst, src).then_inc(loaded[s], 16)
                elif n[:3] == "win":
                    g = int(n[3:])
                    for b in range(4):
                        src = din["winT"][bass.ds(l * DB + 4 * g + b, 1)].rearrange("a p w -> (a p) w")
                        sp.dma_start(dst[:, 512 * b:512 * b + 512], src).then_inc(loaded[s], 16)
                        src = din["win"][bass.ds(l * DB + 4 * g + b, 1), :, 128:256]
                        src = src.rearrange("a (t p) c -> p (a t) c", p=P)
                        sp.dma_start(dst[:, 2048 + 512 * b:2560 + 512 * b].rearrange("p (t c) -> p t c", t=4),
                                     src).then_inc(loaded[s], 16)
                else:
                    load_pages(sp, l, n, loaded[s])

        def gather_pages(pool, l):
            count = 0
            pool.wait_ge(idx_ok, 1)
            for i, n in enumerate(GATHERED):
                pool.wait_ge(*read_at[before[n]])
                if n[:3] == "cmp":
                    load_pages(pool, l, n, gathered)
                for h in range(0 if n[:3] == "cmp" else 2):
                    b = 2 * int(n[1:]) + h
                    pool.indirect_dma_start(
                        out=ring[:, SLOT[n], 2048 * h:2048 * h + 2048], out_offset=None, in_=din[n[0] + "x"],
                        in_offset=bass.IndirectOffsetOnAxis(ap=row[:, b:b + 1], axis=0)).then_inc(gathered, 16)
                count += ARRIVALS[n]
                pool.wait_ge(gathered, l * sum(ARRIVALS.values()) + count)
                pool.sem_inc(gathers_in, 1)

        gain_ld = [None] + [through_layer(f"gain{i}_loaded") for i in range(1, 4)]

        def load_parameters(eng, l, sem_of):
            eng.dma_start(prm[:, :], din["prm"][bass.ds(l, 1)].rearrange("a p w -> (a p) w")).then_inc(sem_of, 16)
            eng.dma_start(gain[:, :], din["gains"][bass.ds(l * 4, 1)].rearrange("a p w -> (a p) w")).then_inc(sem_of, 16)

        def load_gain(act, l, i):
            g = din["gains"][bass.ds(l * 4 + i, 1)].rearrange("a p w -> (a p) w")
            act.dma_start(gain[:, :], g).then_inc(gain_ld[i], 16)

        def products(mms, bank):
            groups = len({m[0][0].start for m in mms})
            for m, ((rows, n), a, b) in enumerate(mms):
                ins = nc.tensor.matmul(bank[rows, 0:n], a, b, start=(m < groups), stop=(m >= len(mms) - groups))
            return ins

        def token_products(t, actT, k_tiles, weights, n):
            if t < TP:
                return [((slice(0, P), n), actT[:, k, t * P:t * P + P], weights(k)) for k in range(k_tiles)]
            return [((slice(NS * (k % 4), NS * (k % 4) + NS), n), actT[:, k, SEQ:TOK], weights(k)) for k in range(k_tiles)]

        def sum_groups(dst, n, groups=4, onto=False):
            def f(link, eng, bank):
                for q in range(groups):
                    src = bank[NS * q:NS * q + NS, 0:n]
                    ins = (nc.vector.tensor_tensor(dst, src, dst, ALU.add) if q or onto else nc.vector.tensor_copy(dst, src))
                    if q < groups - 1:
                        link(ins)
                return ins
            return f

        def norm_gemm_stage(stage, l, src, tiles, gain_i, units, needs, act_first=None, act_last=None,
                            padding=None):
            ssq, msq, rt, hn_ok, tp, ea, ed, prod = [sem(f"{stage}_{n}") for n in
                ("squares", "mean", "root", "rows_ready", "turned", "copied_a", "copied_d", "products")]
            ev = {e: sem(f"{stage}_evicted_{e}") for e in "ad"}
            BANKS = 4
            nth, cnt, steps, t = [], {"a": 0, "d": 0}, [], 0
            for i, u in enumerate(units):
                cnt[u[2]] += 1
                nth.append(cnt[u[2]])
                while t < min(needs[i] + 2, tiles):
                    steps.append(("tile", t))
                    t += 1
                steps.append(("unit", i))
            read_at.update({u[4]: (prod, i + 1) for i, u in enumerate(units) if u[4]})
            bank = lambda i: ps[:, 4 + i % BANKS, :]
            half_tile = lambda t, h: ps[:, 2 * (t % 2) + h, :].rearrange("p (k t) -> p k t", k=4)
            block = new_stage()

            @block.tensor
            def _(pe):
                for kind, i in steps:
                    if kind == "tile":
                        pe.wait_ge(hn_ok, i + 1)
                        if i >= 2:
                            pe.wait_ge(ea, i - 1)
                            pe.wait_ge(ed, i - 1)
                        for k in range(8):
                            ins = nc.tensor.transpose(ps[:, 2 * (i % 2) + k // 4, (k % 4) * P:(k % 4) * P + P],
                                                      hn[:, i % 2, k * P:k * P + P], ident)
                            if k % 4 == 3:
                                ins.then_inc(tp, 1)
                        continue
                    load, mms = units[i][0:2]
                    if load:
                        arrived(pe, load)
                    if i == 0 or needs[i] > max(needs[:i]):
                        pe.wait_ge(ea, needs[i] + 1)
                        pe.wait_ge(ed, needs[i] + 1)
                    if i == 2:
                        pe.wait_ge(ssq, tiles)
                    if i >= BANKS:
                        pe.wait_ge(ev[units[i - BANKS][2]], nth[i - BANKS])
                    products(mms, bank(i)).then_inc(prod, 1)

            @block.scalar
            def _(act):
                if act_first:
                    act_first(act)
                link = act_chain(act)

                def square(t):
                    if t >= tiles:
                        return
                    if t:
                        act.wait_ge(ssq, t)
                    nc.scalar.activation(ps[:, 6:8, :], src[:, t, :].rearrange("p (b c) -> p b c", b=2), ACT.Square,
                                         accum_out=stat[:, t:t + 1]).then_inc(ssq, 1)

                def root(t):
                    if t >= tiles:
                        return
                    act.wait_ge(msq, t + 1)
                    nc.scalar.activation(stat[:, 24 + t:25 + t], stat[:, 16 + t:17 + t], ACT.Sqrt).then_inc(rt, 1)
                square(0)
                square(1)
                root(0)
                square(2)
                root(1)
                for kind, i in steps:
                    if kind == "tile":
                        act.wait_ge(tp, 2 * i + 1)
                        nc.scalar.copy(hT[:, 0:4, i * P:i * P + P], half_tile(i, 0)).then_inc(ea, 1)
                        square(i + 3)
                        root(i + 2)
                    elif units[i][2] == "a":
                        act.wait_ge(prod, i + 1)
                        units[i][3](link, nc.scalar, bank(i)).then_inc(ev["a"], 1)
                if act_last:
                    act_last(act)

            @block.vector
            def _(dve):
                link = dve_chain(dve)

                def mean(t):
                    if t >= tiles:
                        return
                    dve.wait_ge(ssq, t + 1)
                    nc.vector.tensor_scalar(stat[:, 16 + t:17 + t], stat[:, t:t + 1], 1.0 / D, EPS, ALU.mult,
                                            ALU.add).then_inc(msq, 1)

                def rows(t):
                    if t >= tiles:
                        return
                    dve.wait_ge(rt, t + 1)
                    link(nc.vector.reciprocal(stat[:, 32 + t:33 + t], stat[:, 24 + t:25 + t]))
                    if t >= 2:
                        dve.wait_ge(tp, 2 * t - 2)
                    nc.vector.scalar_tensor_tensor(out=hn[:, t % 2, :], in0=src[:, t, :],
                                                   scalar=stat[:, 32 + t:33 + t], in1=gain[:, :],
                                                   op0=ALU.mult, op1=ALU.mult).then_inc(hn_ok, 1)
                if padding is not None:
                    link(nc.vector.memset(padding, 0.0))
                mean(0)
                mean(1)
                if gain_i:
                    dve.wait_ge(gain_ld[gain_i], 16)
                rows(0)
                for kind, i in steps:
                    if kind == "tile":
                        mean(i + 2)
                        rows(i + 1)
                        dve.wait_ge(tp, 2 * i + 2)
                        nc.vector.tensor_copy(hT[:, 4:8, i * P:i * P + P], half_tile(i, 1)).then_inc(ed, 1)
                    elif units[i][2] == "d":
                        dve.wait_ge(prod, i + 1)
                        units[i][3](link, nc.vector, bank(i)).then_inc(ev["d"], 1)

        def gemm_stage(stage, l, units, act_first=None, act_last=None):
            prod, ev = sem(f"{stage}_products"), {e: sem(f"{stage}_evicted_{e}") for e in "ad"}
            nth, cnt = [], {"a": 0, "d": 0}
            for u in units:
                cnt[u[2]] += 1
                nth.append(cnt[u[2]])
            read_at.update({u[4]: (prod, i + 1) for i, u in enumerate(units) if u[4]})
            block = new_stage()
            @block.tensor
            def _(pe):
                for i, (load, mms, e, _, _) in enumerate(units):
                    if load:
                        arrived(pe, load)
                    if i >= 8:
                        pe.wait_ge(ev[units[i - 8][2]], nth[i - 8])
                    products(mms, ps[:, i % 8, :]).then_inc(prod, 1)

            @block.scalar
            def _(act):
                if act_first:
                    act_first(act)
                link = act_chain(act)
                for i, u in enumerate(units):
                    if u[2] == "a":
                        act.wait_ge(prod, i + 1)
                        u[3](link, nc.scalar, ps[:, i % 8, :]).then_inc(ev["a"], 1)
                if act_last:
                    act_last(act)

            @block.vector
            def _(dve):
                link = dve_chain(dve)
                for i, u in enumerate(units):
                    if u[2] == "d":
                        dve.wait_ge(prod, i + 1)
                        u[3](link, nc.vector, ps[:, i % 8, :]).then_inc(ev["d"], 1)

        def copy_to(dst, n):
            def f(link, eng, bank):
                src = bank[:, 0:n]
                return nc.scalar.copy(dst, src) if eng is nc.scalar else nc.vector.tensor_copy(dst, src)
            return f

        def add_to(dst, n):
            return lambda link, eng, bank: nc.vector.tensor_tensor(dst, bank[:, 0:n], dst, ALU.add)

        def head_norm(link, heads, nh_total, act_go, dve_go, width):
            for v, _, c, scratch in heads:
                t, h = v.shape[1], v.shape[2]
                link(nc.vector.tensor_tensor(scratch, v, v, ALU.mult))
                link(nc.vector.tensor_reduce(stat[:, c:c + t * h].rearrange("p (t h) -> p t h", t=t), scratch,
                                             AX.X, ALU.add))
            nc.vector.tensor_scalar(stat[:, 0:nh_total], stat[:, 0:nh_total], 1.0 / width, EPS, ALU.mult,
                                    ALU.add).then_inc(dve_go, 1)
            nc.vector.wait_ge(act_go, 1)
            link(nc.vector.reciprocal(stat[:, 80:80 + nh_total], stat[:, 80:80 + nh_total]))
            for v, g, c, _ in heads:
                t, h, w = v.shape[1], v.shape[2], v.shape[3]
                r = stat[:, 80 + c:80 + c + t * h].rearrange("p (t h o) -> p t h o", t=t, o=1)
                link(nc.vector.tensor_tensor(v, v, r.to_broadcast([P, t, h, w]), ALU.mult))
                gg = g.rearrange("p (a b w) -> p a b w", a=1, b=1).to_broadcast([P, t, h, w])
                link(nc.vector.tensor_tensor(v, v, gg, ALU.mult))


        HALVES = ((0, TOK // 2), (TOK // 2, TOK - TOK // 2))

        def input_projection(l):
            units, needs = [], []
            for c in range(5):
                w = min(NZ, ZW - NZ * c)
                wt = slot(f"in{c}")[:, 0:w * KT].rearrange("p (k n) -> p k n", k=KT)
                for t in range(TT):
                    mms = token_products(t, hT, KT, lambda k: wt[:, k, :], w)
                    a = NZ * c
                    needs.append(t)
                    units.append((f"in{c}" if t == 0 else None, mms, "d" if t == TP else "ad"[(c + t) % 2],
                                  copy_to(z[:, t, a:a + w], w) if t < TP else sum_groups(z[0:NS, TP, a:a + w], w),
                                  f"in{c}" if t == TT - 1 else None))
            for c in range(KT):
                name, q = f"qk{c // 4}", c % 4
                wt = slot(name).rearrange("p (k n) -> p k n", k=KT)
                for part, (a, w) in enumerate(HALVES):
                    mms = [((slice(0, P), w), wt[:, k, q * P:q * P + P], hT[:, k, a:a + w]) for k in range(KT)]
                    needs.append(TT - 1)
                    units.append((name if q == 0 and part == 0 else None, mms, "ad"[c % 2],
                                  copy_to(zqkT[:, c, a:a + w], w), name if q == 3 and part == 1 else None))
            norm_gemm_stage("in", l, x[:, :, :], TT, 0, units, needs, padding=z[:, TP, :])

        kc_s = hn[:, 0, :].rearrange("p (b c) -> p b c", b=DB)
        vc_s = hn[:, 1, :].rearrange("p (b c) -> p b c", b=DB)

        def compression(stage, jobs, with_bias):
            prod, hid_ok, pr2, ev2, bi, bi_ok = [sem(f"{stage}_{n}") for n in
                ("products", "hidden_ready", "outputs", "evicted", "position_bias", "bias_ready")]
            w1 = slot("cmpw").rearrange("p (k j n) -> p k j n", k=2, j=J)
            pos = pr("pos").rearrange("p (k j) -> p k j", k=2)
            w2 = pr("w2").rearrange("p (k d) -> p k d", k=2)
            hid = hTf[:, 3200:4224].rearrange("p (s c) -> p s c", s=2)
            read_at.update({job[0]: (prod, 2 * i + 2) for i, job in enumerate(jobs) if job[0]})
            read_at["cmpw"] = (prod, 2 * len(jobs))

            def tensor_program(pe):
                arrived(pe, "cmpw")
                if with_bias:
                    for k in range(2):
                        for j in range(J):
                            ins = nc.tensor.matmul(ps[:, 7, k:k + 1], w1[:, k, j, :], pos[:, k, j:j + 1],
                                                   start=(j == 0), stop=(j == J - 1))
                    ins.then_inc(bi, 1)

                def second(i):
                    n = jobs[i][2]
                    o = 4 + i % 2
                    pe.wait_ge(hid_ok, 2 * i + 2)
                    if i >= 2:
                        pe.wait_ge(ev2, 2 * (i - 1))
                    h = hid[:, i % 2, 0:4 * n].rearrange("p (k g c) -> p k g c", k=2, g=G)
                    for g in range(G):
                        nc.tensor.matmul(ps[64 * g:64 * g + 64, o, 0:n], w2[:, 0, :], h[:, 0, g, :],
                                         start=True, stop=True)
                    for g in range(G):
                        ins = nc.tensor.matmul(ps[0:n, o, 128 + 64 * g:192 + 64 * g], h[:, 1, g, :], w2[:, 1, :],
                                               start=True, stop=True)
                    ins.then_inc(pr2, 1)
                for i, (load, tok, n, _, _) in enumerate(jobs):
                    if load:
                        arrived(pe, load)
                    if i >= 2:
                        pe.wait_ge(hid_ok, 2 * i - 2)
                    for k in range(2):
                        for j in range(J):
                            v = tok.rearrange("p q (k g) -> p k g q", k=2)[:, k, :, j:j + 8 * (n - 1) + 1:8]
                            ins = nc.tensor.matmul(ps[:, 2 * (i % 2) + k, 0:G * n], w1[:, k, j, :], v,
                                                   start=(j == 0), stop=(j == J - 1))
                        ins.then_inc(prod, 1)
                    if i:
                        second(i - 1)
                second(len(jobs) - 1)

            def hidden(act, i):
                n = jobs[i][2]
                if i == 0 and with_bias:
                    act.wait_ge(bi_ok, 1)
                for k in range(2):
                    act.wait_ge(prod, 2 * i + k + 1)
                    if i >= 2 and k == 0:
                        act.wait_ge(pr2, i - 1)
                    nc.scalar.activation(hid[:, i % 2, 2 * k * n:2 * (k + 1) * n], ps[:, 2 * (i % 2) + k, 0:G * n],
                                         ACT.Silu, bias=stat[:, 158 + k:159 + k]).then_inc(hid_ok, 1)

            def bias(dve):
                dve.wait_ge(bi, 1)
                nc.vector.tensor_copy(stat[:, 158:160], ps[:, 7, 0:2]).then_inc(bi_ok, 1)

            def evict(dve, i):
                _, _, n, kc, vc = jobs[i]
                dve.wait_ge(pr2, i + 1)
                nc.vector.tensor_copy(kc, ps[:, 4 + i % 2, 0:n]).then_inc(ev2, 1)
                nc.vector.tensor_copy(vc, ps[0:n, 4 + i % 2, 128:256]).then_inc(ev2, 1)
            return tensor_program, hidden, bias, evict

        wpcol = cols[:, 48:64].rearrange("p (h t) -> p h t", h=MH)
        m0 = cols[0:MH, 64:64 + DB]
        nT = cols[:, 96:96 + MH * DB].rearrange("p (h b) -> p h b", h=MH)

        def post_stage(l):
            go, root, cv_ld, y0, y1, silu = [sem(f"post_{n}") for n in
                ("squares", "root", "state_loaded", "conv_begun", "conv_done", "silu_done")]
            tensor_program, hidden, bias, evict = compression("compress", [
                (f"cmp{b}", slot(f"cmp{b}").rearrange("p (q w) -> p q w", w=4), NC_S, kc_s[:, b, 0:NC_S],
                 vc_s[0:NC_S, b, :]) for b in range(DB)], True)
            sq = hTf[:, 0:2560]
            tail = hTf[:, 2560:3008].rearrange("p (c b u) -> p c b u", c=KT, b=DB)
            held = hTf[:, 3008:3200]
            q = z[:, :, ZQ:ZQ + 512].rearrange("p t (h d) -> p t h d", h=HEADS)
            ks = [z[:, :, ZK + 256 * r:ZK + 256 * r + 128].rearrange("p t (h d) -> p t h d", h=G) for r in range(3)]
            heads = [(q, pr("qn"), 0, sq.rearrange("p (t h d) -> p t h d", t=TT, h=HEADS))]
            heads += [(ks[r], prm[:, PRM["kn"][0] + 64 * r:PRM["kn"][0] + 64 * r + 64], 40 + 10 * r,
                       sq[:, 0:640].rearrange("p (t h d) -> p t h d", t=TT, h=G)) for r in range(3)]
            block = new_stage()

            @block.tensor
            def _(pe):
                tensor_program(pe)

            @block.scalar
            def _(act):
                link = act_chain(act)
                act.dma_start(held, din["convT"][bass.ds(l, 1)].rearrange("a p w -> (a p) w")).then_inc(cv_ld, 16)
                act.dma_start(dout["convT"][bass.ds(l, 1)].rearrange("a p c t -> (a p) c t"),
                              zqkT[:, :, SEQ - 3:TOK]).then_inc(conv_st, 16)
                act.dma_start(m0, din["mT"][bass.ds(l, 1)].rearrange("a p w -> (a p) w")).then_inc(m0_ld, 16)
                act.dma_start(nT, din["nT"][bass.ds(l, 1)].rearrange("a p (h b) -> (a p) h b", h=MH)).then_inc(n_ld, 16)
                for c in range(KT):
                    w3 = PRM["cw"][0] + 4 * c + 3
                    nc.scalar.activation(qkT[:, c, 0:SEQ], zqkT[:, c, 0:SEQ], ACT.Identity,
                                         bias=prm[:, PRM["cb"][0] + c:PRM["cb"][0] + c + 1],
                                         scale=prm[:, w3:w3 + 1]).then_inc(y0, 1)
                act.wait_ge(go, 1)
                nc.scalar.activation(stat[:, 80:150], stat[:, 0:70], ACT.Sqrt).then_inc(root, 1)
                link(nc.scalar.activation(z[:, :, ZO:ZI], z[:, :, ZO:ZI], ACT.Sigmoid))
                hidden(act, 0)
                hidden(act, 1)
                for c in range(KT):
                    act.wait_ge(y1, c + 1)
                    nc.scalar.activation(qkT[:, c, :], qkT[:, c, :], ACT.Silu).then_inc(silu, 1)
                    if c % 2:
                        hidden(act, 2 + c // 2)
                hidden(act, 6)
                hidden(act, 7)
                act.wait_ge(silu, KT)
                act.wait_ge(conv_st, 16)

            @block.vector
            def _(dve):
                link = dve_chain(dve)
                bias(dve)
                head_norm(link, heads, 70, root, go, HD)
                cos = cs("cos").rearrange("p (t o f) -> p t o f", t=TT, o=1)
                sin = cs("sin").rearrange("p (t o f) -> p t o f", t=TT, o=1)
                for v, h in [(q, HEADS)] + [(k, G) for k in ks]:
                    a, b = v[:, :, :, 0:8], v[:, :, :, 8:16]
                    t = [sq[:, 320 * i:320 * i + TT * h * 8].rearrange("p (t h f) -> p t h f", t=TT, h=h) for i in range(4)]
                    cb, sb_ = cos.to_broadcast([P, TT, h, 8]), sin.to_broadcast([P, TT, h, 8])
                    link(nc.vector.tensor_tensor(t[0], a, cb, ALU.mult))
                    link(nc.vector.tensor_tensor(t[1], b, sb_, ALU.mult))
                    link(nc.vector.tensor_tensor(t[2], b, cb, ALU.mult))
                    link(nc.vector.tensor_tensor(t[3], a, sb_, ALU.mult))
                    link(nc.vector.tensor_tensor(a, t[0], t[1], ALU.subtract))
                    link(nc.vector.tensor_tensor(b, t[2], t[3], ALU.add))
                nc.vector.tensor_copy(stat[:, 0:1], stat[:, 1:2]).then_inc(rows_normed, 1)
                evict(dve, 0)
                dve.wait_ge(cv_ld, 16)
                link(nc.vector.tensor_copy(tail[:, :, :, 0:3], held.rearrange("p (c b u) -> p c b u", c=KT, b=DB)))
                link(nc.vector.tensor_copy(tail[:, :, :, 3:7],
                                           zqkT[:, :, SEQ:TOK].rearrange("p c (b u) -> p c b u", b=DB)))
                for c in range(KT):
                    cw = PRM["cw"][0] + 4 * c
                    dve.wait_ge(y0, c + 1)
                    y = qkT[:, c, SEQ:TOK].rearrange("p (b u) -> p b u", b=DB)
                    for j in range(1, 4):
                        link(nc.vector.scalar_tensor_tensor(
                            out=qkT[:, c, j:SEQ], in0=zqkT[:, c, 0:SEQ - j], scalar=prm[:, cw + 3 - j:cw + 4 - j],
                            in1=qkT[:, c, j:SEQ], op0=ALU.mult, op1=ALU.add))
                    link(nc.vector.tensor_scalar(y, tail[:, c, :, 3:7], prm[:, cw + 3:cw + 4],
                                                 prm[:, PRM["cb"][0] + c:PRM["cb"][0] + c + 1], ALU.mult, ALU.add))
                    for j in range(3):
                        ins = nc.vector.scalar_tensor_tensor(out=y, in0=tail[:, c, :, j:j + 4],
                                                             scalar=prm[:, cw + j:cw + j + 1], in1=y,
                                                             op0=ALU.mult, op1=ALU.add)
                        if j < 2:
                            link(ins)
                    ins.then_inc(y1, 1)
                    if c % 2:
                        evict(dve, 1 + c // 2)
                for i in range(5, DB):
                    evict(dve, i)
                dve.wait_ge(y1, KT)

        grow = gain[0:MH, 0:TOK]
        decay = gain[0:MH, TOK:TOK + DB]
        gcol = cols[:, 0:20].rearrange("p (t h) -> p t h", t=TT)
        emcol = cols[:, 20:40].rearrange("p (t h) -> p t h", t=TT)
        wscol, ascol = cols[0:NS, 40:44], cols[0:NS, 44:48]

        def gates_stage(l):
            tp, ev, ex, exd, rows_ok, tp2, ev2 = [sem(f"gates_{n}") for n in
                ("turned", "rows_in", "to_act", "from_act", "rows_ready", "columns", "columns_out")]
            R = lambda i: hTf[0:MH, i * TOK:i * TOK + TOK]
            li, lf, ab, F, g, zero, wg, av = [R(i) for i in range(8)]
            m = ropf[0:MH, 3792:3792 + TOK]
            s4 = lambda r: r[:, SEQ:TOK].rearrange("p (b u) -> p b u", b=DB)
            block = new_stage()
            @block.tensor
            def _(pe):
                for half in range(2):
                    for t in range(TT):
                        b = 2 * half + t // 4
                        ins = nc.tensor.transpose(ps[0:MH, b, (t % 4) * P:(t % 4) * P + P],
                                                  z[:, t, ZI + MH * half:ZI + MH * half + MH], ident)
                ins.then_inc(tp, 1)
                pe.wait_ge(rows_ok, 1)
                i4 = ident[0:MH, 0:MH]
                for n, r in enumerate((g, m)):
                    for t in range(TT):
                        w = P if t < TP else NS
                        nc.tensor.transpose(ps[0:w, 4, 20 * n + 4 * t:20 * n + 4 * t + 4], r[:, t * P:t * P + w], i4)
                for n, r in enumerate((wg, av)):
                    ins = nc.tensor.transpose(ps[0:NS, 4, 40 + 4 * n:44 + 4 * n], r[:, SEQ:TOK], i4)
                ins.then_inc(tp2, 1)

            @block.scalar
            def _(act):
                link = act_chain(act)
                act.wait_ge(ex, 1)
                link(nc.scalar.activation(ab, lf, ACT.Abs))
                link(nc.scalar.activation(ab, ab, ACT.Exp, scale=-1.0))
                nc.scalar.activation(ab, ab, ACT.Ln, bias=1.0).then_inc(exd, 1)
                act.wait_ge(ex, 2)
                link(nc.scalar.activation(decay, decay, ACT.Exp))
                link(nc.scalar.activation(wg[:, SEQ:TOK], wg[:, SEQ:TOK], ACT.Exp))
                nc.scalar.activation(av[:, SEQ:TOK], av[:, SEQ:TOK], ACT.Exp).then_inc(exd, 1)
                act.wait_ge(rows_ok, 1)
                act.dma_start(dout["mT"][bass.ds(l, 1)].rearrange("a p w -> (a p) w"), m).then_inc(m_st, 16)
                act.wait_ge(ev2, 2)
                link(nc.scalar.activation(cols[:, 20:36], cols[:, 20:36], ACT.Exp, scale=-1.0))
                link(nc.scalar.activation(cols[0:NS, 36:40], cols[0:NS, 36:40], ACT.Exp, scale=-1.0))

            @block.vector
            def _(dve):
                link = dve_chain(dve)
                link(nc.vector.memset(zero, 0.0))
                link(nc.vector.memset(cols[:, 16:20], 0.0))
                link(nc.vector.memset(cols[:, 36:40], 0.0))
                dve.wait_ge(tp, 1)
                for half, (r, b) in enumerate(((li, "bi"), (lf, "bf"))):
                    link(nc.vector.tensor_scalar(r[:, 0:SEQ], ps[0:MH, 2 * half, :], pr(b, MH), None, ALU.add))
                    link(nc.vector.tensor_scalar(r[:, SEQ:TOK], ps[0:MH, 2 * half + 1, 0:NS], pr(b, MH), None, ALU.add))
                nc.vector.tensor_copy(m, li).then_inc(ex, 1)
                dve.wait_ge(exd, 1)
                link(nc.vector.scalar_tensor_tensor(out=lf, in0=lf, scalar=0.0, in1=ab, op0=ALU.min, op1=ALU.subtract))
                link(nc.vector.tensor_tensor_scan(F[:, 0:SEQ], lf[:, 0:SEQ], zero[:, 0:SEQ], 0.0, ALU.add, ALU.add))
                link(nc.vector.tensor_copy(s4(F)[:, :, 0:1], s4(lf)[:, :, 0:1]))
                for u in range(1, DS):
                    link(nc.vector.tensor_tensor(s4(F)[:, :, u:u + 1], s4(F)[:, :, u - 1:u], s4(lf)[:, :, u:u + 1], ALU.add))
                link(nc.vector.tensor_tensor(g, li, F, ALU.subtract))
                link(nc.vector.tensor_tensor_scan(grow[:, 0:SEQ], g[:, 0:SEQ], g[:, 0:SEQ], 0.0, ALU.max, ALU.max))
                dve.wait_ge(m0_ld, 16)
                m3 = m0.rearrange("p (b o) -> p b o", o=1)
                for u in range(DS):
                    prev = m3 if u == 0 else s4(grow)[:, :, u - 1:u]
                    link(nc.vector.tensor_tensor(s4(grow)[:, :, u:u + 1], prev, s4(g)[:, :, u:u + 1], ALU.max))
                link(nc.vector.tensor_tensor(m, F, grow, ALU.add))
                last = s4(grow)[:, :, DS - 1:DS]
                link(nc.vector.tensor_tensor(decay.rearrange("p (b o) -> p b o", o=1), m3, last, ALU.subtract))
                link(nc.vector.tensor_tensor(s4(wg), s4(g), last.to_broadcast([MH, DB, DS]), ALU.subtract))
                nc.vector.tensor_tensor(s4(av), m3.to_broadcast([MH, DB, DS]), s4(grow), ALU.subtract).then_inc(ex, 1)
                dve.wait_ge(exd, 2)
                nc.vector.tensor_copy(zero[:, 0:1], g[:, 0:1]).then_inc(rows_ok, 1)
                dve.wait_ge(tp2, 1)
                for n in range(2):
                    link(nc.vector.tensor_copy(cols[:, 20 * n:20 * n + 16], ps[:, 4, 20 * n:20 * n + 16]))
                    nc.vector.tensor_copy(cols[0:NS, 20 * n + 16:20 * n + 20], ps[0:NS, 4, 20 * n + 16:20 * n + 20]).then_inc(ev2, 1)
                link(nc.vector.tensor_copy(cols[0:NS, 40:48], ps[0:NS, 4, 40:48]))

        KSC = float(MD) ** -0.5
        hh = ropf[:, 0:TT * 512].rearrange("p (t w) -> p t w", t=TT)

        def prompt_mlstm(l):
            gb, s_ok, kt, num, c_ok, w_ok, e_ok, p_ok, kw_ok, h_ok, cc_ok = [sem(f"mlp_{n}") for n in
                ("g_rows", "scores", "keys_turned", "numerators", "state", "exponents", "weights", "probs", "keys_weighted",
                 "hidden", "state_copied")]
            Pb = lambda h: hTf[:, 2048 * (h % 2):2048 * (h % 2) + 2048].rearrange("p (s t) -> p s t", s=TP)
            W = lambda u: hTf[:, 4096 + 512 * (u % 2):4608 + 512 * (u % 2)]
            kw = ropf[:, 2560:3072].rearrange("p (s d) -> p s d", s=TP)
            CT = ropf[:, 3268:3268 + MH * 129].rearrange("p (h v) -> p h v", h=MH)
            one = cs("one")
            block = new_stage()
            @block.tensor
            def _(pe):
                for h in range(MH):
                    if h >= 2:
                        pe.wait_ge(kw_ok, 2 * (h - 1))
                    nc.tensor.matmul(ps[:, h % 2, :], ident[0:MH, h:h + 1].to_broadcast([MH, P]), grow[:, 0:SEQ],
                                     start=True, stop=True).then_inc(gb, 1)
                    for st in range(TP):
                        u = TP * h + st
                        if u >= 2:
                            pe.wait_ge(p_ok, u - 1)
                        nc.tensor.matmul(ps[:, 2 + u % 2, st * P:SEQ], qkT[:, MH + h, st * P:st * P + P],
                                         qkT[:, h, st * P:SEQ], start=True, stop=True).then_inc(s_ok, 1)
                    if h:
                        pe.wait_ge(kw_ok, 2 * h)
                    for st in range(TP):
                        ins = nc.tensor.transpose(ps[:, 4, st * P:st * P + P], qkT[:, MH + h, st * P:st * P + P], ident)
                    ins.then_inc(kt, 1)
                    pe.wait_ge(p_ok, TP * h + TP)
                    for t in range(TP):
                        u = TP * h + t
                        if u >= 2:
                            pe.wait_ge(h_ok, u - 1)
                        o = ps[:, 5 + (TP * h + t) % 2, 0:129]
                        for st in range(t + 1):
                            nc.tensor.matmul(o[:, 0:128], Pb(h)[:, st, t * P:t * P + P],
                                             z[:, st, ZV + MD * h:ZV + MD * h + MD], start=(st == 0), stop=(st == t))
                        for st in range(t + 1):
                            ins = nc.tensor.matmul(o[:, 128:129], Pb(h)[:, st, t * P:t * P + P], one,
                                                   start=(st == 0), stop=(st == t))
                        ins.then_inc(num, 1)
                    pe.wait_ge(kw_ok, 2 * h + 2)
                    if h:
                        pe.wait_ge(cc_ok, h)
                    for st in range(TP):
                        nc.tensor.matmul(ps[:, 7, 0:128], kw[:, st, :], z[:, st, ZV + MD * h:ZV + MD * h + MD],
                                         start=(st == 0), stop=(st == TP - 1))
                    for st in range(TP):
                        ins = nc.tensor.matmul(ps[:, 7, 128:129], kw[:, st, :], one, start=(st == 0), stop=(st == TP - 1))
                    ins.then_inc(c_ok, 1)

            @block.scalar
            def _(act):
                for h in range(MH):
                    for st in range(TP):
                        u = TP * h + st
                        act.wait_ge(w_ok, 5 * h + st + 1)
                        w = W(u)[:, st * P:SEQ]
                        nc.scalar.activation(w, w, ACT.Exp, scale=-1.0).then_inc(e_ok, 1)
                    act.wait_ge(w_ok, 5 * h + 5)
                    nc.scalar.activation(wpcol[:, h, :], wpcol[:, h, :], ACT.Exp).then_inc(e_ok, 1)
                act.wait_ge(cc_ok, MH)
                act.dma_start(dout["cT_p"][bass.ds(l, 1)].rearrange("a p h v -> (a p) h v"), CT).then_inc(ctp_st, 16)

            @block.vector
            def _(dve):
                link = dve_chain(dve)
                tri = cs("tri")
                for h in range(MH):
                    dve.wait_ge(gb, h + 1)
                    B = ps[:, h % 2, :]

                    def weights(st):
                        u = TP * h + st
                        nc.vector.tensor_scalar(W(u)[:, st * P:SEQ], B[:, st * P:SEQ], gcol[:, st, h:h + 1], 0.0,
                                                ALU.subtract, ALU.max).then_inc(w_ok, 1)
                    weights(0)
                    weights(1)
                    for st in range(TP):
                        u = TP * h + st
                        dve.wait_ge(e_ok, 5 * h + st + 1)
                        dve.wait_ge(s_ok, u + 1)
                        pb = Pb(h)[:, st, st * P:SEQ]
                        link(nc.vector.scalar_tensor_tensor(out=pb, in0=ps[:, 2 + u % 2, st * P:SEQ], scalar=KSC,
                                                            in1=W(u)[:, st * P:SEQ], op0=ALU.mult, op1=ALU.mult))
                        d = Pb(h)[:, st, st * P:st * P + P]
                        nc.vector.tensor_tensor(d, d, tri, ALU.mult).then_inc(p_ok, 1)
                        if st + 2 < TP:
                            weights(st + 2)
                    nc.vector.tensor_scalar(wpcol[:, h, :], gcol[:, 0:TP, h], B[:, SEQ - 1:SEQ], None,
                                            ALU.subtract).then_inc(w_ok, 1)
                    dve.wait_ge(e_ok, 5 * h + 5)
                    dve.wait_ge(kt, h + 1)
                    if h:
                        dve.wait_ge(c_ok, h)
                    for st in range(TP):
                        ins = nc.vector.tensor_scalar(kw[:, st, :], ps[:, 4, st * P:st * P + P], wpcol[:, h, st:st + 1],
                                                      KSC, ALU.mult, ALU.mult)
                        link(ins) if st < TP - 2 else ins.then_inc(kw_ok, 1)
                    for t in range(TP):
                        dve.wait_ge(num, TP * h + t + 1)
                        o = ps[:, 5 + (TP * h + t) % 2, 0:129]
                        link(nc.vector.tensor_scalar(stat[:, 0:1], o[:, 128:129], -1.0, emcol[:, t, h:h + 1],
                                                     ALU.mult, ALU.max))
                        link(nc.vector.tensor_scalar(stat[:, 0:1], o[:, 128:129], stat[:, 0:1], None, ALU.max))
                        link(nc.vector.reciprocal(stat[:, 1:2], stat[:, 0:1]))
                        nc.vector.tensor_scalar(hh[:, t, MD * h:MD * h + MD], o[:, 0:128], stat[:, 1:2], None,
                                                ALU.mult).then_inc(h_ok, 1)
                    dve.wait_ge(c_ok, h + 1)
                    nc.vector.tensor_copy(CT[:, h, :], ps[:, 7, 0:129]).then_inc(cc_ok, 1)

        def sample_mlstm(l):
            gb, kt, it, ia, cu, cu_used, nu, dv, ex, cs_st = [sem(f"mls_{n}") for n in
                ("g_rows", "keys_turned", "from_state", "from_chunk", "updates", "updates_read", "n_update", "to_pe", "exp",
                 "c_done")]
            C = slot("cst").rearrange("p (h b v) -> p h b v", h=MH, b=DB)
            kw, pT, tmp, decB, qm = (ropf[0:NS, 2592:2720], ropf[0:NS, 2720:2752], ropf[0:NS, 2752:2881],
                                     ropf[:, 2884:2916].rearrange("p (h b) -> p h b", h=MH),
                                     hTf[:, 0:1024].rearrange("p (h b t) -> p h b t", h=MH, b=DB))
            kwm = hTf[0:NS, 1024:2048].rearrange("p (b d) -> p b d", b=DB)
            W = hTf[0:NS, 2048:2080]
            read_at["cst"] = (cts_st, 16 * CTS_STORES)
            one, oh, ms = cs("one", NS), cs("ohb", NS), cs("ms", NS)
            block = new_stage()
            @block.tensor
            def _(pe):
                arrived(pe, "cst")
                pe.wait_ge(n_ld, 16)
                pe.wait_ge(dv, 1)
                v = z[0:NS, TP, :]
                for h in range(MH):
                    vh = v[:, ZV + MD * h:ZV + MD * h + MD]
                    nc.tensor.matmul(ps[0:NS, 1, 32:64], ident[0:MH, h:h + 1].to_broadcast([MH, NS]), grow[:, SEQ:TOK],
                                     start=True, stop=True)
                    nc.tensor.matmul(ps[:, 1, 64:72], ident[0:MH, h:h + 1].to_broadcast([MH, P]), decay,
                                     start=True, stop=True)
                    nc.tensor.matmul(ps[0:NS, 1, 0:32], qkT[:, MH + h, SEQ:TOK], qkT[:, h, SEQ:TOK],
                                     start=True, stop=True).then_inc(gb, 1)
                    nc.tensor.transpose(ps[0:NS, 2, 0:128], qkT[:, MH + h, SEQ:TOK], ident).then_inc(kt, 1)
                    for b in range(DB):
                        nc.tensor.matmul(ps[0:NS, 0, 0:128], qm[:, h, b, :], C[:, h, b, :], start=(b == 0), stop=(b == DB - 1))
                    for b in range(DB):
                        ins = nc.tensor.matmul(ps[0:NS, 0, 128:129], qm[:, h, b, :], nT[:, h, b:b + 1],
                                               start=(b == 0), stop=(b == DB - 1))
                    ins.then_inc(it, 1)
                    pe.wait_ge(dv, 3 * h + 2)
                    nc.tensor.matmul(ps[0:NS, 3, 0:128], pT, vh, start=True, stop=True)
                    nc.tensor.matmul(ps[0:NS, 3, 128:129], pT, one, start=True, stop=True).then_inc(ia, 1)
                    pe.wait_ge(dv, 3 * h + 3)
                    for b in range(DB):
                        ins = nc.tensor.matmul(ps[:, 5 + b // 4, (b % 4) * P:(b % 4) * P + P], kwm[:, b, :], vh,
                                               start=True, stop=True)
                    ins.then_inc(cu, 1)
                    nc.tensor.matmul(ps[:, 7, 0:DB], kw, oh, start=True, stop=True).then_inc(nu, 1)
                    pe.wait_ge(dv, 3 * h + 4)

            @block.scalar
            def _(act):
                def store(h):
                    act.wait_ge(cs_st, h + 1)
                    w = DB * MD
                    act.dma_start(dout["cT_s"][bass.ds(l, 1), :, h * w:h * w + w].rearrange("a p w -> (a p) w"),
                                  slot("cst")[:, h * w:h * w + w]).then_inc(cts_st, 16)
                for h in range(MH):
                    act.wait_ge(ex, 2 * h + 1)
                    nc.scalar.activation(W, W, ACT.Exp, scale=-1.0).then_inc(ex, 1)
                    if h:
                        store(h - 1)
                store(MH - 1)
                act.dma_start(dout["nT"][bass.ds(l, 1)].rearrange("a p (h b) -> (a p) h b", h=MH), nT).then_inc(cts_st, 16)

            @block.vector
            def _(dve):
                link = dve_chain(dve)
                dve.wait_ge(n_ld, 16)
                arrived(dve, "cst")
                link(nc.vector.memset(qm, 0.0))
                for b in range(DB):
                    ins = nc.vector.tensor_copy(qm[:, :, b, 4 * b:4 * b + 4], qkT[:, 0:MH, SEQ + 4 * b:SEQ + 4 * b + 4])
                    link(ins) if b < DB - 1 else ins.then_inc(dv, 1)
                for h in range(MH):
                    dve.wait_ge(gb, h + 1)
                    nc.vector.tensor_scalar(W, ps[0:NS, 1, 32:64], gcol[0:NS, TP, h:h + 1], 0.0, ALU.subtract,
                                            ALU.max).then_inc(ex, 1)
                    link(nc.vector.tensor_copy(decB[:, h, :], ps[:, 1, 64:72]))
                    dve.wait_ge(ex, 2 * h + 2)
                    link(nc.vector.scalar_tensor_tensor(out=pT, in0=ps[0:NS, 1, 0:32], scalar=KSC, in1=W,
                                                        op0=ALU.mult, op1=ALU.mult))
                    nc.vector.tensor_tensor(pT, pT, ms, ALU.mult).then_inc(dv, 1)
                    dve.wait_ge(kt, h + 1)
                    link(nc.vector.tensor_scalar(kw, ps[0:NS, 2, 0:128], wscol[:, h:h + 1], KSC, ALU.mult, ALU.mult))
                    nc.vector.tensor_tensor(
                        kwm, kw.rearrange("p (o d) -> p o d", o=1).to_broadcast([NS, DB, MD]),
                        oh.rearrange("p (b o) -> p b o", o=1).to_broadcast([NS, DB, MD]), ALU.mult).then_inc(dv, 1)
                    dve.wait_ge(it, h + 1)
                    link(nc.vector.tensor_scalar(tmp, ps[0:NS, 0, 0:129], ascol[:, h:h + 1], None, ALU.mult))
                    dve.wait_ge(ia, h + 1)
                    link(nc.vector.tensor_tensor(tmp, ps[0:NS, 3, 0:129], tmp, ALU.add))
                    link(nc.vector.tensor_scalar(stat[0:NS, 0:1], tmp[:, 128:129], -1.0, emcol[0:NS, TP, h:h + 1],
                                                 ALU.mult, ALU.max))
                    link(nc.vector.tensor_scalar(stat[0:NS, 0:1], tmp[:, 128:129], stat[0:NS, 0:1], None, ALU.max))
                    link(nc.vector.reciprocal(stat[0:NS, 1:2], stat[0:NS, 0:1]))
                    if h == 0:
                        link(nc.vector.memset(hh[:, TP, :], 0.0))
                    link(nc.vector.tensor_scalar(hh[0:NS, TP, MD * h:MD * h + MD], tmp[:, 0:128], stat[0:NS, 1:2], None,
                                                 ALU.mult))
                    dve.wait_ge(cu, h + 1)
                    for b in range(DB):
                        link(nc.vector.scalar_tensor_tensor(out=C[:, h, b, :], in0=C[:, h, b, :],
                                                            scalar=decB[:, h, b:b + 1],
                                                            in1=ps[:, 5 + b // 4, (b % 4) * P:(b % 4) * P + P],
                                                            op0=ALU.mult, op1=ALU.add))
                    dve.wait_ge(nu, h + 1)
                    link(nc.vector.tensor_tensor(nT[:, h, :], nT[:, h, :], decB[:, h, :], ALU.mult))
                    link(nc.vector.tensor_tensor(nT[:, h, :], ps[:, 7, 0:DB], nT[:, h, :], ALU.add))
                    nc.vector.tensor_copy(stat[0:1, 2:3], stat[0:1, 1:2]).then_inc(dv, 1)
                    dve.wait_ge(dv, 3 * h + 4)
                    nc.vector.tensor_copy(stat[0:1, 3:4], stat[0:1, 2:3]).then_inc(cs_st, 1)

        def finish_mlstm(l):
            go, root = sem("mfin_squares"), sem("mfin_root")
            v = hh.rearrange("p t (h d) -> p t h d", h=MH)
            sq = hTf[:, 0:2560]
            block = new_stage()
            @block.scalar
            def _(act):
                act.wait_ge(go, 1)
                nc.scalar.activation(stat[:, 80:100], stat[:, 0:20], ACT.Sqrt).then_inc(root, 1)

            @block.vector
            def _(dve):
                link = dve_chain(dve)
                head_norm(link, [(v, pr("hn"), 0, sq.rearrange("p (t h d) -> p t h d", t=TT, h=MH))], 20, root, go, MD)
                o = z[:, :, ZO:ZO + 512]
                link(nc.vector.tensor_tensor(o, o, hh, ALU.mult))

        kselT, kwinT = ropf[:, 0:TOK], ropf[:, TOK:2 * TOK]
        qT = ropf[:, 2 * TOK:2 * TOK + HG * TOK].rearrange("p (h t) -> p h t", h=HG)
        xp = qkf[:, 0:SEQ // 2 * 4]
        kc_p = qkf[:, 1024:1024 + NC_P]
        vc_p = qkf[0:NC_P, 1056:1056 + P]
        QSC = float(HD) ** -0.5

        def prep_stage(l):
            tp, ea, ed = sem("prep_turned"), sem("prep_copied_a"), sem("prep_copied_d")
            pairs = xp.rearrange("p (q k g) -> p k g q", k=2, g=G)
            block = new_stage()
            @block.tensor
            def _(pe):
                for t in range(TT):
                    if t >= 4:
                        pe.wait_ge(ea, t - 3)
                        pe.wait_ge(ed, t - 3)
                    b = 2 * (t % 4)
                    for hg in range(HG):
                        nc.tensor.transpose(ps[:, b, hg * P:hg * P + P], z[:, t, ZQ + hg * P:ZQ + hg * P + P], ident)
                    for n, c in enumerate((ZK + 256, ZK + 512, ZK, ZK + 128)):
                        if t < TP or n < 2:
                            ins = nc.tensor.transpose(ps[:, b + 1, n * P:n * P + P], z[:, t, c:c + P], ident)
                    ins.then_inc(tp, 1)

            @block.scalar
            def _(act):
                load_gain(act, l, 2)
                for t in range(TT):
                    w = P if t < TP else NS
                    act.wait_ge(tp, t + 1)
                    nc.scalar.activation(qT[:, :, t * P:t * P + w],
                                         ps[:, 2 * (t % 4), :].rearrange("p (h t) -> p h t", h=HG)[:, :, 0:w],
                                         ACT.Copy, scale=QSC).then_inc(ea, 1)

            @block.vector
            def _(dve):
                link = dve_chain(dve)
                for t in range(TT):
                    w = P if t < TP else NS
                    dve.wait_ge(tp, t + 1)
                    s = ps[:, 2 * (t % 4) + 1, :]
                    if t < TP:
                        for k in range(2):
                            for g in range(G):
                                for par in range(2):
                                    a = 256 + 128 * k + par
                                    link(nc.vector.tensor_copy(pairs[64 * par:64 * par + 64, k, g, 64 * t:64 * t + 64],
                                                               s[64 * g:64 * g + 64, a:a + 127:2]))
                    link(nc.vector.tensor_copy(kselT[:, t * P:t * P + w], s[:, 0:w]))
                    nc.vector.tensor_copy(kwinT[:, t * P:t * P + w], s[:, 128:128 + w]).then_inc(ed, 1)

        def prompt_compress(l):
            tensor_program, hidden, _, evict = compression("pcmp", [
                (None, xp.rearrange("p (q w) -> p q w", w=4), NC_P, kc_p, vc_p)], False)
            block = new_stage()

            @block.tensor
            def _(pe):
                tensor_program(pe)

            @block.scalar
            def _(act):
                hidden(act, 0)

            @block.vector
            def _(dve):
                evict(dve, 0)

        def tile_attention(stage, l, units, free=None):
            s_ok, mx, e_ok, pt, ptc, o_ok, o_used, cf = [sem(f"{stage}_{n}") for n in
                ("scores", "maxima", "exponentials", "probs_turned", "probs_copied", "outputs", "outputs_read", "factors")]
            Pb = lambda u: hTf[:, 512 * (u % 4):512 * (u % 4) + 512]
            PT = lambda u: hTf[:, 2048 + 512 * (u % 4):2560 + 512 * (u % 4)]
            st = lambda u, c: stat[:, 8 * (u % 8) + c:8 * (u % 8) + c + 1]
            causal = cs("causal")
            N = len(units)
            block = new_stage()
            @block.tensor
            def _(pe):
                def scores(u):
                    q, k, n = units[u][0:3]
                    if u >= 3:
                        pe.wait_ge(e_ok, u - 2)
                    nc.tensor.matmul(ps[:, u % 3, 0:n], q, k, start=True, stop=True).then_inc(s_ok, 1)

                def turn(u):
                    n = units[u][2]
                    pe.wait_ge(e_ok, u + 1)
                    if u >= 3:
                        pe.wait_ge(ptc, u - 2)
                    for i in range(n // P):
                        ins = nc.tensor.transpose(ps[:, 3 + u % 3, i * P:i * P + P], Pb(u)[:, i * P:i * P + P], ident)
                    ins.then_inc(pt, 1)

                def values(u):
                    n, vs, w = units[u][2], units[u][4], units[u][5]
                    pe.wait_ge(ptc, u + 1)
                    if u >= 2:
                        pe.wait_ge(o_used, u - 1)
                    for i in range(n // P):
                        ins = nc.tensor.matmul(ps[:, 6 + u % 2, 0:w], PT(u)[:, i * P:i * P + P], vs[i],
                                               start=(i == 0), stop=(i == n // P - 1))
                    ins.then_inc(o_ok, 1)
                for u in range(N + 3):
                    if u < N:
                        scores(u)
                    if 2 <= u < N + 2:
                        turn(u - 2)
                    if u >= 3:
                        values(u - 3)

            @block.scalar
            def _(act):
                def copied(u):
                    act.wait_ge(pt, u + 1)
                    n = units[u][2]
                    if u >= 4:
                        act.wait_ge(o_ok, u - 3)
                    nc.scalar.copy(PT(u)[:, 0:n], ps[:, 3 + u % 3, 0:n]).then_inc(ptc, 1)
                for u in range(N + 2):
                    if u < N:
                        n = units[u][2]
                        act.wait_ge(mx, u + 1)
                        if u >= 4:
                            act.wait_ge(pt, u - 3)
                        nc.scalar.activation(Pb(u)[:, 0:n], ps[:, u % 3, 0:n], ACT.Exp, bias=st(u, 0),
                                             accum_out=st(u, 1)).then_inc(e_ok, 1)
                    if u >= 2:
                        copied(u - 2)

            @block.vector
            def _(dve):
                link = dve_chain(dve)

                def output(u):
                    _, _, n, _, _, w, gate, out, adds = units[u]
                    dve.wait_ge(e_ok, u + 1)
                    link(nc.vector.reciprocal(st(u, 2), st(u, 1)))
                    f = st(u, 2)
                    if gate is not None:
                        link(nc.vector.tensor_tensor(st(u, 3), st(u, 2), gate, ALU.mult))
                        f = st(u, 3)
                    dve.wait_ge(o_ok, u + 1)
                    src = ps[:, 6 + u % 2, 0:w]
                    if adds:
                        nc.vector.scalar_tensor_tensor(out=out, in0=src, scalar=f, in1=out, op0=ALU.mult,
                                                       op1=ALU.add).then_inc(o_used, 1)
                    else:
                        nc.vector.tensor_scalar(out, src, f, None, ALU.mult).then_inc(o_used, 1)
                for u in range(N + 3):
                    if u < N:
                        n, diag = units[u][2], units[u][3]
                        dve.wait_ge(s_ok, u + 1)
                        if diag:
                            link(nc.vector.tensor_tensor(ps[:, u % 3, n - P:n], ps[:, u % 3, n - P:n], causal, ALU.add))
                        nc.vector.tensor_reduce(st(u, 0), ps[:, u % 3, 0:n], AX.X, ALU.max, negate=True).then_inc(mx, 1)
                    if u >= 3:
                        if adds_need(units, u - 3):
                            dve.wait_ge(o_used, u - 3)
                        output(u - 3)
                dve.wait_ge(o_used, N)

        def adds_need(units, u):
            return u > 0 and units[u][8]

        def prompt_attention(l):
            s_ok, shifted, r_ok, e_ok, pt, ptc, o_ok, o_used = [sem(f"pc_{n}") for n in
                ("scores", "scores_shifted", "rows", "exponentials", "turned", "copied", "outputs", "outputs_read")]
            n = NC_P
            E = lambda t: hTf[:, 512 * (t % 2):512 * (t % 2) + HEADS * n].rearrange("p (h c) -> p h c", h=HEADS)
            eT = hTf[0:n, 1024:2048].rearrange("p (h t) -> p h t", h=HEADS)
            zg = z[:, :, ZG:ZG + 24].rearrange("p t (h r) -> p t h r", r=3)
            bank = lambda t, g: (0, 4, 5, 6)[2 * (t % 2) + g]
            block = new_stage()

            @block.tensor
            def _(pe):
                def scores(t):
                    for h in range(HEADS):
                        g, hg = h % G, h // G
                        ins = nc.tensor.matmul(ps[:, bank(t, g), n * hg:n * hg + n],
                                               qT[64 * g:64 * g + 64, hg, t * P:t * P + P],
                                               kc_p[64 * g:64 * g + 64, :], start=True, stop=True)
                    ins.then_inc(s_ok, 1)
                scores(0)
                for t in range(TP):
                    if t + 1 < TP:
                        scores(t + 1)
                    pe.wait_ge(r_ok, t + 1)
                    for h in range(HEADS):
                        ins = nc.tensor.transpose(ps[0:n, 1 + h // 4, (h % 4) * P:(h % 4) * P + P], E(t)[:, h, :], ident)
                    ins.then_inc(pt, 1)
                    pe.wait_ge(ptc, t + 1)
                    if t:
                        pe.wait_ge(o_used, t)
                    for h in range(HEADS):
                        ins = nc.tensor.matmul(ps[:, 3, 64 * h:64 * h + 64], eT[:, h, :],
                                               vc_p[:, 64 * (h % G):64 * (h % G) + 64], start=True, stop=True)
                    ins.then_inc(o_ok, 1)

            @block.scalar
            def _(act):
                for t in range(TP):
                    act.wait_ge(shifted, t + 1)
                    nc.scalar.activation(E(t), E(t), ACT.Exp).then_inc(e_ok, 1)

            @block.vector
            def _(dve):
                link = dve_chain(dve)
                bc = lambda a: a.rearrange("p (h o) -> p h o", o=1).to_broadcast([P, HEADS, n])

                def shift(t):
                    e, top_ = E(t), stat[:, 32 * (t % 2):32 * (t % 2) + 8]
                    dve.wait_ge(s_ok, t + 1)
                    ma = cs("cma")[:, n * t:n * t + n].rearrange("p (o c) -> p o c", o=1).to_broadcast([P, HG, n])
                    for g in range(G):
                        src = ps[:, bank(t, g), 0:HG * n].rearrange("p (h c) -> p h c", h=HG)
                        link(nc.vector.tensor_tensor(e[:, g:HEADS:G, :], src, ma, ALU.add))
                    link(nc.vector.tensor_reduce(top_, e, AX.X, ALU.max))
                    nc.vector.tensor_tensor(e, e, bc(top_), ALU.subtract).then_inc(shifted, 1)

                def gated_rows(t):
                    e, st = E(t), lambda i: stat[:, 32 * (t % 2) + 8 * i:32 * (t % 2) + 8 * i + 8]
                    mm = cs("cmm")[:, n * t:n * t + n].rearrange("p (o c) -> p o c", o=1).to_broadcast([P, HEADS, n])
                    dve.wait_ge(e_ok, t + 1)
                    link(nc.vector.tensor_tensor(e, e, mm, ALU.mult))
                    link(nc.vector.tensor_reduce(st(1), e, AX.X, ALU.add))
                    link(nc.vector.tensor_scalar(st(1), st(1), 1e-30, None, ALU.max))
                    link(nc.vector.reciprocal(st(2), st(1)))
                    link(nc.vector.tensor_tensor(st(3), st(2), zg[:, t, :, 0], ALU.mult))
                    nc.vector.tensor_tensor(e, e, bc(st(3)), ALU.mult).then_inc(r_ok, 1)

                def output(t):
                    dve.wait_ge(o_ok, t + 1)
                    nc.vector.tensor_copy(z[:, t, ZQ:ZQ + 512], ps[:, 3, :]).then_inc(o_used, 1)
                shift(0)
                for t in range(TP):
                    if t + 1 < TP:
                        shift(t + 1)
                    gated_rows(t)
                    if t:
                        output(t - 1)
                    dve.wait_ge(pt, t + 1)
                    link(nc.vector.tensor_copy(eT[:, 0:4, :], ps[0:n, 1, :].rearrange("p (h t) -> p h t", h=4)))
                    nc.vector.tensor_copy(eT[:, 4:8, :], ps[0:n, 2, :].rearrange("p (h t) -> p h t", h=4)).then_inc(ptc, 1)
                output(TP - 1)
            units = []
            for t in range(TP):
                for r, kT in ((1, kselT), (2, kwinT)):
                    for h in range(HEADS):
                        g, hg = h % G, h // G
                        vc = ZK + 256 * r + 128 + 64 * g
                        units.append((qT[64 * g:64 * g + 64, hg, t * P:t * P + P], kT[64 * g:64 * g + 64, 0:t * P + P],
                                      t * P + P, True, [z[:, i, vc:vc + 64] for i in range(t + 1)], 64, zg[:, t, h, r:r + 1],
                                      z[:, t, ZQ + 64 * h:ZQ + 64 * h + 64], True))
            tile_attention("att2", l, units)

        s_sel, s_win, s_cmp = qkf[:, 0:PAST + NS], qkf[:, 2080:2080 + WIN + NS], qkf[:, 2624:2752]
        imp, rep, top, impc = qkf[:, 2752:2785], qkf[:, 2786:2819], qkf[:, 2820:2828], qkf[:, 2828:2956]
        oT = qkf[:, 3000:3384].rearrange("p (r h t) -> p r h t", r=3, h=HG)
        qblk = qkf[:, 3400:3656].rearrange("p (b r) -> p b r", b=DB)
        pT = hTf[:, 0:23 * P].rearrange("p (i r) -> p i r", i=23)

        def sample_attention(l, hb):
            stage = f"samp{hb}"
            q_ok, sc, sw, ss, cp, pc_ok, im, im_used, mx, ex, pn, kt, ka, kd, pt, ca, cd, wv, ov = [
                sem(f"{stage}_{n}") for n in
                ("queries", "cmp_scores", "win_scores", "sel_scores", "scores_copied", "cmp_probs", "importance",
                 "importance_read", "maxima", "exponentials", "probs_ready", "keys_turned", "keys_copied_a",
                 "keys_copied_d", "turned", "copied_a", "copied_d", "win_outputs", "outputs")]
            kl, vl = [f"k{2 * hb + i}" for i in range(2)], [f"v{2 * hb + i}" for i in range(2)]
            wl = f"win{hb}"
            read_at.update({kl[i]: (kt, 8 * i + 8) for i in range(2)})
            read_at.update({vl[i]: (ov, i + 1) for i in range(2)})
            read_at[wl] = (wv, 1)
            kT = lambda u: hTf[:, 3072 + 512 * (u % 2):3584 + 512 * (u % 2)]
            UNITS = 16
            tiles = [(s_cmp[:, 0:NC_S], NC_S)] + [(s_win[:, i * P:i * P + P], P) for i in range(4)] + [(s_win[:, WIN:], NS)]
            tiles += [(s_sel[:, i * P:i * P + P], P) for i in range(16)] + [(s_sel[:, PAST:], NS)]
            block = new_stage()
            @block.tensor
            def _(pe):
                pe.wait_ge(q_ok, 1)
                for b4 in range(4):
                    b = 4 * hb + b4
                    r = slice(32 * b4, 32 * b4 + 32)
                    q = qblk[:, b, :]
                    nc.tensor.matmul(ps[r, 0, 0:NC_S], q, kc_s[:, b, 0:NC_S], start=True, stop=True)
                    nc.tensor.matmul(ps[r, 0, 128:160], q, kwinT[:, SEQ:TOK], start=True, stop=True)
                    ins = nc.tensor.matmul(ps[r, 0, 160:192], q, kselT[:, SEQ:TOK], start=True, stop=True)
                ins.then_inc(sc, 1)
                arrived(pe, wl)
                for b4 in range(4):
                    ins = nc.tensor.matmul(ps[32 * b4:32 * b4 + 32, 1, :], qblk[:, 4 * hb + b4, :],
                                           slot(wl)[:, 512 * b4:512 * b4 + 512], start=True, stop=True)
                ins.then_inc(sw, 1)

                def turn_keys(u):
                    b4, c = u // 4, u % 4
                    load = kl[b4 // 2]
                    if u % 8 == 0:
                        arrived(pe, load)
                    if u >= 2:
                        pe.wait_ge((ka, kd)[u % 2], u // 2)
                    keys = slot(load).rearrange("p (b j c) -> p b j c", b=2, j=16)
                    for j in range(4):
                        ins = nc.tensor.transpose(ps[:, 6 + u % 2, j * P:j * P + P], keys[:, b4 % 2, 4 * c + j, :], ident)
                    ins.then_inc(kt, 1)

                def key_scores(u):
                    b4, c = u // 4, u % 4
                    pe.wait_ge((ka, kd)[u % 2], u // 2 + 1)
                    nc.tensor.matmul(ps[32 * b4:32 * b4 + 32, 2 + c, :], qblk[:, 4 * hb + b4, :], kT(u),
                                     start=True, stop=True).then_inc(ss, 1)
                turn_keys(0)
                for u in range(UNITS):
                    if u + 1 < UNITS:
                        turn_keys(u + 1)
                    key_scores(u)
                    if u == 4:
                        pe.wait_ge(pc_ok, 1)
                        pe.wait_ge(cp, 1)
                        nc.tensor.matmul(ps[:, 0, 256:256 + NC_S], cs("grp"), s_cmp[:, 0:NC_S], start=True,
                                         stop=True).then_inc(im, 1)
                for i, (src, n) in enumerate(tiles):
                    if i == 1:
                        pe.wait_ge(pn, 1)
                    if i == 6:
                        pe.wait_ge(pn, 2)
                    if i % 4 == 0:
                        if i == 0:
                            pe.wait_ge(im_used, 1)
                        if i >= 8:
                            pe.wait_ge(ca if (i // 4) % 2 == 0 else cd, (i // 4 - 2) // 2 + 1)
                    ins = nc.tensor.transpose(ps[0:n, (0, 6)[i // 4 % 2], (i % 4) * P:(i % 4) * P + P], src, ident)
                    if i % 4 == 3 or i == 22:
                        ins.then_inc(pt, 1)
                pe.wait_ge(ca, 3)
                pe.wait_ge(cd, 3)
                win_v = slot(wl)[:, 2048:4096].rearrange("p (b t c) -> p b t c", b=4, t=4)
                for b4 in range(4):
                    r = slice(32 * b4, 32 * b4 + 32)
                    nc.tensor.matmul(ps[:, 7, r], vc_s[0:NC_S, 4 * hb + b4, :], pT[0:NC_S, 0, r], start=True, stop=True)
                    for i in range(4):
                        nc.tensor.matmul(ps[:, 7, 128 + 32 * b4:160 + 32 * b4], win_v[:, b4, i, :], pT[:, 1 + i, r],
                                         start=(i == 0), stop=False)
                    ins = nc.tensor.matmul(ps[:, 7, 128 + 32 * b4:160 + 32 * b4], z[0:NS, TP, ZK + 640:ZK + 768],
                                           pT[0:NS, 5, r], start=False, stop=True)
                ins.then_inc(wv, 1)
                for j in range(2):
                    arrived(pe, vl[j])
                    vals = slot(vl[j]).rearrange("p (b i c) -> p b i c", b=2, i=NPG)
                    for b4 in range(2 * j, 2 * j + 2):
                        r = slice(32 * b4, 32 * b4 + 32)
                        o = ps[:, 7, 256 + 32 * b4:288 + 32 * b4]
                        nc.tensor.matmul(o, z[0:NS, TP, ZK + 384:ZK + 512], pT[0:NS, 22, r], start=True, stop=False)
                        for i in range(NPG):
                            ins = nc.tensor.matmul(o, vals[:, b4 % 2, i, :], pT[:, 6 + i, r], start=False, stop=(i == NPG - 1))
                    ins.then_inc(ov, 1)

            @block.scalar
            def _(act):
                link = act_chain(act)
                def exponentials(i):
                    s, a = ((s_cmp[:, 0:NC_S], 0), (s_win, 4), (s_sel, 8))[i]
                    act.wait_ge(mx, i + 1)
                    nc.scalar.activation(s, s, ACT.Exp, bias=stat[:, a:a + 1], accum_out=stat[:, a + 1:a + 2]).then_inc(ex, 1)
                exponentials(0)
                for u in range(0, UNITS, 2):
                    act.wait_ge(kt, u + 1)
                    nc.scalar.copy(kT(u), ps[:, 6, :]).then_inc(ka, 1)
                    if u == 8:
                        exponentials(1)
                exponentials(2)
                for q in (0, 2, 4):
                    act.wait_ge(pt, q + 1)
                    if q == 0:
                        link(nc.scalar.copy(pT[0:NC_S, 0, :], ps[0:NC_S, 0, 0:P]))
                        ins = nc.scalar.copy(pT[:, 1:4, :], ps[:, 0, P:512].rearrange("p (i r) -> p i r", i=3))
                    else:
                        ins = nc.scalar.copy(pT[:, 4 * q:4 * q + 4, :], ps[:, 0, :].rearrange("p (i r) -> p i r", i=4))
                    ins.then_inc(ca, 1)

            @block.vector
            def _(dve):
                link = dve_chain(dve)
                if hb == 0:
                    link(nc.vector.memset(qblk, 0.0))
                    for g in range(G):
                        for hg in range(HG):
                            p = slice(64 * g, 64 * g + 64)
                            c = 16 * g + 4 * hg
                            link(nc.vector.tensor_copy(qblk[p, :, c:c + 4],
                                                       qT[p, hg, SEQ:TOK].rearrange("p (b t) -> p b t", b=DB)))
                nc.vector.memset(impc[:, 127:128], 0.0).then_inc(q_ok, 1)
                dve.wait_ge(q_ok, 1)
                new = cs("new")[:, 32 * hb:32 * hb + 32]
                dve.wait_ge(sc, 1)
                link(nc.vector.tensor_copy(s_cmp[:, 0:NC_S], ps[:, 0, 0:NC_S]))
                link(nc.vector.tensor_reduce(stat[:, 0:1], s_cmp[:, 0:NC_S], AX.X, ALU.max, negate=True))
                link(nc.vector.tensor_tensor(s_win[:, WIN:], ps[:, 0, 128:160], new, ALU.add))
                link(nc.vector.tensor_tensor(s_sel[:, PAST:], ps[:, 0, 160:192], new, ALU.add))
                nc.vector.tensor_copy(stat[:, 2:3], stat[:, 0:1]).then_inc(cp, 1)
                dve.wait_ge(cp, 1)
                nc.vector.tensor_copy(stat[:, 3:4], stat[:, 2:3]).then_inc(mx, 1)

                def copy_keys(u):
                    dve.wait_ge(kt, u + 1)
                    nc.vector.tensor_copy(kT(u), ps[:, 7, :]).then_inc(kd, 1)
                copy_keys(1)
                dve.wait_ge(ex, 1)
                link(nc.vector.reciprocal(stat[:, 2:3], stat[:, 1:2]))
                nc.vector.tensor_scalar(s_cmp[:, 0:NC_S], s_cmp[:, 0:NC_S], stat[:, 2:3], None, ALU.mult).then_inc(pc_ok, 1)
                copy_keys(3)
                dve.wait_ge(sw, 1)
                link(nc.vector.tensor_copy(s_win[:, 4:WIN], ps[:, 1, 4:WIN]))
                link(nc.vector.tensor_tensor(s_win[:, 0:4], ps[:, 1, 0:4], cs("low"), ALU.add))
                nc.vector.tensor_reduce(stat[:, 4:5], s_win, AX.X, ALU.max, negate=True).then_inc(mx, 1)
                copy_keys(5)
                dve.wait_ge(im, 1)
                nc.vector.tensor_copy(impc[:, 0:NC_S], ps[:, 0, 256:256 + NC_S]).then_inc(im_used, 1)
                dve.wait_ge(im_used, 1)
                link(nc.vector.tensor_reduce(imp[:, 0:32], impc.rearrange("p (s u) -> p s u", u=4), AX.X, ALU.add))
                link(nc.vector.tensor_tensor(imp[:, 1:32], imp[:, 1:32], impc[:, 3:124:4], ALU.add))
                copy_keys(7)
                link(nc.vector.memset(imp[:, 0:1], BIG))
                link(nc.vector.memset(imp[:, 32:33], BIG))
                link(nc.vector.max(top, imp))
                link(nc.vector.match_replace(rep, top, imp, 3.0 * BIG))
                link(nc.vector.tensor_scalar(rep, rep, 2.0 * BIG, None, ALU.is_ge))
                link(nc.vector.tensor_scalar(rep, rep, -1.0, BIG, ALU.add, ALU.mult))
                for u in range(9, UNITS, 2):
                    copy_keys(u)
                per_block = rep[:, 0:32].rearrange("p (o s i) -> p o s i", o=1, i=1).to_broadcast([P, 4, 32, 4])
                for c in range(4):
                    dve.wait_ge(ss, 13 + c)
                    link(nc.vector.tensor_tensor(
                        s_sel[:, c * 512:c * 512 + 512].rearrange("p (j s i) -> p j s i", j=4, s=32),
                        ps[:, 2 + c, :].rearrange("p (j s i) -> p j s i", j=4, s=32), per_block, ALU.add))
                nc.vector.tensor_reduce(stat[:, 8:9], s_sel, AX.X, ALU.max, negate=True).then_inc(mx, 1)
                dve.wait_ge(ex, 2)
                link(nc.vector.reciprocal(stat[:, 6:7], stat[:, 5:6]))
                nc.vector.tensor_scalar(s_win, s_win, stat[:, 6:7], None, ALU.mult).then_inc(pn, 1)
                dve.wait_ge(ex, 3)
                link(nc.vector.reciprocal(stat[:, 10:11], stat[:, 9:10]))
                nc.vector.tensor_scalar(s_sel, s_sel, stat[:, 10:11], None, ALU.mult).then_inc(pn, 1)
                for q in (1, 3, 5):
                    dve.wait_ge(pt, q + 1)
                    if q == 1:
                        link(nc.vector.tensor_copy(pT[:, 4, :], ps[:, 6, 0:P]))
                        link(nc.vector.tensor_copy(pT[0:NS, 5, :], ps[0:NS, 6, P:2 * P]))
                        ins = nc.vector.tensor_copy(pT[:, 6:8, :], ps[:, 6, 256:512].rearrange("p (i r) -> p i r", i=2))
                    elif q == 3:
                        ins = nc.vector.tensor_copy(pT[:, 12:16, :], ps[:, 6, :].rearrange("p (i r) -> p i r", i=4))
                    else:
                        link(nc.vector.tensor_copy(pT[:, 20:22, :], ps[:, 6, 0:256].rearrange("p (i r) -> p i r", i=2)))
                        ins = nc.vector.tensor_copy(pT[0:NS, 22, :], ps[0:NS, 6, 256:384])
                    ins.then_inc(cd, 1)
                dve.wait_ge(ov, 2)
                for r, at in enumerate((0, 256, 128)):
                    for g in range(G):
                        p = slice(64 * g, 64 * g + 64)
                        for hg in range(HG):
                            link(nc.vector.tensor_copy(
                                oT[p, r, hg, 16 * hb:16 * hb + 16].rearrange("p (b t) -> p b t", b=4),
                                ps[p, 7, at:at + P].rearrange("p (b w) -> p b w", b=4)[:, :, 16 * g + 4 * hg:16 * g + 4 * hg + 4]))

        def sample_merge(l):
            tp = sem("sfin_turned")
            block = new_stage()
            @block.tensor
            def _(pe):
                for r in range(3):
                    for hg in range(HG):
                        ins = nc.tensor.transpose(ps[0:NS, r, hg * P:hg * P + P], oT[:, r, hg, :], ident)
                ins.then_inc(tp, 1)

            @block.vector
            def _(dve):
                link = dve_chain(dve)
                dve.wait_ge(tp, 1)
                zg = z[0:NS, TP, ZG:ZG + 24].rearrange("p (h r) -> p h r", r=3)
                out = z[0:NS, TP, ZQ:ZQ + 512].rearrange("p (h d) -> p h d", h=HEADS)
                tmp = hTf[0:NS, 0:512].rearrange("p (h d) -> p h d", h=HEADS)
                for r in range(3):
                    src = ps[0:NS, r, :].rearrange("p (h d) -> p h d", h=HEADS)
                    gt = zg[:, :, r:r + 1].to_broadcast([NS, HEADS, HD])
                    if r == 0:
                        link(nc.vector.tensor_tensor(out, src, gt, ALU.mult))
                    else:
                        link(nc.vector.tensor_tensor(tmp, src, gt, ALU.mult))
                        link(nc.vector.tensor_tensor(out, out, tmp, ALU.add))

        def turn_stage(stage, l, tiles, srcs, dst, scale=1.0, act_first=None):
            tp = sem(f"{stage}_turned")
            ev = [sem(f"{stage}_copied_{j}") for j in range(2)]
            n = len(srcs(0))
            nb = -(-n // 4)
            block = new_stage()
            @block.tensor
            def _(pe):
                for t in range(tiles):
                    if t >= 4:
                        for j in range(nb):
                            pe.wait_ge(ev[j], t - 3)
                    for k, src in enumerate(srcs(t)):
                        ins = nc.tensor.transpose(ps[:, 2 * (t % 4) + k // 4, (k % 4) * P:(k % 4) * P + P], src, ident)
                    ins.then_inc(tp, 1)

            def evict(eng, engine_copy, j):
                for t in range(tiles):
                    eng.wait_ge(tp, t + 1)
                    if j < nb:
                        m = min(4, n - 4 * j)
                        engine_copy(dst[:, 4 * j:4 * j + m, t * P:t * P + P],
                                    ps[:, 2 * (t % 4) + j, 0:m * P].rearrange("p (k t) -> p k t", k=m)).then_inc(ev[j], 1)

            @block.scalar
            def _(act):
                if act_first:
                    act_first(act)
                evict(act, nc.scalar.copy, 1)

            @block.vector
            def _(dve):
                evict(dve, lambda o, i: nc.vector.tensor_scalar(o, i, scale, None, ALU.mult), 0)

        A = lambda a, n: arena[:, a:a + n]
        memx = A(0, 2048).rearrange("p (t w) -> p t w", t=MT)
        zm = A(2048, 1024).rearrange("p (t w) -> p t w", t=MT)
        kmT = A(3072, 512).rearrange("p (e m) -> p e m", e=2)
        zx = A(3584, 1280).rearrange("p (t w) -> p t w", t=TT)
        qxT = A(4864, 2 * TT * P).rearrange("p (e t) -> p e t", e=2)
        ox = A(6144, 1280).rearrange("p (t w) -> p t w", t=TT)
        oxT = A(7424, 2 * TT * P).rearrange("p (e t) -> p e t", e=2)
        xsq = A(8704, 1280)
        qxb = A(9984, 512).rearrange("p (e b r) -> p e b r", e=2, b=DB)
        sx, pxT = A(10496, 256), A(10752, 256).rearrange("p (i r) -> p i r", i=2)

        def memory_kv(l):
            wt = slot("wkv").rearrange("p (k n) -> p k n", k=KT)
            norm_gemm_stage("wkv", l, memx, MT, 2, [("wkv" if t == 0 else None,
                                   token_products(t, hT, KT, lambda k: wt[:, k, :], 512),
                                   "ad"[t], copy_to(zm[:, t, :], 512), "wkv" if t == MT - 1 else None) for t in range(MT)],
                            list(range(MT)))

        def head_norm_stage(stage, l, view, g, scratch, act_first=None):
            go, root = sem(f"{stage}_squares"), sem(f"{stage}_root")
            n = view.shape[1] * view.shape[2]
            block = new_stage()
            @block.scalar
            def _(act):
                if act_first:
                    act_first(act)
                act.wait_ge(go, 1)
                nc.scalar.activation(stat[:, 80:80 + n], stat[:, 0:n], ACT.Sqrt).then_inc(root, 1)

            @block.vector
            def _(dve):
                head_norm(dve_chain(dve), [(view, g, 0, scratch)], n, root, go, HD)

        def store_memory(act, l):
            act.dma_start(dout["mem"][bass.ds(l, 1)].rearrange("a p t c -> (a p) t c"), zm).then_inc(mem_st, 16)

        def cross_samples(l):
            q_ok, s_ok, mx, ex, pn, tp, tc, o_ok, o_used = [sem(f"xs_{n}") for n in
                ("queries", "scores", "maxima", "exponentials", "probs", "turned", "copied", "outputs", "outputs_read")]
            read_at.update({f"mc{hb}": (o_ok, hb + 1) for hb in range(2)})
            block = new_stage()
            @block.tensor
            def _(pe):
                pe.wait_ge(q_ok, 1)
                for hb in range(2):
                    arrived(pe, f"mc{hb}")
                    kv = slot(f"mc{hb}").rearrange("p (b w) -> p b w", b=4)
                    for b4 in range(4):
                        for e in range(2):
                            ins = nc.tensor.matmul(ps[32 * b4:32 * b4 + 32, 0, 0:MEM], qxb[:, e, 4 * hb + b4, :],
                                                   kv[:, b4, MEM * e:MEM * e + MEM], start=(e == 0), stop=(e == 1))
                    ins.then_inc(s_ok, 1)
                    pe.wait_ge(pn, hb + 1)
                    for i in range(2):
                        ins = nc.tensor.transpose(ps[:, 1, i * P:i * P + P], sx[:, i * P:i * P + P], ident)
                    ins.then_inc(tp, 1)
                    pe.wait_ge(tc, hb + 1)
                    if hb:
                        pe.wait_ge(o_used, 1)
                    for b4 in range(4):
                        for e in range(2):
                            c = P * e + 32 * b4
                            for i in range(2):
                                v = kv[:, b4, 2 * MEM + MEM * i + P * e:2 * MEM + MEM * i + P * e + P]
                                ins = nc.tensor.matmul(ps[:, 2, c:c + 32], v, pxT[:, i, 32 * b4:32 * b4 + 32],
                                                       start=(i == 0), stop=(i == 1))
                    ins.then_inc(o_ok, 1)

            @block.scalar
            def _(act):
                for hb in range(2):
                    act.wait_ge(mx, hb + 1)
                    nc.scalar.activation(sx, ps[:, 0, 0:MEM], ACT.Exp, bias=stat[:, 0:1], accum_out=stat[:, 1:2]).then_inc(ex, 1)

            @block.vector
            def _(dve):
                link = dve_chain(dve)
                link(nc.vector.memset(qxb, 0.0))
                link(nc.vector.memset(oxT[:, :, SEQ:], 0.0))
                for h in range(XH):
                    p = slice(64 * (h % 2), 64 * (h % 2) + 64)
                    ins = nc.vector.tensor_copy(qxb[p, h // 2, :, 4 * h:4 * h + 4],
                                                qxT[p, h // 2, SEQ:TOK].rearrange("p (b t) -> p b t", b=DB))
                    link(ins) if h < XH - 1 else ins.then_inc(q_ok, 1)
                for hb in range(2):
                    dve.wait_ge(s_ok, hb + 1)
                    nc.vector.tensor_reduce(stat[:, 0:1], ps[:, 0, 0:MEM], AX.X, ALU.max, negate=True).then_inc(mx, 1)
                    dve.wait_ge(ex, hb + 1)
                    link(nc.vector.reciprocal(stat[:, 2:3], stat[:, 1:2]))
                    nc.vector.tensor_scalar(sx, sx, stat[:, 2:3], None, ALU.mult).then_inc(pn, 1)
                    dve.wait_ge(tp, hb + 1)
                    nc.vector.tensor_copy(pxT, ps[:, 1, 0:256].rearrange("p (i r) -> p i r", i=2)).then_inc(tc, 1)
                    dve.wait_ge(o_ok, hb + 1)
                    for h in range(XH):
                        p = slice(64 * (h % 2), 64 * (h % 2) + 64)
                        src = ps[p, 2, P * (h // 2):P * (h // 2) + P].rearrange("p (b w) -> p b w", b=4)[:, :, 4 * h:4 * h + 4]
                        dst = oxT[p, h // 2, SEQ + 16 * hb:SEQ + 16 * hb + 16].rearrange("p (b t) -> p b t", b=4)
                        ins = nc.vector.tensor_copy(dst, src)
                        link(ins) if h < XH - 1 else ins.then_inc(o_used, 1)

        hf = arena[:, 0:FF // P * TOK].rearrange("p (f t) -> p f t", f=FF // P)

        def mlp_hidden(l, arena_stored):
            def relu2(dst, n):
                def f(link, eng, bank):
                    if eng is nc.scalar:
                        link(nc.scalar.activation(dst, bank[:, 0:n], ACT.Relu))
                        return nc.scalar.activation(dst, dst, ACT.Square)
                    link(nc.vector.tensor_scalar(dst, bank[:, 0:n], 0.0, None, ALU.max))
                    return nc.vector.tensor_tensor(dst, dst, dst, ALU.mult)
                return f
            units = []
            for f in range(FF // P):
                name, q = f"w1_{f // 4}", f % 4
                wt = slot(name).rearrange("p (k n) -> p k n", k=KT)
                for part, (a, w) in enumerate(HALVES):
                    mms = [((slice(0, P), w), wt[:, k, q * P:q * P + P], hT[:, k, a:a + w]) for k in range(KT)]
                    units.append((name if q == 0 and part == 0 else None, mms, "ad"[f % 2], relu2(hf[:, f, a:a + w], w),
                                  name if q == 3 and part == 1 else None))
            norm_gemm_stage("mlp1", l, x[:, :, :], TT, 3, units, [(HALVES[i % 2][0] + HALVES[i % 2][1] - 1) // P
                            for i in range(len(units))], arena_stored)

        def mlp_out(l):
            prod, ev, rd = sem("mlp2_products"), sem("mlp2_added"), sem("mlp2_weights_read")
            bank = lambda half, t: (5 * half + t) % 8
            read_at.update({f"w2_{4 * h + c}": (rd, 3 * h + c + 1) if c < 3 else (prod, TT * (h + 1))
                            for h in range(2) for c in range(4)})
            block = new_stage()
            @block.tensor
            def _(pe):
                for half in range(2):
                    for c in range(4):
                        name = f"w2_{4 * half + c}"
                        arrived(pe, name)
                        wt = slot(name).rearrange("p (f n) -> p f n", f=8)
                        for t in range(TT):
                            w = P if t < TP else NS
                            if half and c == 0 and t >= 3:
                                pe.wait_ge(ev, t - 2)
                            groups = 1 if t < TP else 4
                            for f in range(8):
                                g = f % groups
                                ins = nc.tensor.matmul(ps[g * NS:g * NS + w, bank(half, t), :],
                                                       hf[:, 8 * c + f, t * P:t * P + w], wt[:, f, :],
                                                       start=(c == 0 and f < groups), stop=(c == 3 and f >= 8 - groups))
                            if c == 3:
                                ins.then_inc(prod, 1)
                        if c < 3:
                            ins.then_inc(rd, 1)

            @block.scalar
            def _(act):
                load_parameters(act, l + 1, prm_ld)
                act.wait_ge(prm_ld, 32)

            @block.vector
            def _(dve):
                link = dve_chain(dve)
                for half in range(2):
                    for t in range(TT):
                        dve.wait_ge(prod, 5 * half + t + 1)
                        cols_ = slice(512 * half, 512 * half + 512)
                        add = add_to(x[:, t, cols_], 512) if t < TP else sum_groups(x[0:NS, TP, cols_], 512, onto=True)
                        add(link, nc.vector, ps[:, bank(half, t), :]).then_inc(ev, 1)

        first, done = whole("inputs_loaded"), whole("tokens_stored")
        with nc.Block() as block:
            @block.sync
            def _(sp):
                sp.dma_start(pages[:, :], din["pages"]).then_inc(first, 16)
                sp.dma_start(cst[:, :], din["consts"]).then_inc(first, 16)
                sp.dma_start(x[:, :, :], din["x"]).then_inc(first, 16)
                sp.dma_start(gpage[:, :], din["gather"]).then_inc(first, 16)
                load_parameters(sp, 0, first)
                sp.wait_ge(first, 96)

            @block.vector
            def _(dve):
                dve.wait_ge(first, 96)
                link = idx_chain(dve)
                link(nc.vector.tensor_scalar(row[:, :], gpage[:, 0:DB], 8, -8 * POOL, ALU.mult, ALU.add))
                link(nc.vector.tensor_tensor(row[:, :], row[:, :], gpage[:, DB:2 * DB], ALU.add))

        def output_projection(l):
            units = []
            for c in range(2):
                wt = slot(f"w_out{c}").rearrange("p (k n) -> p k n", k=KT)
                for t in range(TT):
                    mms = token_products(t, hT, KT, lambda k: wt[:, k, :], 512)
                    a = 512 * c
                    units.append((f"w_out{c}" if t == 0 else None, mms, "d",
                                  add_to(x[:, t, a:a + 512], 512) if t < TP else sum_groups(x[0:NS, TP, a:a + 512], 512, onto=True),
                                  f"w_out{c}" if t == TT - 1 else None))


            def load_memory(act):
                act.wait_ge(kv_st, 16 * KV_STORES)
                act.dma_start(memx, din["mem"]).then_inc(mem_ld, 16)
            gemm_stage("out", l, units, load_memory, lambda act: act.wait_ge(mem_ld, 16))

        def cross_queries(l):
            wq = slot("wqo")[:, 0:2048].rearrange("p (k n) -> p k n", k=KT)
            norm_gemm_stage("wq", l, x[:, :, :], TT, 1, [("wqo" if t == 0 else None,
                                  token_products(t, hT, KT, lambda k: wq[:, k, :], 256), "d" if t == TP else "ad"[t % 2],
                                  copy_to(zx[:, t, :], 256) if t < TP else sum_groups(zx[0:NS, TP, :], 256), None) for t in range(TT)], list(range(TT)),
                            padding=zx[:, TP, :])

        def cross_output(l):
            wo = slot("wqo")[:, 2048:4096].rearrange("p (k n) -> p k n", k=2)
            units = []
            for t in range(TT):
                for c in range(2):
                    a = 512 * c
                    mms = token_products(t, oxT, 2, lambda k: wo[:, k, a:a + 512], 512)
                    units.append((None, mms, "d", add_to(x[:, t, a:a + 512], 512) if t < TP else
                                  sum_groups(x[0:NS, TP, a:a + 512], 512, groups=2, onto=True),
                                  "wqo" if (t, c) == (TT - 1, 1) else None))
            gemm_stage("wo", l, units)

        def run_half(l, loads, begin):
            with nc.Block() as block:
                @block.sync
                def _(sp):
                    fill_ring(sp, l, loads)
                    if begin:
                        for s, n in ((win_moved, DB), (kv_st, KV_STORES), (conv_st, 1), (m_st, 1), (ctp_st, 1),
                                     (cts_st, CTS_STORES), (mem_st, 1)):
                            sp.wait_ge(s, 16 * n)

                @block.gpsimd
                def _(pool):
                    if not begin:
                        gather_pages(pool, l)

                @block.tensor
                def _(pe):
                    for k in range(begin, len(stages)):
                        if "pe" in stages[k].parts:
                            stages[k].parts["pe"](pe)
                        meet(pe, "pe", k + 1)

                @block.scalar
                def _(act):
                    for k in range(begin, len(stages)):
                        if "act" in stages[k].parts:
                            stages[k].parts["act"](act)
                        meet(act, "act", k + 1)

                @block.vector
                def _(dve):
                    if not begin:
                        nc.vector.tensor_scalar(row[:, :], row[:, :], 8 * POOL, None, ALU.add).then_inc(idx_ok, 1)
                    for k in range(begin, len(stages)):
                        if "dve" in stages[k].parts:
                            stages[k].parts["dve"](dve)
                        meet(dve, "dve", k + 1)

        def clear(sems):
            with nc.Block() as block:
                @block.gpsimd
                def _(pool):
                    for s in sems[0::4]:
                        pool.sem_clear(s)

                @block.scalar
                def _(act):
                    for s in sems[1::4]:
                        act.sem_clear(s)

                @block.vector
                def _(dve):
                    for s in sems[2::4]:
                        dve.sem_clear(s)

                @block.tensor
                def _(pe):
                    for s in sems[3::4]:
                        pe.sem_clear(s)

        with nc.Fori(0, DEPTH) as l:
            def arena_stored(act):
                for s, n in ((m_st, 1), (ctp_st, 1), (mem_st, 1)):
                    act.wait_ge(s, 16 * n)

            input_projection(l)
            post_stage(l)
            gates_stage(l)
            prompt_mlstm(l)
            sample_mlstm(l)
            finish_mlstm(l)
            prep_stage(l)
            prompt_compress(l)
            prompt_attention(l)
            sample_attention(l, 0)
            sample_attention(l, 1)
            sample_merge(l)
            turn_stage("mix", l, TT, lambda t: [z[:, t, ZQ + P * k:ZQ + P * k + P] for k in range(4)]
                       + [z[:, t, ZO + P * k:ZO + P * k + P] for k in range(4)], hT)
            output_projection(l)
            stages_before = len(stages)
            run_half(l, FIRST_LOADS, 0)
            clear(half["sems"])
            half["held"].close()
            half["held"], half["sems"] = ExitStack(), []
            memory_kv(l)
            head_norm_stage("memk", l, zm[:, :, 0:256].rearrange("p t (h d) -> p t h d", h=XH), pr("xk"),
                            xsq[:, 0:512].rearrange("p (t h d) -> p t h d", t=MT, h=XH), lambda act: load_gain(act, l, 1))
            turn_stage("memT", l, MT, lambda t: [zm[:, t, P * e:P * e + P] for e in range(2)], kmT,
                       act_first=lambda act: store_memory(act, l))
            cross_queries(l)
            head_norm_stage("xprep", l, zx.rearrange("p t (h d) -> p t h d", h=XH), pr("xq"),
                            xsq.rearrange("p (t h d) -> p t h d", t=TT, h=XH), lambda act: load_gain(act, l, 3))
            turn_stage("xqT", l, TT, lambda t: [zx[:, t, P * e:P * e + P] for e in range(2)], qxT, QSC)
            tile_attention("xatt", l, [
                (qxT[64 * (h % 2):64 * (h % 2) + 64, h // 2, t * P:t * P + P], kmT[64 * (h % 2):64 * (h % 2) + 64, h // 2, :],
                 MEM, False, [zm[:, i, 256 + 64 * h:320 + 64 * h] for i in range(MT)], 64, None,
                 ox[:, t, 64 * h:64 * h + 64], False) for t in range(TP) for h in range(XH)])
            cross_samples(l)
            turn_stage("xT", l, TP, lambda t: [ox[:, t, P * e:P * e + P] for e in range(2)], oxT)
            cross_output(l)
            mlp_hidden(l, arena_stored)
            mlp_out(l)
            run_half(l, SECOND_LOADS, stages_before)
            clear(half["sems"] + layer_sems)

        with nc.Block() as block:
            @block.sync
            def _(sp):
                sp.dma_start(dout["y"], x[:, :, :]).then_inc(done, 16)
                sp.wait_ge(done, 16)
    return nc


def constants():
    c = np.zeros((P, NCST), np.float32)
    put = lambda n, a: c.__setitem__((slice(0, a.shape[0]), slice(*CST[n])), a)
    p = np.arange(P)
    put("id", np.eye(P, dtype=np.float32))
    put("causal", np.where(p[None, :] <= p[:, None], 0.0, NEG).astype(np.float32))
    put("tri", (p[:, None] <= p[None, :]).astype(np.float32))
    half = HD // 8
    freqs = np.float32(500000.0) ** (-np.arange(half, dtype=np.float32) / np.float32(half))
    pos = np.zeros((TT, P), np.float32)
    pos[:TP] = np.arange(SEQ).reshape(TP, P)
    pos[TP, :NS] = PAST + np.arange(NS) % DS
    ang = (pos[:, :, None] * freqs.astype(np.float32)).astype(np.float32)
    put("cos", np.cos(ang).transpose(1, 0, 2).reshape(P, -1))
    put("sin", np.sin(ang).transpose(1, 0, 2).reshape(P, -1))
    end = np.arange(NC_P) * STRIDE + CMP_LEN - 1
    seen = (end[None, None, :] <= (np.arange(TP)[None, :, None] * P + p[:, None, None]))
    put("cma", np.where(seen, 0.0, NEG).reshape(P, -1))
    put("cmm", seen.astype(np.float32).reshape(P, -1))
    tok = np.arange(NS)
    b4, t = p // 32, p % DS
    new = np.stack([((tok[None, :] // DS == 4 * hb + b4[:, None]) & (tok[None, :] % DS <= t[:, None])) for hb in range(2)], 1)
    put("new", np.where(new, 0.0, NEG).reshape(P, -1))
    put("low", np.where(np.arange(4)[None, :] >= t[:, None], 0.0, NEG))
    put("ms", ((tok[:, None] // DS == tok[None, :] // DS) & (tok[:, None] <= tok[None, :])).astype(np.float32))
    put("ohb", (tok[:, None] // DS == np.arange(DB)[None, :]).astype(np.float32))
    key = (p // 16) * DS + t
    put("grp", (key[:, None] == key[None, :]).astype(np.float32))
    put("one", np.ones((P, 1), np.float32))
    return c


def lay_out(x_prompt, x_sample, mem_prompt, cache_nsa_kv, cache_win_kv, cache_mem_kv, state_mlstm_C, state_mlstm_n,
            state_mlstm_m, state_conv, page_table, norm_mix_g, w_in, nsa_qn_g, nsa_kn_g, cmp_pos, cmp_w1, cmp_w2,
            ml_conv_w, ml_conv_b, ml_gate_b, ml_hn_g, w_out, norm_xa_g, norm_mem_g, xa_wq, xa_wkv, xa_qn_g, xa_kn_g,
            xa_wo, norm_mlp_g, mlp_w1, mlp_w2):
    L = DEPTH
    a = {}
    xs = np.zeros((P, D), np.float32)
    xs[:NS] = x_sample.reshape(NS, D)
    a["x"] = np.concatenate([x_prompt.reshape(TP, P, D), xs[None]]).transpose(1, 0, 2)
    a["mem"] = mem_prompt.reshape(MT, P, D).transpose(1, 0, 2)
    a["pages"] = page_table.reshape(1, DB * NPG)
    eighth = np.broadcast_to((np.arange(P) % 8)[:, None], (P, DB)).astype(page_table.dtype)
    a["gather"] = np.concatenate([np.repeat(page_table, 8, axis=1).T, eighth], 1)
    a["consts"] = constants()
    gains = np.stack([norm_mix_g, norm_xa_g, norm_mem_g, norm_mlp_g], 1).reshape(L * 4, 1, D)
    a["gains"] = np.broadcast_to(np.concatenate([gains, gains[:4]]), (L * 4 + 4, P, D))
    pm = np.zeros((L, P, NPRM), np.float32)

    def put(n, v, rows=P):
        pm[:, :rows, slice(*PRM[n])] = v
    put("qn", nsa_qn_g[:, None, :])
    put("kn", nsa_kn_g.reshape(L, 1, 192))
    put("hn", ml_hn_g[:, None, :])
    put("xq", xa_qn_g[:, None, :])
    put("xk", xa_kn_g[:, None, :])
    put("cw", ml_conv_w.reshape(L, 4, KT, P).transpose(0, 3, 2, 1).reshape(L, P, 32))
    put("cb", ml_conv_b.reshape(L, KT, P).transpose(0, 2, 1))
    put("bi", ml_gate_b[:, :MH, None], MH)
    put("bf", ml_gate_b[:, MH:, None], MH)
    put("w2", cmp_w2.transpose(0, 2, 1, 3).reshape(L, P, 128))
    put("pos", cmp_pos.reshape(L, 2, J, P).transpose(0, 3, 1, 2).reshape(L, P, 32))
    a["prm"] = np.concatenate([pm, pm[:1]])
    cols = lambda w, k: w.reshape(L, k, P, -1).transpose(0, 2, 1, 3)
    q, kv, g, qk, v, o, f = np.split(w_in, np.cumsum([512, 768, 24, 1024, 512, 512]).tolist(), axis=-1)
    q = q.reshape(L, D, G, HG, HD).transpose(0, 1, 3, 2, 4).reshape(L, D, 512)
    g = g.reshape(L, D, G, HG, 3).transpose(0, 1, 3, 2, 4).reshape(L, D, 24)
    wa = w_out[:, :512].reshape(L, G, HG, HD, D).transpose(0, 2, 1, 3, 4).reshape(L, 512, D)
    w_out = np.concatenate([wa, w_out[:, 512:]], 1)
    wi = cols(np.concatenate([q, kv, v, o, g, f], -1), KT)
    wqk, wo_, w1, w2 = cols(qk, KT), cols(w_out, KT), cols(mlp_w1, KT), cols(mlp_w2, FF // P)
    ch = {f"in{i}": wi[..., NZ * i:NZ * i + NZ] for i in range(5)}
    for i in range(2):
        ch[f"qk{i}"] = wqk[..., 512 * i:512 * i + 512]
        ch[f"w_out{i}"] = wo_[..., 512 * i:512 * i + 512]
    ch["cmpw"] = cmp_w1.reshape(L, 2, J, P, HID).transpose(0, 3, 1, 2, 4)
    ch["wkv"] = cols(xa_wkv, KT)
    ch["wqo"] = np.concatenate([cols(xa_wq, KT).reshape(L, P, -1), cols(xa_wo, 2).reshape(L, P, -1)], -1)
    for i in range(8):
        ch[f"w1_{i}"] = w1[..., 512 * i:512 * i + 512]
        ch[f"w2_{i}"] = w2[:, :, 8 * (i % 4):8 * (i % 4) + 8, 512 * (i // 4):512 * (i // 4) + 512]
    a["wst"] = np.concatenate([ch[n].reshape(L, -1) for n, _ in CHUNKS], 1)
    c = cache_nsa_kv.reshape(POOL, PAGE // 2, 2, L, 4, G, HD)
    a["cx"] = c[:, :, :, :, 0:2].transpose(3, 0, 2, 6, 1, 4, 5).reshape(L * POOL, P, 256)
    c = cache_nsa_kv.reshape(POOL * 8, 16, L, 4, P)
    a["kx"] = c[:, :, :, 2].transpose(2, 0, 1, 3).reshape(L * POOL * 8, 2048)
    a["vx"] = c[:, :, :, 3].transpose(2, 0, 1, 3).reshape(L * POOL * 8, 2048)
    w = cache_win_kv.reshape(L * DB, WIN, 2 * P)
    a["win"] = w
    a["winT"] = w[:, :, 0:P].transpose(0, 2, 1)
    m = cache_mem_kv.reshape(L, 2, 4, MEM, 2, 2, P)
    k_ = m[:, :, :, :, 0].transpose(0, 1, 5, 2, 4, 3)
    v_ = m[:, :, :, :, 1].reshape(L, 2, 4, MT, P, 2, P).transpose(0, 1, 4, 2, 3, 5, 6)
    a["mkv"] = np.concatenate([k_.reshape(L, 2, P, 4, 512), v_.reshape(L, 2, P, 4, 512)], -1).reshape(L * 2, P, 4096)
    a["cT"] = state_mlstm_C.transpose(0, 4, 2, 1, 3).reshape(L, P, 4096)
    a["nT"] = state_mlstm_n.transpose(0, 3, 2, 1).reshape(L, P, MH * DB)
    a["mT"] = state_mlstm_m.transpose(0, 2, 1)
    a["convT"] = state_conv.reshape(L, DB, 3, KT, P).transpose(0, 4, 3, 1, 2).reshape(L, P, KT * DB * 3)
    return {n: np.ascontiguousarray(v) for n, v in a.items()}


OUTS = {
    "y": (P, TT, D), "nsa_p": (DEPTH, P, TP, 512), "nsa_s": (DEPTH, NS, 512), "win_p": (DEPTH, P, TP, 256),
    "win_s": (DEPTH * DB, WIN, 256), "convT": (DEPTH, P, KT, NS + 3), "mT": (DEPTH, MH, TOK),
    "cT_p": (DEPTH, P, MH, 129), "cT_s": (DEPTH, P, 4096), "nT": (DEPTH, P, MH * DB), "mem": (DEPTH, P, MT, 512),
}


def kernel(**inputs):
    import concourse.bacc as _bacc
    from concourse.bass_utils import run_bass_kernel_spmd as _run

    arrays = lay_out(**{n: np.asarray(v) for n, v in inputs.items()})
    nc = _bacc.Bacc("TRN2", target_bir_lowering=False, num_devices=1)
    din = {n: nc.dram_tensor(f"in_{n}", v.shape, mybir.dt.from_np(v.dtype), kind="ExternalInput").ap()
           for n, v in arrays.items()}
    dout = {n: nc.dram_tensor(f"out_{n}", s, F32, kind="ExternalOutput").ap() for n, s in OUTS.items()}
    build(nc, din, dout)
    r = _run(nc, [{f"in_{n}": v for n, v in arrays.items()}], core_ids=[0])
    o = {n: np.asarray(r.results[0][f"out_{n}"]) for n in OUTS}
    L = DEPTH
    rows = o["y"].transpose(1, 0, 2)
    tok = lambda n, w: o[n].transpose(0, 2, 1, 3).reshape(L, SEQ, w)
    ct = o["cT_p"]
    cs_ = o["cT_s"].reshape(L, P, MH, DB, MD)
    cv = o["convT"]
    return (
        rows[:TP].reshape(1, SEQ, D), rows[TP, :NS].reshape(DB, DS, D),
        tok("nsa_p", 512).transpose(1, 0, 2).reshape(1, SEQ, L, 4, G, HD),
        o["nsa_s"].reshape(L, DB, DS, 4, G, HD).transpose(1, 2, 0, 3, 4, 5),
        tok("win_p", 256).reshape(L, 1, WIN, 2, G, HD),
        o["win_s"].reshape(L, DB, WIN, 2, G, HD),
        ct[..., 0:MD].transpose(0, 2, 3, 1).reshape(L, 1, MH, MD, MD),
        cs_.transpose(0, 3, 2, 4, 1),
        ct[..., MD].transpose(0, 2, 1).reshape(L, 1, MH, MD),
        o["nT"].reshape(L, MD, MH, DB).transpose(0, 3, 2, 1),
        o["mT"][:, :, SEQ - 1].reshape(L, 1, MH),
        o["mT"][:, :, SEQ + DS - 1::DS].transpose(0, 2, 1),
        cv[..., 0:3].transpose(0, 3, 2, 1).reshape(L, 1, 3, KT * P),
        cv[..., 3:].reshape(L, P, KT, DB, DS)[..., 1:].transpose(0, 3, 4, 2, 1).reshape(L, DB, 3, KT * P),
        o["mem"].transpose(0, 2, 1, 3).reshape(L, 1, MEM, 2, XH, HD),
    )
```

```python
from contextlib import ExitStack

import numpy as np

import concourse.bass as bass
from concourse import mybir

F32 = mybir.dt.float32
I32 = mybir.dt.int32
ALU = mybir.AluOpType
ACT = mybir.ActivationFunctionType
AX = mybir.AxisListType

P = 128
D = 1024
KT = D // P
SEQ, DB, DS = 512, 8, 4
NS = DB * DS
TP = SEQ // P
TT = TP + 1
TOK = SEQ + NS
DEPTH = 2
PAST, PAGE = 2048, 128
NPG = PAST // PAGE
POOL = DB * NPG * 5 // 4
HEADS, G, HG, HD = 8, 2, 4, 64
CMP_LEN, STRIDE, HID = 32, 16, 128
J = CMP_LEN // 2
NC_P = (SEQ - CMP_LEN) // STRIDE + 1
NC_S = (PAST + DS - CMP_LEN) // STRIDE + 1
SELB = 64
WIN = 512
MH, MD = 4, 128
XH = 4
MEM = 256
MT = MEM // P
FF = 4 * D
EPS = 1e-6
NEG = -1.0e30
BIG = 1.0e30

ZQ, ZK, ZV, ZO, ZG, ZI = 0, 512, 1280, 1792, 2304, 2328
ZW = 2336
NZ = 512

PRM = {}
_at = 0
for _n, _w in (("qn", 64), ("kn", 192), ("hn", 128), ("xq", 64), ("xk", 64), ("cw", 32), ("cb", 8),
               ("bi", 1), ("bf", 1), ("w2", 128), ("pos", 32)):
    PRM[_n] = (_at, _at + _w)
    _at += _w
NPRM = _at

CST = {}
_at = 0
for _n, _w in (("id", 128), ("causal", 128), ("tri", 128), ("cos", 40), ("sin", 40), ("cma", 4 * NC_P),
               ("cmm", 4 * NC_P), ("new", 64), ("low", 4), ("ms", 32), ("ohb", 8), ("grp", 128), ("one", 1),
               ("xnew", 4)):
    CST[_n] = (_at, _at + _w)
    _at += _w
NCST = _at

CHUNKS = [(f"in{i}", NZ * KT) for i in range(4)] + [("in4", (ZW - 4 * NZ) * KT), ("qk0", 4096), ("qk1", 4096),
          ("cmpw", 4096), ("w_out0", 4096), ("w_out1", 4096), ("wkv", 4096), ("wqo", 4096)] \
    + [(f"w1_{i}", 4096) for i in range(8)] + [(f"w2_{i}", 4096) for i in range(8)]
CH_AT = {}
_at = 0
for _n, _w in CHUNKS:
    CH_AT[_n] = (_at, _w)
    _at += P * _w
WTOT = _at

ORDER = ["in0", "in1", "in2", "in3", "in4", "qk0", "qk1", "cmpw"] + [f"cmp{b}" for b in range(DB)] + ["cst"]
for _g in range(2):
    ORDER += [f"k{2 * _g}", f"k{2 * _g + 1}", f"win{_g}", f"v{2 * _g}", f"v{2 * _g + 1}"]
ORDER += ["w_out0", "w_out1", "wkv", "wqo", "mc0", "mc1"] + [f"w1_{i}" for i in range(8)] + [f"w2_{i}" for i in range(8)]
FIRST_LOADS, SECOND_LOADS = ORDER[:ORDER.index("w1_0")], ORDER[ORDER.index("w1_0"):]
SLOT = {}
for _i, _n in enumerate(ORDER):
    if _n == "cmpw":
        SLOT[_n] = 3
        _rot = 0
    elif _n.startswith("cmp") or _n == "cst":
        SLOT[_n] = _rot % 3
        _rot += 1
    elif _i < ORDER.index("cmpw"):
        SLOT[_n] = _i % 4
    else:
        SLOT[_n] = (_i + 1) % 4


def slot_users():
    before, last = {}, {}
    for n in ORDER:
        before[n] = last.get(SLOT[n])
        last[SLOT[n]] = n
    return before


GATHERED = [f"cmp{b}" for b in range(1, DB, 2)] + [f"{k}{i}" for g in range(2) for k in "kv" for i in (2 * g, 2 * g + 1)]
ARRIVALS = {n: 16 * (NPG if n[:3] == "cmp" else 2) for n in GATHERED}


class Stage:

    def __init__(self):
        self.parts = {}

    def tensor(self, part):
        self.parts["pe"] = part

    def scalar(self, part):
        self.parts["act"] = part

    def vector(self, part):
        self.parts["dve"] = part


def build(nc, din, dout):
    before = slot_users()
    with ExitStack() as ctx:
        sb = lambda name, shape, dt=F32: ctx.enter_context(nc.sbuf_tensor(name, shape, dt))
        whole = lambda name: ctx.enter_context(nc.semaphore(name))
        layer_sems = []
        half = {"held": ExitStack(), "sems": []}

        def through_layer(name):
            layer_sems.append(whole(name))
            return layer_sems[-1]

        def sem(name):
            half["sems"].append(half["held"].enter_context(nc.semaphore(name)))
            return half["sems"][-1]

        x = sb("x", [P, TT, D])
        hT = sb("hT", [P, KT, TT * P])
        ring = sb("ring", [P, 4, 4096])
        arena = sb("arena", [P, TT * ZW + 2 * KT * TOK])
        hn = sb("hn", [P, 2, D])
        gain = sb("gain", [P, D])
        prm = sb("prm", [P, NPRM])
        cst = sb("cst", [P, NCST])
        stat = sb("stat", [P, 160])
        cols = sb("cols", [P, 128])
        pages = sb("pages", [1, DB * NPG], I32)
        row = sb("row", [P, DB], I32)
        gpage = sb("gpage", [P, 2 * DB], I32)
        ps = ctx.enter_context(nc.psum_tensor("ps", [P, 8, 512], F32))

        z = arena[:, 0:TT * ZW].rearrange("p (t w) -> p t w", t=TT)
        _o = TT * ZW
        zqkT = arena[:, _o:_o + KT * TOK].rearrange("p (c t) -> p c t", c=KT)
        qkT = arena[:, _o + KT * TOK:_o + 2 * KT * TOK].rearrange("p (c t) -> p c t", c=KT)
        hTf = hT[:, :, :].rearrange("p k t -> p (k t)")
        ropf = arena[:, _o:_o + KT * TOK]
        qkf = arena[:, _o + KT * TOK:_o + 2 * KT * TOK]

        def pr(n, rows=P):
            return prm[0:rows, PRM[n][0]:PRM[n][1]]

        def cs(n, rows=P):
            return cst[0:rows, CST[n][0]:CST[n][1]]

        ident = cs("id")
        loaded = [through_layer(f"slot_loaded{i}") for i in range(4)]
        gathered = whole("pages_arrived")
        idx_ok, gathers_in = through_layer("gather_rows_ready"), through_layer("gathers_arrived")
        win_moved = through_layer("window_rows_moved")
        prm_ld, m0_ld, n_ld, mem_ld = [through_layer(f"{n}_loaded") for n in ("parameters", "mlstm_m", "mlstm_n", "memory")]
        rows_normed, kv_st = through_layer("keys_values_ready"), through_layer("keys_values_stored")
        conv_st, m_st, ctp_st, cts_st, mem_st = [through_layer(f"{n}_stored") for n in
            ("conv_state", "mlstm_m", "prompt_c", "sample_c_n", "memory_kv")]
        KV_STORES, CTS_STORES = 3 + DB, MH + 1
        met = {e: through_layer(f"{e}_stages_done") for e in ("pe", "act", "dve")}
        stages, read_at = [], {}
        in_slot = [0] * 4
        loaded_at = {}
        for n in ORDER:
            if n not in GATHERED:
                in_slot[SLOT[n]] += 16 * (NPG if n[:3] == "cmp" and n != "cmpw" else 8 if n[:3] == "win" else 1)
                loaded_at[n] = in_slot[SLOT[n]]

        def slot(n):
            return ring[:, SLOT[n], :]

        def arrived(eng, n):
            if n in GATHERED:
                eng.wait_ge(gathers_in, GATHERED.index(n) + 1)
            else:
                eng.wait_ge(loaded[SLOT[n]], loaded_at[n])

        class Chain:

            def __init__(self, done):
                self.done, self.count = done, 0

            def __call__(self, eng):
                def link(ins):
                    self.count += 1
                    ins.then_inc(self.done, 1)
                    eng.wait_ge(self.done, self.count)
                return link

        act_chain, dve_chain = Chain(through_layer("act_step_done")), Chain(through_layer("dve_step_done"))
        idx_chain = Chain(whole("rows_step_done"))

        def new_stage():
            stages.append(Stage())
            return stages[-1]

        def meet(eng, name, count):
            eng.drain().then_inc(met[name], 1)
            for other in met:
                if other != name:
                    eng.wait_ge(met[other], count)

        def store_keys_values(sp, l):
            sp.wait_ge(rows_normed, 1)
            sp.dma_start(dout["nsa_p"][bass.ds(l, 1)].rearrange("a p t c -> (a p) t c"),
                         z[:, 0:TP, ZK:ZK + 512]).then_inc(kv_st, 16)
            sp.dma_start(dout["nsa_s"][bass.ds(l, 1)].rearrange("a r c -> (a r) c"),
                         z[0:NS, TP, ZK:ZK + 512]).then_inc(kv_st, 16)
            sp.dma_start(dout["win_p"][bass.ds(l, 1)].rearrange("a p t c -> (a p) t c"),
                         z[:, 0:TP, ZK + 512:ZK + 768]).then_inc(kv_st, 16)
            for b in range(DB):
                sp.dma_start(dout["win_s"][bass.ds(l * DB + b, 1), WIN - DS:WIN].rearrange("a r c -> (a r) c"),
                             z[4 * b:4 * b + 4, TP, ZK + 512:ZK + 768]).then_inc(kv_st, 16)

        def load_pages(eng, l, n, arrives):
            first_page = NPG * int(n[3:])
            with eng.Fori(0, NPG // 4) as i:
                for j in range(4):
                    page = eng.value_load(pages[0:1, bass.ds(i * 4 + (first_page + j), 1)], min_val=0, max_val=POOL - 1)
                    src = din["cx"][bass.ds(page + l * POOL, 1)].rearrange("a p w -> (a p) w")
                    eng.dma_start(slot(n)[:, bass.ds(i * 1024 + 256 * j, 256)], src).then_inc(arrives, 16)

        def fill_ring(sp, l, loads):
            for n in loads:
                if n in GATHERED:
                    continue
                if n == "cst":
                    store_keys_values(sp, l)
                if n == "win0":
                    for b in range(DB):
                        sp.dma_start(dout["win_s"][bass.ds(l * DB + b, 1), 0:WIN - DS],
                                     din["win"][bass.ds(l * DB + b, 1), DS:WIN]).then_inc(win_moved, 16)
                s = SLOT[n]
                if before[n]:
                    sp.wait_ge(*read_at[before[n]])
                dst = ring[:, s, :]
                if n in CH_AT:
                    at, w = CH_AT[n]
                    src = din["wst"][bass.ds(l, 1), at:at + P * w].rearrange("a (p w) -> (a p) w", p=P)
                    sp.dma_start(dst[:, 0:w], src).then_inc(loaded[s], 16)
                elif n == "cst":
                    sp.dma_start(dst, din["cT"][bass.ds(l, 1)].rearrange("a p w -> (a p) w")).then_inc(loaded[s], 16)
                elif n[:2] == "mc":
                    g = int(n[2:])
                    src = din["mkv"][bass.ds(l * 2 + g, 1)].rearrange("a p w -> (a p) w")
                    sp.dma_start(dst, src).then_inc(loaded[s], 16)
                elif n[:3] == "win":
                    g = int(n[3:])
                    for b in range(4):
                        src = din["winT"][bass.ds(l * DB + 4 * g + b, 1)].rearrange("a p w -> (a p) w")
                        sp.dma_start(dst[:, 512 * b:512 * b + 512], src).then_inc(loaded[s], 16)
                        src = din["win"][bass.ds(l * DB + 4 * g + b, 1), :, 128:256]
                        src = src.rearrange("a (t p) c -> p (a t) c", p=P)
                        sp.dma_start(dst[:, 2048 + 512 * b:2560 + 512 * b].rearrange("p (t c) -> p t c", t=4),
                                     src).then_inc(loaded[s], 16)
                else:
                    load_pages(sp, l, n, loaded[s])

        def gather_pages(pool, l):
            count = 0
            pool.wait_ge(idx_ok, 1)
            for i, n in enumerate(GATHERED):
                pool.wait_ge(*read_at[before[n]])
                if n[:3] == "cmp":
                    load_pages(pool, l, n, gathered)
                for h in range(0 if n[:3] == "cmp" else 2):
                    b = 2 * int(n[1:]) + h
                    pool.indirect_dma_start(
                        out=ring[:, SLOT[n], 2048 * h:2048 * h + 2048], out_offset=None, in_=din[n[0] + "x"],
                        in_offset=bass.IndirectOffsetOnAxis(ap=row[:, b:b + 1], axis=0)).then_inc(gathered, 16)
                count += ARRIVALS[n]
                pool.wait_ge(gathered, l * sum(ARRIVALS.values()) + count)
                pool.sem_inc(gathers_in, 1)

        gain_ld = [None] + [through_layer(f"gain{i}_loaded") for i in range(1, 4)]

        def load_parameters(eng, l, sem_of):
            eng.dma_start(prm[:, :], din["prm"][bass.ds(l, 1)].rearrange("a p w -> (a p) w")).then_inc(sem_of, 16)
            eng.dma_start(gain[:, :], din["gains"][bass.ds(l * 4, 1)].rearrange("a p w -> (a p) w")).then_inc(sem_of, 16)

        def load_gain(act, l, i):
            g = din["gains"][bass.ds(l * 4 + i, 1)].rearrange("a p w -> (a p) w")
            act.dma_start(gain[:, :], g).then_inc(gain_ld[i], 16)

        def products(mms, bank):
            groups = len({m[0][0].start for m in mms})
            for m, ((rows, n), a, b) in enumerate(mms):
                ins = nc.tensor.matmul(bank[rows, 0:n], a, b, start=(m < groups), stop=(m >= len(mms) - groups))
            return ins

        def tile_of(actT, t):
            return lambda k: actT[:, k, t * P:t * P + P]

        def token_products(t, act_tile, k_tiles, weights, n):
            if t < TP:
                return [((slice(0, P), n), act_tile(k), weights(k)) for k in range(k_tiles)]
            return [((slice(NS * (k % 4), NS * (k % 4) + NS), n), act_tile(k)[:, 0:NS], weights(k)) for k in range(k_tiles)]

        def sum_groups(dst, n, groups=4, onto=False):
            def f(link, eng, bank):
                for q in range(groups):
                    src = bank[NS * q:NS * q + NS, 0:n]
                    ins = (nc.vector.tensor_tensor(dst, src, dst, ALU.add) if q or onto else nc.vector.tensor_copy(dst, src))
                    if q < groups - 1:
                        link(ins)
                return ins
            return f

        def norm_gemm_stage(stage, l, src, tiles, gain_i, units, needs, act_first=None, act_last=None,
                            padding=None):
            ssq, msq, rt, hn_ok, tp, ea, ed, prod = [sem(f"{stage}_{n}") for n in
                ("squares", "mean", "root", "rows_ready", "turned", "copied_a", "copied_d", "products")]
            ev = {e: sem(f"{stage}_evicted_{e}") for e in "ad"}
            BANKS = 4
            nth, cnt, steps, t = [], {"a": 0, "d": 0}, [], 0
            for i, u in enumerate(units):
                cnt[u[2]] += 1
                nth.append(cnt[u[2]])
                while t < min(needs[i] + 2, tiles):
                    steps.append(("tile", t))
                    t += 1
                steps.append(("unit", i))
            read_at.update({u[4]: (prod, i + 1) for i, u in enumerate(units) if u[4]})
            bank = lambda i: ps[:, 4 + i % BANKS, :]
            half_tile = lambda t, h: ps[:, 2 * (t % 2) + h, :].rearrange("p (k t) -> p k t", k=4)
            block = new_stage()


            @block.tensor
            def _(pe):
                for kind, i in steps:
                    if kind == "tile":
                        pe.wait_ge(hn_ok, i + 1)
                        if i >= 2:
                            pe.wait_ge(ea, i - 1)
                            pe.wait_ge(ed, i - 1)
                        for k in range(8):
                            ins = nc.tensor.transpose(ps[:, 2 * (i % 2) + k // 4, (k % 4) * P:(k % 4) * P + P],
                                                      hn[:, i % 2, k * P:k * P + P], ident)
                            if k % 4 == 3:
                                ins.then_inc(tp, 1)
                        continue
                    load, mms = units[i][0:2]
                    if load:
                        arrived(pe, load)
                    if i == 0 or needs[i] > max(needs[:i]):
                        pe.wait_ge(ea, needs[i] + 1)
                        pe.wait_ge(ed, needs[i] + 1)
                    if i == 2:
                        pe.wait_ge(ssq, tiles)
                    if i >= BANKS:
                        pe.wait_ge(ev[units[i - BANKS][2]], nth[i - BANKS])
                    products(mms, bank(i)).then_inc(prod, 1)

            @block.scalar
            def _(act):
                if act_first:
                    act_first(act)
                link = act_chain(act)

                def square(t):
                    if t >= tiles:
                        return
                    if t:
                        act.wait_ge(ssq, t)
                    nc.scalar.activation(ps[:, 6:8, :], src[:, t, :].rearrange("p (b c) -> p b c", b=2), ACT.Square,
                                         accum_out=stat[:, t:t + 1]).then_inc(ssq, 1)

                def root(t):
                    if t >= tiles:
                        return
                    act.wait_ge(msq, t + 1)
                    nc.scalar.activation(stat[:, 24 + t:25 + t], stat[:, 16 + t:17 + t], ACT.Sqrt).then_inc(rt, 1)
                square(0)
                square(1)
                root(0)
                square(2)
                root(1)
                for kind, i in steps:
                    if kind == "tile":
                        act.wait_ge(tp, 2 * i + 1)
                        nc.scalar.copy(hT[:, 0:4, i * P:i * P + P], half_tile(i, 0)).then_inc(ea, 1)
                        square(i + 3)
                        root(i + 2)
                    elif units[i][2] == "a":
                        act.wait_ge(prod, i + 1)
                        units[i][3](link, nc.scalar, bank(i)).then_inc(ev["a"], 1)
                if act_last:
                    act_last(act)

            @block.vector
            def _(dve):
                link = dve_chain(dve)

                def mean(t):
                    if t >= tiles:
                        return
                    dve.wait_ge(ssq, t + 1)
                    nc.vector.tensor_scalar(stat[:, 16 + t:17 + t], stat[:, t:t + 1], 1.0 / D, EPS, ALU.mult,
                                            ALU.add).then_inc(msq, 1)

                def rows(t):
                    if t >= tiles:
                        return
                    dve.wait_ge(rt, t + 1)
                    link(nc.vector.reciprocal(stat[:, 32 + t:33 + t], stat[:, 24 + t:25 + t]))
                    if t >= 2:
                        dve.wait_ge(tp, 2 * t - 2)
                    nc.vector.scalar_tensor_tensor(out=hn[:, t % 2, :], in0=src[:, t, :],
                                                   scalar=stat[:, 32 + t:33 + t], in1=gain[:, :],
                                                   op0=ALU.mult, op1=ALU.mult).then_inc(hn_ok, 1)
                if padding is not None:
                    link(nc.vector.memset(padding, 0.0))
                mean(0)
                mean(1)
                if gain_i:
                    dve.wait_ge(gain_ld[gain_i], 16)
                rows(0)
                for kind, i in steps:
                    if kind == "tile":
                        mean(i + 2)
                        rows(i + 1)
                        dve.wait_ge(tp, 2 * i + 2)
                        nc.vector.tensor_copy(hT[:, 4:8, i * P:i * P + P], half_tile(i, 1)).then_inc(ed, 1)
                    elif units[i][2] == "d":
                        dve.wait_ge(prod, i + 1)
                        units[i][3](link, nc.vector, bank(i)).then_inc(ev["d"], 1)

        def gemm_stage(stage, l, units, act_first=None, act_last=None):
            prod, ev = sem(f"{stage}_products"), {e: sem(f"{stage}_evicted_{e}") for e in {u[2] for u in units}}
            nth, cnt = [], {"a": 0, "d": 0}
            for u in units:
                cnt[u[2]] += 1
                nth.append(cnt[u[2]])
            read_at.update({u[4]: (prod, i + 1) for i, u in enumerate(units) if u[4]})
            block = new_stage()

            @block.tensor
            def _(pe):
                for i, (load, mms, e, _, _) in enumerate(units):
                    if load:
                        arrived(pe, load)
                    if i >= 8:
                        pe.wait_ge(ev[units[i - 8][2]], nth[i - 8])
                    products(mms, ps[:, i % 8, :]).then_inc(prod, 1)

            @block.scalar
            def _(act):
                if act_first:
                    act_first(act)
                link = act_chain(act)
                for i, u in enumerate(units):
                    if u[2] == "a":
                        act.wait_ge(prod, i + 1)
                        u[3](link, nc.scalar, ps[:, i % 8, :]).then_inc(ev["a"], 1)
                if act_last:
                    act_last(act)

            @block.vector
            def _(dve):
                link = dve_chain(dve)
                for i, u in enumerate(units):
                    if u[2] == "d":
                        dve.wait_ge(prod, i + 1)
                        u[3](link, nc.vector, ps[:, i % 8, :]).then_inc(ev["d"], 1)

        def copy_to(dst, n):
            def f(link, eng, bank):
                src = bank[:, 0:n]
                return nc.scalar.copy(dst, src) if eng is nc.scalar else nc.vector.tensor_copy(dst, src)
            return f

        def add_to(dst, n):
            return lambda link, eng, bank: nc.vector.tensor_tensor(dst, bank[:, 0:n], dst, ALU.add)

        def head_norm(link, heads, nh_total, act_go, dve_go, width):
            for v, _, c, scratch in heads:
                t, h = v.shape[1], v.shape[2]
                link(nc.vector.tensor_tensor(scratch, v, v, ALU.mult))
                link(nc.vector.tensor_reduce(stat[:, c:c + t * h].rearrange("p (t h) -> p t h", t=t), scratch,
                                             AX.X, ALU.add))
            nc.vector.tensor_scalar(stat[:, 0:nh_total], stat[:, 0:nh_total], 1.0 / width, EPS, ALU.mult,
                                    ALU.add).then_inc(dve_go, 1)
            nc.vector.wait_ge(act_go, 1)
            link(nc.vector.reciprocal(stat[:, 80:80 + nh_total], stat[:, 80:80 + nh_total]))
            for v, g, c, _ in heads:
                t, h, w = v.shape[1], v.shape[2], v.shape[3]
                r = stat[:, 80 + c:80 + c + t * h].rearrange("p (t h o) -> p t h o", t=t, o=1)
                link(nc.vector.tensor_tensor(v, v, r.to_broadcast([P, t, h, w]), ALU.mult))
                gg = g.rearrange("p (a b w) -> p a b w", a=1, b=1).to_broadcast([P, t, h, w])
                link(nc.vector.tensor_tensor(v, v, gg, ALU.mult))


        HALVES = ((0, TOK // 2), (TOK // 2, TOK - TOK // 2))

        def input_projection(l):
            units, needs = [], []
            for c in range(5):
                w = min(NZ, ZW - NZ * c)
                wt = slot(f"in{c}")[:, 0:w * KT].rearrange("p (k n) -> p k n", k=KT)
                for t in range(TT):
                    mms = token_products(t, tile_of(hT, t), KT, lambda k: wt[:, k, :], w)
                    a = NZ * c
                    needs.append(t)
                    units.append((f"in{c}" if t == 0 else None, mms, "d" if t == TP else "ad"[(c + t) % 2],
                                  copy_to(z[:, t, a:a + w], w) if t < TP else sum_groups(z[0:NS, TP, a:a + w], w),
                                  f"in{c}" if t == TT - 1 else None))
            for c in range(KT):
                name, q = f"qk{c // 4}", c % 4
                wt = slot(name).rearrange("p (k n) -> p k n", k=KT)
                for part, (a, w) in enumerate(HALVES):
                    mms = [((slice(0, P), w), wt[:, k, q * P:q * P + P], hT[:, k, a:a + w]) for k in range(KT)]
                    needs.append(TT - 1)
                    units.append((name if q == 0 and part == 0 else None, mms, "ad"[c % 2],
                                  copy_to(zqkT[:, c, a:a + w], w), name if q == 3 and part == 1 else None))
            norm_gemm_stage("in", l, x[:, :, :], TT, 0, units, needs, padding=z[:, TP, :])

        kc_s = hn[:, 0, :].rearrange("p (b c) -> p b c", b=DB)
        vc_s = hn[:, 1, :].rearrange("p (b c) -> p b c", b=DB)

        def compression(stage, jobs, with_bias):
            prod, hid_ok, pr2, ev2, bi, bi_ok = [sem(f"{stage}_{n}") for n in
                ("products", "hidden_ready", "outputs", "evicted", "position_bias", "bias_ready")]
            w1 = slot("cmpw").rearrange("p (k j n) -> p k j n", k=2, j=J)
            pos = pr("pos").rearrange("p (k j) -> p k j", k=2)
            w2 = pr("w2").rearrange("p (k d) -> p k d", k=2)
            hid = hTf[:, 3200:4224].rearrange("p (s c) -> p s c", s=2)
            read_at.update({job[0]: (prod, 2 * i + 2) for i, job in enumerate(jobs) if job[0]})
            read_at["cmpw"] = (prod, 2 * len(jobs))

            def tensor_program(pe, between=None):
                arrived(pe, "cmpw")
                if with_bias:
                    for k in range(2):
                        for j in range(J):
                            ins = nc.tensor.matmul(ps[:, 4, k:k + 1], w1[:, k, j, :], pos[:, k, j:j + 1],
                                                   start=(j == 0), stop=(j == J - 1))
                    ins.then_inc(bi, 1)

                def second(i):
                    n = jobs[i][2]
                    o = 4 + i % 2
                    pe.wait_ge(hid_ok, 2 * i + 2)
                    if i >= 2:
                        pe.wait_ge(ev2, 2 * (i - 1))
                    h = hid[:, i % 2, 0:4 * n].rearrange("p (k g c) -> p k g c", k=2, g=G)
                    for g in range(G):
                        nc.tensor.matmul(ps[64 * g:64 * g + 64, o, 0:n], w2[:, 0, :], h[:, 0, g, :],
                                         start=True, stop=True)
                    for g in range(G):
                        ins = nc.tensor.matmul(ps[0:n, o, 128 + 64 * g:192 + 64 * g], h[:, 1, g, :], w2[:, 1, :],
                                               start=True, stop=True)
                    ins.then_inc(pr2, 1)
                for i, (load, tok, n, _, _) in enumerate(jobs):
                    if between and between[0] == i:
                        between[1](pe)
                    if load:
                        arrived(pe, load)
                    if i >= 2:
                        pe.wait_ge(hid_ok, 2 * i - 2)
                    for k in range(2):
                        for j in range(J):
                            v = tok.rearrange("p q (k g) -> p k g q", k=2)[:, k, :, j:j + 8 * (n - 1) + 1:8]
                            ins = nc.tensor.matmul(ps[:, 2 * (i % 2) + k, 0:G * n], w1[:, k, j, :], v,
                                                   start=(j == 0), stop=(j == J - 1))
                        ins.then_inc(prod, 1)
                    if i:
                        second(i - 1)
                second(len(jobs) - 1)

            def hidden(act, i):
                n = jobs[i][2]
                if i == 0 and with_bias:
                    act.wait_ge(bi_ok, 1)
                for k in range(2):
                    act.wait_ge(prod, 2 * i + k + 1)
                    if i >= 2 and k == 0:
                        act.wait_ge(pr2, i - 1)
                    nc.scalar.activation(hid[:, i % 2, 2 * k * n:2 * (k + 1) * n], ps[:, 2 * (i % 2) + k, 0:G * n],
                                         ACT.Silu, bias=stat[:, 158 + k:159 + k]).then_inc(hid_ok, 1)

            def bias(dve):
                dve.wait_ge(bi, 1)
                nc.vector.tensor_copy(stat[:, 158:160], ps[:, 4, 0:2]).then_inc(bi_ok, 1)

            def evict(dve, i):
                _, _, n, kc, vc = jobs[i]
                dve.wait_ge(pr2, i + 1)
                nc.vector.tensor_copy(kc, ps[:, 4 + i % 2, 0:n]).then_inc(ev2, 1)
                nc.vector.tensor_copy(vc, ps[0:n, 4 + i % 2, 128:256]).then_inc(ev2, 1)
            return tensor_program, hidden, bias, evict

        wpcol = cols[:, 48:64].rearrange("p (h t) -> p h t", h=MH)
        m0 = cols[0:MH, 64:64 + DB]
        nT = cols[:, 96:96 + MH * DB].rearrange("p (h b) -> p h b", h=MH)

        grow = gain[0:MH, 0:TOK]
        decay = gain[0:MH, TOK:TOK + DB]
        gcol = cols[:, 0:20].rearrange("p (t h) -> p t h", t=TT)
        emcol = cols[:, 20:40].rearrange("p (t h) -> p t h", t=TT)
        wscol, ascol = cols[0:NS, 40:44], cols[0:NS, 44:48]

        def mlstm_gates(l):
            tp, ex, exd, rows_ok, tp2, ev2 = [sem(f"gates_{n}") for n in
                ("turned", "to_act", "from_act", "rows_ready", "columns", "columns_out")]
            R = lambda a, n=TOK: hTf[0:MH, a:a + n]
            li, lf, F, g, zero, m = R(4224), grow, R(0), R(TOK), R(2 * TOK), R(3 * TOK)
            ab, wg, av = F, R(4 * TOK, NS), R(4 * TOK + NS, NS)
            s4 = lambda r: r[:, SEQ:TOK].rearrange("p (b u) -> p b u", b=DB)
            n4 = lambda r: r.rearrange("p (b u) -> p b u", b=DB)

            def turn_gates(pe):
                for half in range(2):
                    for t in range(TT):
                        b, c = (6 + half, t * P) if t < TP else (5, half * P)
                        ins = nc.tensor.transpose(ps[0:MH, b, c:c + P], z[:, t, ZI + MH * half:ZI + MH * half + MH], ident)
                ins.then_inc(tp, 1)

            def turn_rows(pe):
                pe.wait_ge(rows_ok, 1)
                i4 = ident[0:MH, 0:MH]
                for n, r in enumerate((g, m)):
                    for t in range(TT):
                        w = P if t < TP else NS
                        nc.tensor.transpose(ps[0:w, 6, 20 * n + 4 * t:20 * n + 4 * t + 4], r[:, t * P:t * P + w], i4)
                for n, r in enumerate((wg, av)):
                    ins = nc.tensor.transpose(ps[0:NS, 6, 40 + 4 * n:44 + 4 * n], r, i4)
                ins.then_inc(tp2, 1)

            def log_terms(act, link):
                act.wait_ge(ex, 1)
                link(nc.scalar.activation(ab, lf, ACT.Abs))
                link(nc.scalar.activation(ab, ab, ACT.Exp, scale=-1.0))
                nc.scalar.activation(ab, ab, ACT.Ln, bias=1.0).then_inc(exd, 1)

            def decays(act, link):
                act.wait_ge(ex, 2)
                link(nc.scalar.activation(decay, decay, ACT.Exp))
                link(nc.scalar.activation(wg, wg, ACT.Exp))
                nc.scalar.activation(av, av, ACT.Exp).then_inc(exd, 1)
                act.wait_ge(rows_ok, 1)
                act.dma_start(dout["mT"][bass.ds(l, 1)].rearrange("a p w -> (a p) w"), m).then_inc(m_st, 16)

            def column_terms(act, link):
                act.wait_ge(ev2, 2)
                link(nc.scalar.activation(cols[:, 20:36], cols[:, 20:36], ACT.Exp, scale=-1.0))
                link(nc.scalar.activation(cols[0:NS, 36:40], cols[0:NS, 36:40], ACT.Exp, scale=-1.0))

            def take_gates(dve, link):
                link(nc.vector.memset(cols[:, 16:20], 0.0))
                link(nc.vector.memset(cols[:, 36:40], 0.0))
                dve.wait_ge(tp, 1)
                for half, (r, b) in enumerate(((li, "bi"), (lf, "bf"))):
                    link(nc.vector.tensor_scalar(r[:, 0:SEQ], ps[0:MH, 6 + half, :], pr(b, MH), None, ALU.add))
                    link(nc.vector.tensor_scalar(r[:, SEQ:TOK], ps[0:MH, 5, half * P:half * P + NS], pr(b, MH), None, ALU.add))

            def scan_rows(dve, link):
                nc.vector.memset(zero, 0.0).then_inc(ex, 1)
                dve.wait_ge(ex, 1)
                dve.wait_ge(exd, 1)
                link(nc.vector.scalar_tensor_tensor(out=lf, in0=lf, scalar=0.0, in1=ab, op0=ALU.min, op1=ALU.subtract))
                link(nc.vector.tensor_tensor_scan(F[:, 0:SEQ], lf[:, 0:SEQ], zero[:, 0:SEQ], 0.0, ALU.add, ALU.add))
                link(nc.vector.tensor_copy(s4(F)[:, :, 0:1], s4(lf)[:, :, 0:1]))
                for u in range(1, DS):
                    link(nc.vector.tensor_tensor(s4(F)[:, :, u:u + 1], s4(F)[:, :, u - 1:u], s4(lf)[:, :, u:u + 1], ALU.add))
                link(nc.vector.tensor_tensor(g, li, F, ALU.subtract))
                link(nc.vector.tensor_tensor_scan(grow[:, 0:SEQ], g[:, 0:SEQ], g[:, 0:SEQ], 0.0, ALU.max, ALU.max))
                dve.wait_ge(m0_ld, 16)
                m3 = m0.rearrange("p (b o) -> p b o", o=1)
                for u in range(DS):
                    prev = m3 if u == 0 else s4(grow)[:, :, u - 1:u]
                    link(nc.vector.tensor_tensor(s4(grow)[:, :, u:u + 1], prev, s4(g)[:, :, u:u + 1], ALU.max))
                link(nc.vector.tensor_tensor(m, F, grow, ALU.add))
                last = s4(grow)[:, :, DS - 1:DS]
                link(nc.vector.tensor_tensor(decay.rearrange("p (b o) -> p b o", o=1), m3, last, ALU.subtract))
                link(nc.vector.tensor_tensor(n4(wg), s4(g), last.to_broadcast([MH, DB, DS]), ALU.subtract))
                nc.vector.tensor_tensor(n4(av), m3.to_broadcast([MH, DB, DS]), s4(grow), ALU.subtract).then_inc(ex, 1)

            def rows_ready(dve, link):
                dve.wait_ge(exd, 2)
                nc.vector.tensor_copy(zero[:, 0:1], g[:, 0:1]).then_inc(rows_ok, 1)

            def take_columns(dve, link):
                dve.wait_ge(tp2, 1)
                for n in range(2):
                    link(nc.vector.tensor_copy(cols[:, 20 * n:20 * n + 16], ps[:, 6, 20 * n:20 * n + 16]))
                    nc.vector.tensor_copy(cols[0:NS, 20 * n + 16:20 * n + 20], ps[0:NS, 6, 20 * n + 16:20 * n + 20]).then_inc(ev2, 1)
                link(nc.vector.tensor_copy(cols[0:NS, 40:48], ps[0:NS, 6, 40:48]))
            return (turn_gates, turn_rows), (log_terms, decays, column_terms), (take_gates, scan_rows, rows_ready, take_columns)

        def post_stage(l):
            go, root, cv_ld, y0, y1, silu, gated = [sem(f"post_{n}") for n in
                ("squares", "root", "state_loaded", "conv_begun", "conv_done", "silu_done", "gates_ready")]
            tensor_program, hidden, bias, evict = compression("compress", [
                (f"cmp{b}", slot(f"cmp{b}").rearrange("p (q w) -> p q w", w=4), NC_S, kc_s[:, b, 0:NC_S],
                 vc_s[0:NC_S, b, :]) for b in range(DB)], True)
            (turn_gates, turn_rows), (log_terms, decays, column_terms), (take_gates, scan_rows, rows_ready, take_columns) = \
                mlstm_gates(l)
            sq = hTf[:, 0:2560]
            tail = hTf[:, 2560:3008].rearrange("p (c b u) -> p c b u", c=KT, b=DB)
            held = hTf[:, 3008:3200]
            q = z[:, :, ZQ:ZQ + 512].rearrange("p t (h d) -> p t h d", h=HEADS)
            ks = [z[:, :, ZK + 256 * r:ZK + 256 * r + 128].rearrange("p t (h d) -> p t h d", h=G) for r in range(3)]
            heads = [(q, pr("qn"), 0, sq.rearrange("p (t h d) -> p t h d", t=TT, h=HEADS))]
            heads += [(ks[r], prm[:, PRM["kn"][0] + 64 * r:PRM["kn"][0] + 64 * r + 64], 40 + 10 * r,
                       sq[:, 0:640].rearrange("p (t h d) -> p t h d", t=TT, h=G)) for r in range(3)]
            block = new_stage()


            @block.tensor
            def _(pe):
                turn_gates(pe)
                tensor_program(pe, (6, turn_rows))

            @block.scalar
            def _(act):
                link = act_chain(act)
                act.dma_start(held, din["convT"][bass.ds(l, 1)].rearrange("a p w -> (a p) w")).then_inc(cv_ld, 16)
                act.dma_start(dout["convT"][bass.ds(l, 1)].rearrange("a p c t -> (a p) c t"),
                              zqkT[:, :, SEQ - 3:TOK]).then_inc(conv_st, 16)
                act.dma_start(m0, din["mT"][bass.ds(l, 1)].rearrange("a p w -> (a p) w")).then_inc(m0_ld, 16)
                act.dma_start(nT, din["nT"][bass.ds(l, 1)].rearrange("a p (h b) -> (a p) h b", h=MH)).then_inc(n_ld, 16)
                for c in range(KT):
                    w3 = PRM["cw"][0] + 4 * c + 3
                    nc.scalar.activation(qkT[:, c, 0:SEQ], zqkT[:, c, 0:SEQ], ACT.Identity,
                                         bias=prm[:, PRM["cb"][0] + c:PRM["cb"][0] + c + 1],
                                         scale=prm[:, w3:w3 + 1]).then_inc(y0, 1)
                act.wait_ge(go, 1)
                nc.scalar.activation(stat[:, 80:150], stat[:, 0:70], ACT.Sqrt).then_inc(root, 1)
                nc.scalar.activation(z[:, :, ZO:ZI], z[:, :, ZO:ZI], ACT.Sigmoid).then_inc(gated, 1)
                hidden(act, 0)
                hidden(act, 1)
                log_terms(act, link)
                decays(act, link)
                for c in range(KT):
                    act.wait_ge(y1, c + 1)
                    nc.scalar.activation(qkT[:, c, :], qkT[:, c, :], ACT.Silu).then_inc(silu, 1)
                    if c % 2:
                        hidden(act, 2 + c // 2)
                column_terms(act, link)
                hidden(act, 6)
                hidden(act, 7)
                act.wait_ge(silu, KT)
                act.wait_ge(m_st, 16)
                act.wait_ge(conv_st, 16)

            @block.vector
            def _(dve):
                link = dve_chain(dve)
                take_gates(dve, link)
                bias(dve)
                head_norm(link, heads, 70, root, go, HD)
                cos = cs("cos").rearrange("p (t o f) -> p t o f", t=TT, o=1)
                sin = cs("sin").rearrange("p (t o f) -> p t o f", t=TT, o=1)
                for v, h in [(q, HEADS)] + [(k, G) for k in ks]:
                    a, b = v[:, :, :, 0:8], v[:, :, :, 8:16]
                    t = [sq[:, 320 * i:320 * i + TT * h * 8].rearrange("p (t h f) -> p t h f", t=TT, h=h) for i in range(4)]
                    cb, sb_ = cos.to_broadcast([P, TT, h, 8]), sin.to_broadcast([P, TT, h, 8])
                    link(nc.vector.tensor_tensor(t[0], a, cb, ALU.mult))
                    link(nc.vector.tensor_tensor(t[1], b, sb_, ALU.mult))
                    link(nc.vector.tensor_tensor(t[2], b, cb, ALU.mult))
                    link(nc.vector.tensor_tensor(t[3], a, sb_, ALU.mult))
                    link(nc.vector.tensor_tensor(a, t[0], t[1], ALU.subtract))
                    link(nc.vector.tensor_tensor(b, t[2], t[3], ALU.add))
                nc.vector.tensor_copy(stat[:, 0:1], stat[:, 1:2]).then_inc(rows_normed, 1)
                scan_rows(dve, link)
                evict(dve, 0)
                rows_ready(dve, link)
                dve.wait_ge(cv_ld, 16)
                link(nc.vector.tensor_copy(tail[:, :, :, 0:3], held.rearrange("p (c b u) -> p c b u", c=KT, b=DB)))
                link(nc.vector.tensor_copy(tail[:, :, :, 3:7],
                                           zqkT[:, :, SEQ:TOK].rearrange("p c (b u) -> p c b u", b=DB)))
                for c in range(KT):
                    cw = PRM["cw"][0] + 4 * c
                    dve.wait_ge(y0, c + 1)
                    y = qkT[:, c, SEQ:TOK].rearrange("p (b u) -> p b u", b=DB)
                    for j in range(1, 4):
                        link(nc.vector.scalar_tensor_tensor(
                            out=qkT[:, c, j:SEQ], in0=zqkT[:, c, 0:SEQ - j], scalar=prm[:, cw + 3 - j:cw + 4 - j],
                            in1=qkT[:, c, j:SEQ], op0=ALU.mult, op1=ALU.add))
                    link(nc.vector.tensor_scalar(y, tail[:, c, :, 3:7], prm[:, cw + 3:cw + 4],
                                                 prm[:, PRM["cb"][0] + c:PRM["cb"][0] + c + 1], ALU.mult, ALU.add))
                    for j in range(3):
                        ins = nc.vector.scalar_tensor_tensor(out=y, in0=tail[:, c, :, j:j + 4],
                                                             scalar=prm[:, cw + j:cw + j + 1], in1=y,
                                                             op0=ALU.mult, op1=ALU.add)
                        if j < 2:
                            link(ins)
                    ins.then_inc(y1, 1)
                    if c % 2:
                        evict(dve, 1 + c // 2)
                dve.wait_ge(gated, 1)
                o = z[:, :, ZO:ZO + 512].rearrange("p t (h d) -> p t h d", h=MH)
                hn_gain = pr("hn").rearrange("p (a b w) -> p a b w", a=1, b=1).to_broadcast([P, TT, MH, MD])
                link(nc.vector.tensor_tensor(o, o, hn_gain, ALU.mult))
                take_columns(dve, link)
                for i in range(5, DB):
                    evict(dve, i)
                dve.wait_ge(y1, KT)

        KSC = float(MD) ** -0.5
        hh = ropf[:, 0:TT * 512].rearrange("p (t w) -> p t w", t=TT)
        hsq = lambda t, h: stat[:, 100 + MH * t + h:101 + MH * t + h]

        def square_head(t, h):
            return nc.scalar.activation(gain[:, 640:640 + MD], hh[:, t, MD * h:MD * h + MD], ACT.Square, accum_out=hsq(t, h))

        def prompt_mlstm(l):
            gb, s_ok, kt, num, c_ok, w_ok, e_ok, p_ok, kw_ok, h_ok, cc_ok = [sem(f"mlp_{n}") for n in
                ("g_rows", "scores", "keys_turned", "numerators", "state", "exponents", "weights", "probs", "keys_weighted",
                 "hidden", "state_copied")]
            Pb = lambda h: hTf[:, 2048 * (h % 2):2048 * (h % 2) + 2048].rearrange("p (s t) -> p s t", s=TP)
            W = lambda u: hTf[:, 4096 + 512 * (u % 2):4608 + 512 * (u % 2)]
            kw = ropf[:, 2560:3072].rearrange("p (s d) -> p s d", s=TP)
            CT = ropf[:, 3268:3268 + MH * 129].rearrange("p (h v) -> p h v", h=MH)
            one = cs("one")
            block = new_stage()
            @block.tensor
            def _(pe):
                def gate_rows(h):
                    nc.tensor.matmul(ps[:, h % 2, :], ident[0:MH, h:h + 1].to_broadcast([MH, P]), grow[:, 0:SEQ],
                                     start=True, stop=True).then_inc(gb, 1)

                def scores(h, st):
                    u = TP * h + st
                    if u >= 2:
                        pe.wait_ge(p_ok, u - 1)
                    nc.tensor.matmul(ps[:, 2 + u % 2, st * P:SEQ], qkT[:, MH + h, st * P:st * P + P],
                                     qkT[:, h, st * P:SEQ], start=True, stop=True).then_inc(s_ok, 1)
                gate_rows(0)
                for st in range(TP):
                    scores(0, st)
                for h in range(MH):
                    if h:
                        pe.wait_ge(kw_ok, 2 * h)
                    if h + 1 < MH:
                        gate_rows(h + 1)
                    for st in range(TP):
                        ins = nc.tensor.transpose(ps[:, 4, st * P:st * P + P], qkT[:, MH + h, st * P:st * P + P], ident)
                    ins.then_inc(kt, 1)
                    for t in range(TP):
                        if h + 1 < MH:
                            scores(h + 1, t)
                        u = TP * h + t
                        if t == 0:
                            pe.wait_ge(p_ok, TP * h + TP)
                        if u >= 2:
                            pe.wait_ge(h_ok, u - 1)
                        o = ps[:, 5 + u % 2, 0:129]
                        for st in range(t + 1):
                            nc.tensor.matmul(o[:, 0:128], Pb(h)[:, st, t * P:t * P + P],
                                             z[:, st, ZV + MD * h:ZV + MD * h + MD], start=(st == 0), stop=(st == t))
                        for st in range(t + 1):
                            ins = nc.tensor.matmul(o[:, 128:129], Pb(h)[:, st, t * P:t * P + P], one,
                                                   start=(st == 0), stop=(st == t))
                        ins.then_inc(num, 1)
                    pe.wait_ge(kw_ok, 2 * h + 2)
                    if h:
                        pe.wait_ge(cc_ok, h)
                    for st in range(TP):
                        nc.tensor.matmul(ps[:, 7, 0:128], kw[:, st, :], z[:, st, ZV + MD * h:ZV + MD * h + MD],
                                         start=(st == 0), stop=(st == TP - 1))
                    for st in range(TP):
                        ins = nc.tensor.matmul(ps[:, 7, 128:129], kw[:, st, :], one, start=(st == 0), stop=(st == TP - 1))
                    ins.then_inc(c_ok, 1)

            @block.scalar
            def _(act):
                link = act_chain(act)

                def exponent(h, st):
                    act.wait_ge(w_ok, 5 * h + st + 1)
                    w = W(TP * h + st)[:, st * P:SEQ]
                    nc.scalar.activation(w, w, ACT.Exp, scale=-1.0).then_inc(e_ok, 1)

                def state_weights(h):
                    act.wait_ge(w_ok, 5 * h + 5)
                    nc.scalar.activation(wpcol[:, h, :], wpcol[:, h, :], ACT.Exp).then_inc(e_ok, 1)

                def square(h, t):
                    act.wait_ge(h_ok, TP * h + t + 1)
                    link(square_head(t, h))
                for st in range(TP):
                    exponent(0, st)
                state_weights(0)
                for h in range(MH):
                    if h + 1 < MH:
                        exponent(h + 1, 0)
                        exponent(h + 1, 1)
                    for t in range(TP):
                        square(h, t)
                        if h + 1 < MH and t + 2 < TP:
                            exponent(h + 1, t + 2)
                    if h + 1 < MH:
                        state_weights(h + 1)
                act.wait_ge(cc_ok, MH)
                act.dma_start(dout["cT_p"][bass.ds(l, 1)].rearrange("a p h v -> (a p) h v"), CT).then_inc(ctp_st, 16)

            @block.vector
            def _(dve):
                link = dve_chain(dve)
                tri = cs("tri")

                def weights(h, st):
                    if st == 0:
                        dve.wait_ge(gb, h + 1)
                    nc.vector.tensor_scalar(W(TP * h + st)[:, st * P:SEQ], ps[:, h % 2, st * P:SEQ], gcol[:, st, h:h + 1],
                                            0.0, ALU.subtract, ALU.max).then_inc(w_ok, 1)

                def probabilities(h, st):
                    u = TP * h + st
                    dve.wait_ge(e_ok, 5 * h + st + 1)
                    dve.wait_ge(s_ok, u + 1)
                    pb = Pb(h)[:, st, st * P:SEQ]
                    link(nc.vector.scalar_tensor_tensor(out=pb, in0=ps[:, 2 + u % 2, st * P:SEQ], scalar=KSC,
                                                        in1=W(u)[:, st * P:SEQ], op0=ALU.mult, op1=ALU.mult))
                    d = Pb(h)[:, st, st * P:st * P + P]
                    nc.vector.tensor_tensor(d, d, tri, ALU.mult).then_inc(p_ok, 1)
                    if st + 2 < TP:
                        weights(h, st + 2)
                weights(0, 0)
                weights(0, 1)
                for st in range(TP):
                    probabilities(0, st)
                for h in range(MH):
                    nc.vector.tensor_scalar(wpcol[:, h, :], gcol[:, 0:TP, h], ps[:, h % 2, SEQ - 1:SEQ], None,
                                            ALU.subtract).then_inc(w_ok, 1)
                    if h + 1 < MH:
                        weights(h + 1, 0)
                        weights(h + 1, 1)
                    dve.wait_ge(e_ok, 5 * h + 5)
                    dve.wait_ge(kt, h + 1)
                    if h:
                        dve.wait_ge(c_ok, h)
                    for st in range(TP):
                        ins = nc.vector.tensor_scalar(kw[:, st, :], ps[:, 4, st * P:st * P + P], wpcol[:, h, st:st + 1],
                                                      KSC, ALU.mult, ALU.mult)
                        link(ins) if st < TP - 2 else ins.then_inc(kw_ok, 1)
                    for t in range(TP):
                        if h + 1 < MH:
                            probabilities(h + 1, t)
                        dve.wait_ge(num, TP * h + t + 1)
                        o = ps[:, 5 + (TP * h + t) % 2, 0:129]
                        link(nc.vector.tensor_scalar(stat[:, 0:1], o[:, 128:129], -1.0, emcol[:, t, h:h + 1],
                                                     ALU.mult, ALU.max))
                        link(nc.vector.tensor_scalar(stat[:, 0:1], o[:, 128:129], stat[:, 0:1], None, ALU.max))
                        link(nc.vector.reciprocal(stat[:, 1:2], stat[:, 0:1]))
                        nc.vector.tensor_scalar(hh[:, t, MD * h:MD * h + MD], o[:, 0:128], stat[:, 1:2], None,
                                                ALU.mult).then_inc(h_ok, 1)
                    dve.wait_ge(c_ok, h + 1)
                    nc.vector.tensor_copy(CT[:, h, :], ps[:, 7, 0:129]).then_inc(cc_ok, 1)

        def sample_mlstm(l):
            gb, kt, it, ia, cu, nu, dv, ex, cs_st = [sem(f"mls_{n}") for n in
                ("g_rows", "keys_turned", "from_state", "from_chunk", "updates", "n_update", "to_pe", "exp",
                 "c_done")]
            C = slot("cst").rearrange("p (h b v) -> p h b v", h=MH, b=DB)
            kw, pT, tmp, decB, qm = (ropf[0:NS, 2592:2720], ropf[0:NS, 2720:2752], ropf[0:NS, 2752:2881],
                                     ropf[:, 2884:2916].rearrange("p (h b) -> p h b", h=MH),
                                     hTf[:, 0:1024].rearrange("p (h b t) -> p h b t", h=MH, b=DB))
            vm = hTf[0:NS, 1024:2048].rearrange("p (b d) -> p b d", b=DB)
            W = hTf[0:NS, 2048:2080]
            read_at["cst"] = (cts_st, 16 * CTS_STORES)
            one, oh, ms = cs("one", NS), cs("ohb", NS), cs("ms", NS)
            block = new_stage()

            @block.tensor
            def _(pe):
                arrived(pe, "cst")
                pe.wait_ge(n_ld, 16)
                pe.wait_ge(dv, 1)
                v = z[0:NS, TP, :]
                for h in range(MH):
                    vh = v[:, ZV + MD * h:ZV + MD * h + MD]
                    nc.tensor.matmul(ps[0:NS, 1, 32:64], ident[0:MH, h:h + 1].to_broadcast([MH, NS]), grow[:, SEQ:TOK],
                                     start=True, stop=True)
                    nc.tensor.matmul(ps[:, 1, 64:72], ident[0:MH, h:h + 1].to_broadcast([MH, P]), decay,
                                     start=True, stop=True)
                    nc.tensor.matmul(ps[0:NS, 1, 0:32], qkT[:, MH + h, SEQ:TOK], qkT[:, h, SEQ:TOK],
                                     start=True, stop=True).then_inc(gb, 1)
                    nc.tensor.transpose(ps[0:NS, 2, 0:128], qkT[:, MH + h, SEQ:TOK], ident).then_inc(kt, 1)
                    for b in range(DB):
                        nc.tensor.matmul(ps[0:NS, (0, 4)[h % 2], 0:128], qm[:, h, b, :], C[:, h, b, :], start=(b == 0), stop=(b == DB - 1))
                    for b in range(DB):
                        ins = nc.tensor.matmul(ps[0:NS, (0, 4)[h % 2], 128:129], qm[:, h, b, :], nT[:, h, b:b + 1],
                                               start=(b == 0), stop=(b == DB - 1))
                    ins.then_inc(it, 1)
                    pe.wait_ge(dv, 3 * h + 2)
                    nc.tensor.matmul(ps[0:NS, 3, 0:128], pT, vh, start=True, stop=True)
                    nc.tensor.matmul(ps[0:NS, 3, 128:129], pT, one, start=True, stop=True).then_inc(ia, 1)
                    pe.wait_ge(dv, 3 * h + 3)
                    for q in range(2):
                        ins = nc.tensor.matmul(ps[:, 5 + q, :], kw, hTf[0:NS, 1024 + 512 * q:1536 + 512 * q],
                                               start=True, stop=True)
                    ins.then_inc(cu, 1)
                    nc.tensor.matmul(ps[:, 7, 0:DB], kw, oh, start=True, stop=True).then_inc(nu, 1)

            @block.scalar
            def _(act):
                def store(h):
                    act.wait_ge(cs_st, h + 1)
                    w = DB * MD
                    act.dma_start(dout["cT_s"][bass.ds(l, 1), :, h * w:h * w + w].rearrange("a p w -> (a p) w"),
                                  slot("cst")[:, h * w:h * w + w]).then_inc(cts_st, 16)
                for h in range(MH):
                    act.wait_ge(ex, 2 * h + 1)
                    nc.scalar.activation(W, W, ACT.Exp, scale=-1.0).then_inc(ex, 1)
                    if h:
                        store(h - 1)
                store(MH - 1)
                act.dma_start(dout["nT"][bass.ds(l, 1)].rearrange("a p (h b) -> (a p) h b", h=MH), nT).then_inc(cts_st, 16)

            @block.vector
            def _(dve):
                link = dve_chain(dve)
                dve.wait_ge(n_ld, 16)
                arrived(dve, "cst")
                link(nc.vector.memset(qm, 0.0))
                for b in range(DB):
                    ins = nc.vector.tensor_copy(qm[:, :, b, 4 * b:4 * b + 4], qkT[:, 0:MH, SEQ + 4 * b:SEQ + 4 * b + 4])
                    link(ins) if b < DB - 1 else ins.then_inc(dv, 1)
                for h in range(MH):
                    dve.wait_ge(gb, h + 1)
                    nc.vector.tensor_scalar(W, ps[0:NS, 1, 32:64], gcol[0:NS, TP, h:h + 1], 0.0, ALU.subtract,
                                            ALU.max).then_inc(ex, 1)
                    link(nc.vector.tensor_copy(decB[:, h, :], ps[:, 1, 64:72]))
                    dve.wait_ge(ex, 2 * h + 2)
                    link(nc.vector.scalar_tensor_tensor(out=pT, in0=ps[0:NS, 1, 0:32], scalar=KSC, in1=W,
                                                        op0=ALU.mult, op1=ALU.mult))
                    nc.vector.tensor_tensor(pT, pT, ms, ALU.mult).then_inc(dv, 1)
                    dve.wait_ge(kt, h + 1)
                    link(nc.vector.tensor_scalar(kw, ps[0:NS, 2, 0:128], wscol[:, h:h + 1], KSC, ALU.mult, ALU.mult))
                    nc.vector.tensor_tensor(
                        vm, z[0:NS, TP, ZV + MD * h:ZV + MD * h + MD].rearrange("p (o d) -> p o d", o=1)
                        .to_broadcast([NS, DB, MD]),
                        oh.rearrange("p (b o) -> p b o", o=1).to_broadcast([NS, DB, MD]), ALU.mult).then_inc(dv, 1)
                    dve.wait_ge(it, h + 1)
                    link(nc.vector.tensor_scalar(tmp, ps[0:NS, (0, 4)[h % 2], 0:129], ascol[:, h:h + 1], None, ALU.mult))
                    dve.wait_ge(ia, h + 1)
                    link(nc.vector.tensor_tensor(tmp, ps[0:NS, 3, 0:129], tmp, ALU.add))
                    link(nc.vector.tensor_scalar(stat[0:NS, 0:1], tmp[:, 128:129], -1.0, emcol[0:NS, TP, h:h + 1],
                                                 ALU.mult, ALU.max))
                    link(nc.vector.tensor_scalar(stat[0:NS, 0:1], tmp[:, 128:129], stat[0:NS, 0:1], None, ALU.max))
                    link(nc.vector.reciprocal(stat[0:NS, 1:2], stat[0:NS, 0:1]))
                    if h == 0:
                        link(nc.vector.memset(hh[:, TP, :], 0.0))
                    link(nc.vector.tensor_scalar(hh[0:NS, TP, MD * h:MD * h + MD], tmp[:, 0:128], stat[0:NS, 1:2], None,
                                                 ALU.mult))
                    dve.wait_ge(cu, h + 1)
                    for b in range(DB):
                        link(nc.vector.scalar_tensor_tensor(out=C[:, h, b, :], in0=C[:, h, b, :],
                                                            scalar=decB[:, h, b:b + 1],
                                                            in1=ps[:, 5 + b // 4, (b % 4) * P:(b % 4) * P + P],
                                                            op0=ALU.mult, op1=ALU.add))
                    dve.wait_ge(nu, h + 1)
                    link(nc.vector.tensor_tensor(nT[:, h, :], nT[:, h, :], decB[:, h, :], ALU.mult))
                    link(nc.vector.tensor_tensor(nT[:, h, :], ps[:, 7, 0:DB], nT[:, h, :], ALU.add))
                    nc.vector.tensor_copy(stat[0:1, 2:3], stat[0:1, 1:2]).then_inc(dv, 1)
                    dve.wait_ge(dv, 3 * h + 4)
                    nc.vector.tensor_copy(stat[0:1, 3:4], stat[0:1, 2:3]).then_inc(cs_st, 1)

        def finish_mlstm(l):
            last, go, root = sem("mfin_last_squares"), sem("mfin_means"), sem("mfin_root")
            block = new_stage()


            @block.scalar
            def _(act):
                link = act_chain(act)
                for h in range(MH):
                    ins = square_head(TP, h)
                    link(ins) if h < MH - 1 else ins.then_inc(last, 1)
                act.wait_ge(go, 1)
                nc.scalar.activation(stat[:, 20:40], stat[:, 0:20], ACT.Sqrt).then_inc(root, 1)

            @block.vector
            def _(dve):
                link = dve_chain(dve)
                dve.wait_ge(last, 1)
                nc.vector.tensor_scalar(stat[:, 0:20], stat[:, 100:120], 1.0 / MD, EPS, ALU.mult, ALU.add).then_inc(go, 1)
                dve.wait_ge(root, 1)
                link(nc.vector.reciprocal(stat[:, 40:60], stat[:, 20:40]))
                for t in range(TT):
                    for h in range(MH):
                        o = z[:, t, ZO + MD * h:ZO + MD * h + MD]
                        nc.vector.scalar_tensor_tensor(
                            out=o, in0=hh[:, t, MD * h:MD * h + MD], scalar=stat[:, 40 + MH * t + h:41 + MH * t + h],
                            in1=o, op0=ALU.mult, op1=ALU.mult)

        kselT, kwinT = ropf[:, 0:TOK], ropf[:, TOK:2 * TOK]
        qT = ropf[:, 2 * TOK:2 * TOK + HG * TOK].rearrange("p (h t) -> p h t", h=HG)
        xp = qkf[:, 0:SEQ // 2 * 4]
        kc_p = qkf[:, 1024:1024 + NC_P]
        vc_p = qkf[0:NC_P, 1056:1056 + P]
        QSC = float(HD) ** -0.5

        def prep_stage(l):
            tp, ea, ed = sem("prep_turned"), sem("prep_copied_a"), sem("prep_copied_d")
            pairs = xp.rearrange("p (q k g) -> p k g q", k=2, g=G)
            bank = lambda t, i: 3 * (t % 2) + i
            block = new_stage()

            def rows_out(t, k, dst, src, copy):
                if t < TP:
                    for g in range(G):
                        for par in range(2):
                            copy(pairs[64 * par:64 * par + 64, k, g, 64 * t:64 * t + 64],
                                 src[64 * g:64 * g + 64, par:par + 127:2])
                w = P if t < TP else NS
                return dst[:, t * P:t * P + w], src[:, P:P + w]

            @block.tensor
            def _(pe):
                for t in range(TT):
                    if t >= 2:
                        pe.wait_ge(ea, t - 1)
                        pe.wait_ge(ed, t - 1)
                    for hg in range(HG):
                        nc.tensor.transpose(ps[:, bank(t, 0), hg * P:hg * P + P], z[:, t, ZQ + hg * P:ZQ + hg * P + P], ident)
                    for i, (c, c2) in enumerate(((ZK, ZK + 256), (ZK + 128, ZK + 512))):
                        if t < TP:
                            nc.tensor.transpose(ps[:, bank(t, 1 + i), 0:P], z[:, t, c:c + P], ident)
                        ins = nc.tensor.transpose(ps[:, bank(t, 1 + i), P:2 * P], z[:, t, c2:c2 + P], ident)
                    ins.then_inc(tp, 1)

            @block.scalar
            def _(act):
                load_gain(act, l, 2)
                link = act_chain(act)
                for t in range(TT):
                    w = P if t < TP else NS
                    act.wait_ge(tp, t + 1)
                    link(nc.scalar.activation(qT[:, :, t * P:t * P + w],
                                              ps[:, bank(t, 0), :].rearrange("p (h t) -> p h t", h=HG)[:, :, 0:w],
                                              ACT.Copy, scale=QSC))
                    o, i = rows_out(t, 1, kwinT, ps[:, bank(t, 2), :], lambda o, i: link(nc.scalar.copy(o, i)))
                    nc.scalar.copy(o, i).then_inc(ea, 1)

            @block.vector
            def _(dve):
                link = dve_chain(dve)
                for t in range(TT):
                    dve.wait_ge(tp, t + 1)
                    o, i = rows_out(t, 0, kselT, ps[:, bank(t, 1), :], lambda o, i: link(nc.vector.tensor_copy(o, i)))
                    nc.vector.tensor_copy(o, i).then_inc(ed, 1)

        def prompt_compress(l):
            tensor_program, hidden, _, evict = compression("pcmp", [
                (None, xp.rearrange("p (q w) -> p q w", w=4), NC_P, kc_p, vc_p)], False)
            block = new_stage()


            @block.tensor
            def _(pe):
                tensor_program(pe)

            @block.scalar
            def _(act):
                hidden(act, 0)

            @block.vector
            def _(dve):
                evict(dve, 0)

        def tile_attention(stage, l, per_pair, units, outs, adds):
            s_ok, mx, e_ok, scaled, pt, ptc, o_ok, o_used = [sem(f"{stage}_{n}") for n in
                ("scores", "maxima", "exponentials", "probs_scaled", "probs_turned", "probs_copied", "outputs", "outputs_read")]
            Pb = lambda u: hTf[:, 512 * (u % 6):512 * (u % 6) + 512]
            PT = lambda u: hTf[:, 3072 + 512 * (u % 4):3584 + 512 * (u % 4)]
            st = lambda u, c: stat[:, 8 * (u % 8) + c:8 * (u % 8) + c + 1]
            causal = cs("causal")
            N = len(units)
            block = new_stage()


            @block.tensor
            def _(pe):
                def scores(u):
                    q, k, n = units[u][0:3]
                    if u >= 3:
                        pe.wait_ge(e_ok, u - 2)
                    nc.tensor.matmul(ps[:, u % 3, 0:n], q, k, start=True, stop=True).then_inc(s_ok, 1)

                def turn(u):
                    n = units[u][2]
                    pe.wait_ge(scaled, u + 1)
                    if u >= 3:
                        pe.wait_ge(ptc, u - 2)
                    for i in range(n // P):
                        ins = nc.tensor.transpose(ps[:, 3 + u % 3, i * P:i * P + P], Pb(u)[:, i * P:i * P + P], ident)
                    ins.then_inc(pt, 1)

                def values(u):
                    pe.wait_ge(ptc, u + 2)
                    pair, first_, last = u // per_pair, u % per_pair == 0, u % per_pair == per_pair - 2
                    if first_ and pair >= 2:
                        pe.wait_ge(o_used, pair - 1)
                    tiles = units[u][2] // P
                    for i in range(tiles):
                        for g in range(2):
                            ins = nc.tensor.matmul(ps[64 * g:64 * g + 64, 6 + pair % 2, 0:P], units[u + g][4][i],
                                                   PT(u + g)[:, i * P:i * P + P], start=(first_ and i == 0),
                                                   stop=(last and i == tiles - 1))
                    ins.then_inc(o_ok, 1)
                for u in range(N + 8):
                    if u < N and u % 2 == 0:
                        scores(u)
                        scores(u + 1)
                    if 4 <= u < N + 4:
                        turn(u - 4)
                    if u >= 8 and u % 2 == 0:
                        values(u - 8)

            @block.scalar
            def _(act):
                def copied(u):
                    act.wait_ge(pt, u + 1)
                    n = units[u][2]
                    if u >= 4:
                        act.wait_ge(o_ok, (u - 4) // 2 + 1)
                    nc.scalar.copy(PT(u)[:, 0:n], ps[:, 3 + u % 3, 0:n]).then_inc(ptc, 1)
                for u in range(N + 5):
                    if u < N:
                        n = units[u][2]
                        act.wait_ge(mx, u + 1)
                        if u >= 6:
                            act.wait_ge(pt, u - 5)
                        nc.scalar.activation(Pb(u)[:, 0:n], ps[:, u % 3, 0:n], ACT.Exp, bias=st(u, 0),
                                             accum_out=st(u, 1)).then_inc(e_ok, 1)
                    if u >= 5:
                        copied(u - 5)

            @block.vector
            def _(dve):
                link = dve_chain(dve)

                def scale(u):
                    n, gate = units[u][2], units[u][5]
                    dve.wait_ge(e_ok, u + 1)
                    link(nc.vector.reciprocal(st(u, 2), st(u, 1)))
                    f, p = st(u, 2), Pb(u)[:, 0:n]
                    if gate is None:
                        nc.vector.tensor_scalar(p, p, f, None, ALU.mult).then_inc(scaled, 1)
                    else:
                        nc.vector.tensor_scalar(p, p, f, gate, ALU.mult, ALU.mult).then_inc(scaled, 1)

                def output(pair):
                    dve.wait_ge(o_ok, (pair + 1) * per_pair // 2)
                    src, out = ps[:, 6 + pair % 2, 0:P], outs[pair]
                    if adds:
                        nc.vector.tensor_tensor(out, src, out, ALU.add).then_inc(o_used, 1)
                    else:
                        nc.vector.tensor_copy(out, src).then_inc(o_used, 1)
                for u in range(N + 9):
                    if u < N:
                        n, diag = units[u][2], units[u][3]
                        dve.wait_ge(s_ok, u + 1)
                        if diag:
                            link(nc.vector.tensor_tensor(ps[:, u % 3, n - P:n], ps[:, u % 3, n - P:n], causal, ALU.add))
                        nc.vector.tensor_reduce(st(u, 0), ps[:, u % 3, 0:n], AX.X, ALU.max, negate=True).then_inc(mx, 1)
                    if 2 <= u < N + 2:
                        scale(u - 2)
                    if u >= 9 and (u - 8) % per_pair == per_pair - 1:
                        output((u - 9) // per_pair)

        def prompt_attention(l):
            s_ok, shifted, r_ok, e_ok, pt, ptc, o_ok, o_used = [sem(f"pc_{n}") for n in
                ("scores", "scores_shifted", "rows", "exponentials", "turned", "copied", "outputs", "outputs_read")]
            n = NC_P
            E = lambda t: hTf[:, 512 * (t % 2):512 * (t % 2) + HEADS * n].rearrange("p (h c) -> p h c", h=HEADS)
            eT = hTf[0:n, 1024:2048].rearrange("p (h t) -> p h t", h=HEADS)
            zg = z[:, :, ZG:ZG + 24].rearrange("p t (h r) -> p t h r", r=3)
            bank = lambda t, g: (0, 4, 5, 6)[2 * (t % 2) + g]
            block = new_stage()


            @block.tensor
            def _(pe):
                def scores(t):
                    for h in range(HEADS):
                        g, hg = h % G, h // G
                        ins = nc.tensor.matmul(ps[:, bank(t, g), n * hg:n * hg + n],
                                               qT[64 * g:64 * g + 64, hg, t * P:t * P + P],
                                               kc_p[64 * g:64 * g + 64, :], start=True, stop=True)
                    ins.then_inc(s_ok, 1)
                scores(0)
                scores(1)
                for t in range(TP):
                    pe.wait_ge(r_ok, t + 1)
                    for h in range(HEADS):
                        ins = nc.tensor.transpose(ps[0:n, 1 + h // 4, (h % 4) * P:(h % 4) * P + P], E(t)[:, h, :], ident)
                    ins.then_inc(pt, 1)
                    if t + 2 < TP:
                        scores(t + 2)
                    pe.wait_ge(ptc, t + 1)
                    if t:
                        pe.wait_ge(o_used, t)
                    for h in range(HEADS):
                        g, hg = h % G, h // G
                        ins = nc.tensor.matmul(ps[64 * g:64 * g + 64, 3, P * hg:P * hg + P], vc_p[:, 64 * g:64 * g + 64],
                                               eT[:, h, :], start=True, stop=True)
                    ins.then_inc(o_ok, 1)

            @block.scalar
            def _(act):
                for t in range(TP):
                    act.wait_ge(shifted, t + 1)
                    nc.scalar.activation(E(t), E(t), ACT.Exp).then_inc(e_ok, 1)

            @block.vector
            def _(dve):
                link = dve_chain(dve)
                bc = lambda a: a.rearrange("p (h o) -> p h o", o=1).to_broadcast([P, HEADS, n])

                def shift(t):
                    e, top_ = E(t), stat[:, 32 * (t % 2):32 * (t % 2) + 8]
                    dve.wait_ge(s_ok, t + 1)
                    ma = cs("cma")[:, n * t:n * t + n].rearrange("p (o c) -> p o c", o=1).to_broadcast([P, HG, n])
                    for g in range(G):
                        src = ps[:, bank(t, g), 0:HG * n].rearrange("p (h c) -> p h c", h=HG)
                        link(nc.vector.tensor_tensor(e[:, g:HEADS:G, :], src, ma, ALU.add))
                    link(nc.vector.tensor_reduce(top_, e, AX.X, ALU.max))
                    nc.vector.tensor_tensor(e, e, bc(top_), ALU.subtract).then_inc(shifted, 1)

                def gated_rows(t):
                    e, st = E(t), lambda i: stat[:, 32 * (t % 2) + 8 * i:32 * (t % 2) + 8 * i + 8]
                    mm = cs("cmm")[:, n * t:n * t + n].rearrange("p (o c) -> p o c", o=1).to_broadcast([P, HEADS, n])
                    dve.wait_ge(e_ok, t + 1)
                    link(nc.vector.tensor_tensor(e, e, mm, ALU.mult))
                    link(nc.vector.tensor_reduce(st(1), e, AX.X, ALU.add))
                    link(nc.vector.tensor_scalar(st(1), st(1), 1e-30, None, ALU.max))
                    link(nc.vector.reciprocal(st(2), st(1)))
                    link(nc.vector.tensor_tensor(st(3), st(2), zg[:, t, :, 0], ALU.mult))
                    nc.vector.tensor_tensor(e, e, bc(st(3)), ALU.mult).then_inc(r_ok, 1)

                def output(t):
                    dve.wait_ge(o_ok, t + 1)
                    nc.vector.tensor_copy(z[:, t, ZQ:ZQ + 512], ps[:, 3, :]).then_inc(o_used, 1)
                shift(0)
                for t in range(TP):
                    gated_rows(t)
                    if t + 1 < TP:
                        shift(t + 1)
                    if t:
                        output(t - 1)
                    dve.wait_ge(pt, t + 1)
                    link(nc.vector.tensor_copy(eT[:, 0:4, :], ps[0:n, 1, :].rearrange("p (h t) -> p h t", h=4)))
                    nc.vector.tensor_copy(eT[:, 4:8, :], ps[0:n, 2, :].rearrange("p (h t) -> p h t", h=4)).then_inc(ptc, 1)
                output(TP - 1)
            units, outs = [], []
            for t in range(TP):
                for hg in range(HG):
                    outs.append(z[:, t, ZQ + P * hg:ZQ + P * hg + P])
                    for r, kT in ((1, kselT), (2, kwinT)):
                        for g in range(G):
                            vc = ZK + 256 * r + 128 + 64 * g
                            units.append((qT[64 * g:64 * g + 64, hg, t * P:t * P + P], kT[64 * g:64 * g + 64, 0:t * P + P],
                                          t * P + P, True, [z[:, i, vc:vc + 64] for i in range(t + 1)],
                                          zg[:, t, G * hg + g, r:r + 1]))
            tile_attention("att2", l, 4, units, outs, True)

        s_sel, s_win, s_cmp = qkf[:, 0:PAST + NS], qkf[:, 2080:2080 + WIN + NS], qkf[:, 2624:2752]
        imp, rep, top, impc = qkf[:, 2752:2785], qkf[:, 2786:2819], qkf[:, 2820:2828], qkf[:, 2828:2956]
        oT = qkf[:, 3000:3384].rearrange("p (r h t) -> p r h t", r=3, h=HG)
        qblk = qkf[:, 3400:3656].rearrange("p (b r) -> p b r", b=DB)
        pT = hTf[:, 0:23 * P].rearrange("p (i r) -> p i r", i=23)

        def sample_attention(l, hb):
            stage = f"samp{hb}"
            q_ok, sc, sw, ss, cp, pc_ok, im, im_used, mx, ex, kt, ka, kd, pt, ca, cd, wv, ov, ob, ot = [
                sem(f"{stage}_{n}") for n in
                ("queries", "cmp_scores", "win_scores", "sel_scores", "scores_copied", "cmp_probs", "importance",
                 "importance_read", "maxima", "exponentials", "keys_turned", "keys_copied_a",
                 "keys_copied_d", "turned", "copied_a", "copied_d", "win_outputs", "outputs",
                 "outputs_copied", "outputs_turned")]
            kl, vl = [f"k{2 * hb + i}" for i in range(2)], [f"v{2 * hb + i}" for i in range(2)]
            wl = f"win{hb}"
            read_at.update({kl[i]: (kt, 14 + 2 * i) for i in range(2)})
            read_at.update({vl[i]: (ov, i + 1) for i in range(2)})
            read_at[wl] = (wv, 1)
            kT = lambda u: hTf[:, 3072 + 512 * (u % 2):3584 + 512 * (u % 2)]
            orow = hTf[:, 4096:4096 + 3 * P]
            UNITS = 16
            tiles = [(s_cmp[:, 0:NC_S], NC_S)] + [(s_win[:, i * P:i * P + P], P) for i in range(4)] + [(s_win[:, WIN:], NS)]
            tiles += [(s_sel[:, i * P:i * P + P], P) for i in range(16)] + [(s_sel[:, PAST:], NS)]
            block = new_stage()

            @block.tensor
            def _(pe):
                pe.wait_ge(q_ok, 1)
                for b4 in range(4):
                    b = 4 * hb + b4
                    r = slice(32 * b4, 32 * b4 + 32)
                    q = qblk[:, b, :]
                    nc.tensor.matmul(ps[r, 0, 0:NC_S], q, kc_s[:, b, 0:NC_S], start=True, stop=True)
                    nc.tensor.matmul(ps[r, 0, 128:160], q, kwinT[:, SEQ:TOK], start=True, stop=True)
                    ins = nc.tensor.matmul(ps[r, 0, 160:192], q, kselT[:, SEQ:TOK], start=True, stop=True)
                ins.then_inc(sc, 1)

                def turn_keys(u):
                    b4, c = u % 4, u // 4
                    load = kl[b4 // 2]
                    if u in (0, 2):
                        arrived(pe, load)
                    if u >= 2:
                        pe.wait_ge((ka, kd)[u % 2], u // 2)
                    keys = slot(load).rearrange("p (b j c) -> p b j c", b=2, j=16)
                    for j in range(4):
                        ins = nc.tensor.transpose(ps[:, 6 + u % 2, j * P:j * P + P], keys[:, b4 % 2, 4 * c + j, :], ident)
                    ins.then_inc(kt, 1)

                def key_scores(u):
                    b4, c = u % 4, u // 4
                    pe.wait_ge((ka, kd)[u % 2], u // 2 + 1)
                    nc.tensor.matmul(ps[32 * b4:32 * b4 + 32, 2 + c, :], qblk[:, 4 * hb + b4, :], kT(u),
                                     start=True, stop=True).then_inc(ss, 1)
                turn_keys(0)
                for u in range(UNITS):
                    if u + 1 < UNITS:
                        turn_keys(u + 1)
                    key_scores(u)
                    if u == 4:
                        pe.wait_ge(pc_ok, 1)
                        pe.wait_ge(cp, 1)
                        nc.tensor.matmul(ps[:, 0, 256:256 + NC_S], cs("grp"), s_cmp[:, 0:NC_S], start=True,
                                         stop=True).then_inc(im, 1)
                    if u == 12:
                        arrived(pe, wl)
                        for b4 in range(4):
                            ins = nc.tensor.matmul(ps[32 * b4:32 * b4 + 32, 1, :], qblk[:, 4 * hb + b4, :],
                                                   slot(wl)[:, 512 * b4:512 * b4 + 512], start=True, stop=True)
                        ins.then_inc(sw, 1)
                for i, (src, n) in enumerate(tiles):
                    if i == 1:
                        pe.wait_ge(ex, 2)
                    if i == 6:
                        pe.wait_ge(ex, 3)
                    if i % 4 == 0:
                        if i == 0:
                            pe.wait_ge(im_used, 1)
                        if i >= 8:
                            pe.wait_ge(ca if (i // 4) % 2 == 0 else cd, (i // 4 - 2) // 2 + 1)
                    ins = nc.tensor.transpose(ps[0:n, (0, 6)[i // 4 % 2], (i % 4) * P:(i % 4) * P + P], src, ident)
                    if i % 4 == 3 or i == 22:
                        ins.then_inc(pt, 1)
                pe.wait_ge(ca, 3)
                pe.wait_ge(cd, 3)
                win_v = slot(wl)[:, 2048:4096].rearrange("p (b t c) -> p b t c", b=4, t=4)
                rows = [slice(32 * b4, 32 * b4 + 32) for b4 in range(4)]
                C_AT, W_AT, S_AT = (slice(a, a + P) for a in (0, 128, 256))
                for b4 in range(4):
                    nc.tensor.matmul(ps[rows[b4], 7, C_AT], pT[0:NC_S, 0, rows[b4]], vc_s[0:NC_S, 4 * hb + b4, :],
                                     start=True, stop=True)
                for i in range(4):
                    for b4 in range(4):
                        nc.tensor.matmul(ps[rows[b4], 7, W_AT], pT[:, 1 + i, rows[b4]], win_v[:, b4, i, :],
                                         start=(i == 0), stop=False)
                for b4 in range(4):
                    ins = nc.tensor.matmul(ps[rows[b4], 7, W_AT], pT[0:NS, 5, rows[b4]], z[0:NS, TP, ZK + 640:ZK + 768],
                                           start=False, stop=True)
                ins.then_inc(wv, 1)
                for j in range(2):
                    arrived(pe, vl[j])
                    vals = slot(vl[j]).rearrange("p (b i c) -> p b i c", b=2, i=NPG)
                    for i in range(NPG + 1):
                        for b4 in range(2 * j, 2 * j + 2):
                            o = ps[rows[b4], 7, S_AT]
                            if i == 0:
                                nc.tensor.matmul(o, pT[0:NS, 22, rows[b4]], z[0:NS, TP, ZK + 384:ZK + 512],
                                                 start=True, stop=False)
                            else:
                                ins = nc.tensor.matmul(o, pT[:, 5 + i, rows[b4]], vals[:, b4 % 2, i - 1, :],
                                                       start=False, stop=(i == NPG))
                    ins.then_inc(ov, 1)
                pe.wait_ge(ob, 1)
                for i in range(3):
                    ins = nc.tensor.transpose(ps[:, 6, i * P:i * P + P], orow[:, i * P:i * P + P], ident)
                ins.then_inc(ot, 1)

            @block.scalar
            def _(act):
                link = act_chain(act)
                def exponentials(i):
                    s, a = ((s_cmp[:, 0:NC_S], 0), (s_win, 4), (s_sel, 8))[i]
                    act.wait_ge(mx, i + 1)
                    nc.scalar.activation(s, s, ACT.Exp, bias=stat[:, a:a + 1], accum_out=stat[:, a + 1:a + 2]).then_inc(ex, 1)
                exponentials(0)
                for u in range(0, UNITS, 2):
                    act.wait_ge(kt, u + 1)
                    nc.scalar.copy(kT(u), ps[:, 6, :]).then_inc(ka, 1)
                exponentials(1)
                exponentials(2)
                for q in (0, 2, 4):
                    act.wait_ge(pt, q + 1)
                    if q == 0:
                        link(nc.scalar.copy(pT[0:NC_S, 0, :], ps[0:NC_S, 0, 0:P]))
                        ins = nc.scalar.copy(pT[:, 1:4, :], ps[:, 0, P:512].rearrange("p (i r) -> p i r", i=3))
                    else:
                        ins = nc.scalar.copy(pT[:, 4 * q:4 * q + 4, :], ps[:, 0, :].rearrange("p (i r) -> p i r", i=4))
                    ins.then_inc(ca, 1)

            @block.vector
            def _(dve):
                link = dve_chain(dve)
                if hb == 0:
                    link(nc.vector.memset(qblk, 0.0))
                    for g in range(G):
                        for hg in range(HG):
                            p = slice(64 * g, 64 * g + 64)
                            c = 16 * g + 4 * hg
                            link(nc.vector.tensor_copy(qblk[p, :, c:c + 4],
                                                       qT[p, hg, SEQ:TOK].rearrange("p (b t) -> p b t", b=DB)))
                nc.vector.memset(impc[:, 127:128], 0.0).then_inc(q_ok, 1)
                dve.wait_ge(q_ok, 1)
                new = cs("new")[:, 32 * hb:32 * hb + 32]
                dve.wait_ge(sc, 1)
                link(nc.vector.tensor_copy(s_cmp[:, 0:NC_S], ps[:, 0, 0:NC_S]))
                link(nc.vector.tensor_reduce(stat[:, 0:1], s_cmp[:, 0:NC_S], AX.X, ALU.max, negate=True))
                link(nc.vector.tensor_tensor(s_win[:, WIN:], ps[:, 0, 128:160], new, ALU.add))
                link(nc.vector.tensor_tensor(s_sel[:, PAST:], ps[:, 0, 160:192], new, ALU.add))
                nc.vector.tensor_copy(stat[:, 2:3], stat[:, 0:1]).then_inc(cp, 1)
                dve.wait_ge(cp, 1)
                nc.vector.tensor_copy(stat[:, 3:4], stat[:, 2:3]).then_inc(mx, 1)

                def copy_keys(u):
                    dve.wait_ge(kt, u + 1)
                    nc.vector.tensor_copy(kT(u), ps[:, 7, :]).then_inc(kd, 1)
                copy_keys(1)
                dve.wait_ge(ex, 1)
                link(nc.vector.reciprocal(stat[:, 2:3], stat[:, 1:2]))
                nc.vector.tensor_scalar(s_cmp[:, 0:NC_S], s_cmp[:, 0:NC_S], stat[:, 2:3], None, ALU.mult).then_inc(pc_ok, 1)
                copy_keys(3)
                copy_keys(5)
                dve.wait_ge(im, 1)
                nc.vector.tensor_copy(impc[:, 0:NC_S], ps[:, 0, 256:256 + NC_S]).then_inc(im_used, 1)
                dve.wait_ge(im_used, 1)
                link(nc.vector.tensor_reduce(imp[:, 0:32], impc.rearrange("p (s u) -> p s u", u=4), AX.X, ALU.add))
                link(nc.vector.tensor_tensor(imp[:, 1:32], imp[:, 1:32], impc[:, 3:124:4], ALU.add))
                copy_keys(7)
                link(nc.vector.memset(imp[:, 0:1], BIG))
                link(nc.vector.memset(imp[:, 32:33], BIG))
                link(nc.vector.max(top, imp))
                link(nc.vector.match_replace(rep, top, imp, 3.0 * BIG))
                link(nc.vector.tensor_scalar(rep, rep, 2.0 * BIG, None, ALU.is_ge))
                link(nc.vector.tensor_scalar(rep, rep, -1.0, BIG, ALU.add, ALU.mult))
                per_block = rep[:, 0:32].rearrange("p (o s i) -> p o s i", o=1, i=1).to_broadcast([P, 4, 32, 4])

                def biased_scores(c):
                    dve.wait_ge(ss, 4 * c + 4)
                    quarter = s_sel[:, c * 512:c * 512 + 512]
                    link(nc.vector.tensor_tensor(
                        quarter.rearrange("p (j s i) -> p j s i", j=4, s=32),
                        ps[:, 2 + c, :].rearrange("p (j s i) -> p j s i", j=4, s=32), per_block, ALU.add))
                    link(nc.vector.tensor_reduce(stat[:, 12 + c:13 + c], quarter, AX.X, ALU.max))
                link(nc.vector.tensor_reduce(stat[:, 16:17], s_sel[:, PAST:], AX.X, ALU.max))
                copy_keys(9)
                biased_scores(0)
                copy_keys(11)
                biased_scores(1)
                copy_keys(13)
                dve.wait_ge(sw, 1)
                link(nc.vector.tensor_copy(s_win[:, 4:WIN], ps[:, 1, 4:WIN]))
                link(nc.vector.tensor_tensor(s_win[:, 0:4], ps[:, 1, 0:4], cs("low"), ALU.add))
                nc.vector.tensor_reduce(stat[:, 4:5], s_win, AX.X, ALU.max, negate=True).then_inc(mx, 1)
                biased_scores(2)
                copy_keys(15)
                biased_scores(3)
                nc.vector.tensor_reduce(stat[:, 8:9], stat[:, 12:17], AX.X, ALU.max, negate=True).then_inc(mx, 1)
                for q in (1, 3, 5):
                    dve.wait_ge(pt, q + 1)
                    if q == 1:
                        link(nc.vector.tensor_copy(pT[:, 4, :], ps[:, 6, 0:P]))
                        link(nc.vector.tensor_copy(pT[0:NS, 5, :], ps[0:NS, 6, P:2 * P]))
                        ins = nc.vector.tensor_copy(pT[:, 6:8, :], ps[:, 6, 256:512].rearrange("p (i r) -> p i r", i=2))
                    elif q == 3:
                        ins = nc.vector.tensor_copy(pT[:, 12:16, :], ps[:, 6, :].rearrange("p (i r) -> p i r", i=4))
                    else:
                        link(nc.vector.tensor_copy(pT[:, 20:22, :], ps[:, 6, 0:256].rearrange("p (i r) -> p i r", i=2)))
                        ins = nc.vector.tensor_copy(pT[0:NS, 22, :], ps[0:NS, 6, 256:384])
                    ins.then_inc(cd, 1)
                dve.wait_ge(ov, 2)
                dve.wait_ge(ex, 3)
                link(nc.vector.reciprocal(stat[:, 6:7], stat[:, 5:6]))
                link(nc.vector.reciprocal(stat[:, 10:11], stat[:, 9:10]))
                link(nc.vector.tensor_copy(orow[:, 0:P], ps[:, 7, 0:P]))
                link(nc.vector.tensor_scalar(orow[:, P:2 * P], ps[:, 7, P:2 * P], stat[:, 6:7], None, ALU.mult))
                nc.vector.tensor_scalar(orow[:, 2 * P:3 * P], ps[:, 7, 2 * P:3 * P], stat[:, 10:11], None, ALU.mult).then_inc(ob, 1)
                dve.wait_ge(ot, 1)
                for r, at in enumerate((0, 256, 128)):
                    for g in range(G):
                        p = slice(64 * g, 64 * g + 64)
                        src = ps[p, 6, at:at + P].rearrange("p (b g h t) -> p g h b t", b=4, g=G, h=HG)[:, g]
                        nc.vector.tensor_copy(
                            oT[p, r, :, 16 * hb:16 * hb + 16].rearrange("p h (b t) -> p h b t", b=4), src)

        def sample_merge(l):
            tp = sem("sfin_turned")
            block = new_stage()

            @block.tensor
            def _(pe):
                for r in range(3):
                    for hg in range(HG):
                        ins = nc.tensor.transpose(ps[0:NS, r, hg * P:hg * P + P], oT[:, r, hg, :], ident)
                ins.then_inc(tp, 1)

            @block.vector
            def _(dve):
                link = dve_chain(dve)
                dve.wait_ge(tp, 1)
                zg = z[0:NS, TP, ZG:ZG + 24].rearrange("p (h r) -> p h r", r=3)
                out = z[0:NS, TP, ZQ:ZQ + 512].rearrange("p (h d) -> p h d", h=HEADS)
                tmp = hTf[0:NS, 0:512].rearrange("p (h d) -> p h d", h=HEADS)
                for r in range(3):
                    src = ps[0:NS, r, :].rearrange("p (h d) -> p h d", h=HEADS)
                    gt = zg[:, :, r:r + 1].to_broadcast([NS, HEADS, HD])
                    if r == 0:
                        link(nc.vector.tensor_tensor(out, src, gt, ALU.mult))
                    else:
                        link(nc.vector.tensor_tensor(tmp, src, gt, ALU.mult))
                        link(nc.vector.tensor_tensor(out, out, tmp, ALU.add))

        def turn_stage(stage, l, tiles, srcs, dst, scale=1.0, act_first=None):
            tp = sem(f"{stage}_turned")
            n = len(srcs(0))
            nb = -(-n // 4)
            ev = [sem(f"{stage}_copied_{j}") for j in range(nb)]
            block = new_stage()

            @block.tensor
            def _(pe):
                for t in range(tiles):
                    if t >= 4:
                        for j in range(nb):
                            pe.wait_ge(ev[j], t - 3)
                    for k, src in enumerate(srcs(t)):
                        ins = nc.tensor.transpose(ps[:, 2 * (t % 4) + k // 4, (k % 4) * P:(k % 4) * P + P], src, ident)
                    ins.then_inc(tp, 1)

            def evict(eng, engine_copy, j):
                for t in range(tiles):
                    eng.wait_ge(tp, t + 1)
                    if j < nb:
                        m = min(4, n - 4 * j)
                        engine_copy(dst[:, 4 * j:4 * j + m, t * P:t * P + P],
                                    ps[:, 2 * (t % 4) + j, 0:m * P].rearrange("p (k t) -> p k t", k=m)).then_inc(ev[j], 1)

            @block.scalar
            def _(act):
                if act_first:
                    act_first(act)
                evict(act, nc.scalar.copy, 1)

            @block.vector
            def _(dve):
                evict(dve, lambda o, i: nc.vector.tensor_scalar(o, i, scale, None, ALU.mult), 0)

        A = lambda a, n: arena[:, a:a + n]
        memx = A(TT * ZW, 2048).rearrange("p (t w) -> p t w", t=MT)
        zm = A(2048, 1024).rearrange("p (t w) -> p t w", t=MT)
        kmT = A(3072, 512).rearrange("p (e m) -> p e m", e=2)
        zx = A(3584, 1280).rearrange("p (t w) -> p t w", t=TT)
        qxT = A(4864, 2 * TT * P).rearrange("p (e t) -> p e t", e=2)
        oxT = A(7424, 2 * TT * P).rearrange("p (e t) -> p e t", e=2)
        xsq = A(8704, 1280)
        qxb = A(9984, 512).rearrange("p (e b r) -> p e b r", e=2, b=DB)
        sx, pxT = A(10496, 256), A(10752, 256).rearrange("p (i r) -> p i r", i=2)

        def memory_kv(l):
            wt = slot("wkv").rearrange("p (k n) -> p k n", k=KT)
            norm_gemm_stage("wkv", l, memx, MT, 2, [("wkv" if t == 0 else None,
                                   token_products(t, tile_of(hT, t), KT, lambda k: wt[:, k, :], 512),
                                   "ad"[t], copy_to(zm[:, t, :], 512), "wkv" if t == MT - 1 else None) for t in range(MT)],
                            list(range(MT)))

        def head_norm_stage(stage, l, view, g, scratch, act_first=None):
            go, root = sem(f"{stage}_squares"), sem(f"{stage}_root")
            n = view.shape[1] * view.shape[2]
            block = new_stage()

            @block.scalar
            def _(act):
                if act_first:
                    act_first(act)
                act.wait_ge(go, 1)
                nc.scalar.activation(stat[:, 80:80 + n], stat[:, 0:n], ACT.Sqrt).then_inc(root, 1)

            @block.vector
            def _(dve):
                head_norm(dve_chain(dve), [(view, g, 0, scratch)], n, root, go, HD)

        def store_memory(act, l):
            act.dma_start(dout["mem"][bass.ds(l, 1)].rearrange("a p t c -> (a p) t c"), zm).then_inc(mem_st, 16)

        def cross_samples(l):
            q_ok, s_ok, mx, ex, pn, tp, tc, o_ok, o_used, ob, ot = [sem(f"xs_{n}") for n in
                ("queries", "scores", "maxima", "exponentials", "probs", "turned", "copied", "outputs", "outputs_read",
                 "outputs_copied", "outputs_turned")]
            read_at.update({f"mc{hb}": (o_ok, hb + 1) for hb in range(2)})
            block = new_stage()

            @block.tensor
            def _(pe):
                pe.wait_ge(q_ok, 1)
                for hb in range(2):
                    arrived(pe, f"mc{hb}")
                    kv = slot(f"mc{hb}").rearrange("p (b w) -> p b w", b=4)
                    for b4 in range(4):
                        for e in range(2):
                            ins = nc.tensor.matmul(ps[32 * b4:32 * b4 + 32, 0, 0:MEM], qxb[:, e, 4 * hb + b4, :],
                                                   kv[:, b4, MEM * e:MEM * e + MEM], start=(e == 0), stop=(e == 1))
                    ins.then_inc(s_ok, 1)
                    pe.wait_ge(pn, hb + 1)
                    for i in range(2):
                        ins = nc.tensor.transpose(ps[:, 1, i * P:i * P + P], sx[:, i * P:i * P + P], ident)
                    ins.then_inc(tp, 1)
                    pe.wait_ge(tc, hb + 1)
                    if hb:
                        pe.wait_ge(o_used, 1)
                    for i in range(2):
                        for b4 in range(4):
                            a = 2 * MEM + MEM * i
                            ins = nc.tensor.matmul(ps[32 * b4:32 * b4 + 32, 2, 0:MEM], pxT[:, i, 32 * b4:32 * b4 + 32],
                                                   kv[:, b4, a:a + MEM], start=(i == 0), stop=(i == 1))
                    ins.then_inc(o_ok, 1)
                    pe.wait_ge(ob, hb + 1)
                    for e in range(2):
                        ins = nc.tensor.transpose(ps[:, 3, e * P:e * P + P], sx[:, e * P:e * P + P], ident)
                    ins.then_inc(ot, 1)

            @block.scalar
            def _(act):
                for hb in range(2):
                    act.wait_ge(mx, hb + 1)
                    nc.scalar.activation(sx, ps[:, 0, 0:MEM], ACT.Exp, bias=stat[:, 0:1], accum_out=stat[:, 1:2]).then_inc(ex, 1)

            @block.vector
            def _(dve):
                link = dve_chain(dve)
                link(nc.vector.memset(qxb, 0.0))
                link(nc.vector.memset(oxT[:, :, SEQ:], 0.0))
                for h in range(XH):
                    p = slice(64 * (h % 2), 64 * (h % 2) + 64)
                    ins = nc.vector.tensor_copy(qxb[p, h // 2, :, 4 * h:4 * h + 4],
                                                qxT[p, h // 2, SEQ:TOK].rearrange("p (b t) -> p b t", b=DB))
                    link(ins) if h < XH - 1 else ins.then_inc(q_ok, 1)
                for hb in range(2):
                    dve.wait_ge(s_ok, hb + 1)
                    nc.vector.tensor_reduce(stat[:, 0:1], ps[:, 0, 0:MEM], AX.X, ALU.max, negate=True).then_inc(mx, 1)
                    dve.wait_ge(ex, hb + 1)
                    link(nc.vector.reciprocal(stat[:, 2:3], stat[:, 1:2]))
                    nc.vector.tensor_scalar(sx, sx, stat[:, 2:3], None, ALU.mult).then_inc(pn, 1)
                    dve.wait_ge(tp, hb + 1)
                    nc.vector.tensor_copy(pxT, ps[:, 1, 0:256].rearrange("p (i r) -> p i r", i=2)).then_inc(tc, 1)
                    dve.wait_ge(o_ok, hb + 1)
                    nc.vector.tensor_copy(sx, ps[:, 2, 0:MEM]).then_inc(ob, 1)
                    dve.wait_ge(ot, hb + 1)
                    for h in range(XH):
                        p = slice(64 * (h % 2), 64 * (h % 2) + 64)
                        src = ps[p, 3, P * (h // 2):P * (h // 2) + P].rearrange("p (b w) -> p b w", b=4)[:, :, 4 * h:4 * h + 4]
                        dst = oxT[p, h // 2, SEQ + 16 * hb:SEQ + 16 * hb + 16].rearrange("p (b t) -> p b t", b=4)
                        ins = nc.vector.tensor_copy(dst, src)
                        link(ins) if h < XH - 1 else ins.then_inc(o_used, 1)

        hf = arena[:, 0:FF // P * TOK].rearrange("p (f t) -> p f t", f=FF // P)

        def mlp_hidden(l, arena_stored):
            def relu2(dst, n):
                def f(link, eng, bank):
                    if eng is nc.scalar:
                        link(nc.scalar.activation(dst, bank[:, 0:n], ACT.Relu))
                        return nc.scalar.activation(dst, dst, ACT.Square)
                    link(nc.vector.tensor_scalar(dst, bank[:, 0:n], 0.0, None, ALU.max))
                    return nc.vector.tensor_tensor(dst, dst, dst, ALU.mult)
                return f
            units = []
            for f in range(FF // P):
                name, q = f"w1_{f // 4}", f % 4
                wt = slot(name).rearrange("p (k n) -> p k n", k=KT)
                for part, (a, w) in enumerate(HALVES):
                    mms = [((slice(0, P), w), wt[:, k, q * P:q * P + P], hT[:, k, a:a + w]) for k in range(KT)]
                    units.append((name if q == 0 and part == 0 else None, mms, "ad"[f % 2], relu2(hf[:, f, a:a + w], w),
                                  name if q == 3 and part == 1 else None))
            norm_gemm_stage("mlp1", l, x[:, :, :], TT, 3, units, [(HALVES[i % 2][0] + HALVES[i % 2][1] - 1) // P
                            for i in range(len(units))], arena_stored)

        def mlp_out(l):
            prod, ev, rd = sem("mlp2_products"), sem("mlp2_added"), sem("mlp2_weights_read")
            bank = lambda half, t: (5 * half + t) % 8
            read_at.update({f"w2_{4 * h + c}": (rd, 3 * h + c + 1) if c < 3 else (prod, TT * (h + 1))
                            for h in range(2) for c in range(4)})
            block = new_stage()

            @block.tensor
            def _(pe):
                for half in range(2):
                    for c in range(4):
                        name = f"w2_{4 * half + c}"
                        arrived(pe, name)
                        wt = slot(name).rearrange("p (f n) -> p f n", f=8)
                        for t in range(TT):
                            w = P if t < TP else NS
                            if half and c == 0 and t >= 3:
                                pe.wait_ge(ev, t - 2)
                            groups = 1 if t < TP else 4
                            for f in range(8):
                                g = f % groups
                                ins = nc.tensor.matmul(ps[g * NS:g * NS + w, bank(half, t), :],
                                                       hf[:, 8 * c + f, t * P:t * P + w], wt[:, f, :],
                                                       start=(c == 0 and f < groups), stop=(c == 3 and f >= 8 - groups))
                            if c == 3:
                                ins.then_inc(prod, 1)
                        if c < 3:
                            ins.then_inc(rd, 1)

            @block.scalar
            def _(act):
                load_parameters(act, l + 1, prm_ld)
                act.wait_ge(prm_ld, 32)

            @block.vector
            def _(dve):
                link = dve_chain(dve)
                for half in range(2):
                    for t in range(TT):
                        dve.wait_ge(prod, 5 * half + t + 1)
                        half_cols = slice(512 * half, 512 * half + 512)
                        add = add_to(x[:, t, half_cols], 512) if t < TP else sum_groups(x[0:NS, TP, half_cols], 512, onto=True)
                        add(link, nc.vector, ps[:, bank(half, t), :]).then_inc(ev, 1)

        first, done = whole("inputs_loaded"), whole("tokens_stored")
        with nc.Block() as block:
            @block.sync
            def _(sp):
                sp.dma_start(pages[:, :], din["pages"]).then_inc(first, 16)
                sp.dma_start(cst[:, :], din["consts"]).then_inc(first, 16)
                sp.dma_start(x[:, :, :], din["x"]).then_inc(first, 16)
                sp.dma_start(gpage[:, :], din["gather"]).then_inc(first, 16)
                load_parameters(sp, 0, first)
                sp.wait_ge(first, 96)

            @block.vector
            def _(dve):
                dve.wait_ge(first, 96)
                link = idx_chain(dve)
                link(nc.vector.tensor_scalar(row[:, :], gpage[:, 0:DB], 8, -8 * POOL, ALU.mult, ALU.add))
                link(nc.vector.tensor_tensor(row[:, :], row[:, :], gpage[:, DB:2 * DB], ALU.add))

        def output_projection(l):
            units = []
            for c in range(2):
                wt = slot(f"w_out{c}").rearrange("p (k n) -> p k n", k=KT)
                for t in range(TT):
                    act_tile = lambda k, t=t: (z[:, t, ZQ + P * k:ZQ + P * k + P] if k < 4 and t < TP else
                                               hT[:, k, t * P:t * P + P])
                    mms = token_products(t, act_tile, KT, lambda k: wt[:, k, :], 512)
                    a = 512 * c
                    units.append((f"w_out{c}" if t == 0 else None, mms, "d",
                                  add_to(x[:, t, a:a + 512], 512) if t < TP else sum_groups(x[0:NS, TP, a:a + 512], 512, onto=True),
                                  f"w_out{c}" if t == TT - 1 else None))


            def load_memory(act):
                act.dma_start(memx, din["mem"]).then_inc(mem_ld, 16)
                act.wait_ge(kv_st, 16 * KV_STORES)
            gemm_stage("out", l, units, load_memory, lambda act: act.wait_ge(mem_ld, 16))

        def cross_queries(l):
            wq = slot("wqo")[:, 0:2048].rearrange("p (k n) -> p k n", k=KT)
            norm_gemm_stage("wq", l, x[:, :, :], TT, 1, [("wqo" if t == 0 else None,
                                  token_products(t, tile_of(hT, t), KT, lambda k: wq[:, k, :], 256), "d" if t == TP else "ad"[t % 2],
                                  copy_to(zx[:, t, :], 256) if t < TP else sum_groups(zx[0:NS, TP, :], 256), None) for t in range(TT)], list(range(TT)),
                            padding=zx[:, TP, :])

        def cross_output(l):
            wo = slot("wqo")[:, 2048:4096].rearrange("p (k n) -> p k n", k=2)
            units = []
            for t in range(TT):
                for c in range(2):
                    a = 512 * c
                    mms = token_products(t, tile_of(oxT, t), 2, lambda k: wo[:, k, a:a + 512], 512)
                    units.append((None, mms, "d", add_to(x[:, t, a:a + 512], 512) if t < TP else
                                  sum_groups(x[0:NS, TP, a:a + 512], 512, groups=2, onto=True),
                                  "wqo" if (t, c) == (TT - 1, 1) else None))
            gemm_stage("wo", l, units)

        def run_half(l, loads, begin):
            with nc.Block() as block:
                @block.sync
                def _(sp):
                    fill_ring(sp, l, loads)
                    if begin:
                        for s, n in ((win_moved, DB), (kv_st, KV_STORES), (conv_st, 1), (m_st, 1), (ctp_st, 1),
                                     (cts_st, CTS_STORES), (mem_st, 1)):
                            sp.wait_ge(s, 16 * n)

                @block.gpsimd
                def _(pool):
                    if not begin:
                        gather_pages(pool, l)

                @block.tensor
                def _(pe):
                    for k in range(begin, len(stages)):
                        if "pe" in stages[k].parts:
                            stages[k].parts["pe"](pe)
                        meet(pe, "pe", k + 1)

                @block.scalar
                def _(act):
                    for k in range(begin, len(stages)):
                        if "act" in stages[k].parts:
                            stages[k].parts["act"](act)
                        meet(act, "act", k + 1)

                @block.vector
                def _(dve):
                    if not begin:
                        nc.vector.tensor_scalar(row[:, :], row[:, :], 8 * POOL, None, ALU.add).then_inc(idx_ok, 1)
                    for k in range(begin, len(stages)):
                        if "dve" in stages[k].parts:
                            stages[k].parts["dve"](dve)
                        meet(dve, "dve", k + 1)

        def clear(sems):
            with nc.Block() as block:
                @block.gpsimd
                def _(pool):
                    for s in sems[0::4]:
                        pool.sem_clear(s)

                @block.scalar
                def _(act):
                    for s in sems[1::4]:
                        act.sem_clear(s)

                @block.vector
                def _(dve):
                    for s in sems[2::4]:
                        dve.sem_clear(s)

                @block.tensor
                def _(pe):
                    for s in sems[3::4]:
                        pe.sem_clear(s)

        with nc.Fori(0, DEPTH) as l:
            def arena_stored(act):
                for s, n in ((m_st, 1), (ctp_st, 1), (mem_st, 1)):
                    act.wait_ge(s, 16 * n)

            input_projection(l)
            post_stage(l)
            prompt_mlstm(l)
            sample_mlstm(l)
            finish_mlstm(l)
            prep_stage(l)
            prompt_compress(l)
            prompt_attention(l)
            sample_attention(l, 0)
            sample_attention(l, 1)
            sample_merge(l)
            turn_stage("mix", l, TT, lambda t: [z[:, t, ZO + P * k:ZO + P * k + P] for k in range(4)], hT[:, 4:8, :])
            turn_stage("mixs", l, 1, lambda t: [z[:, TP, ZQ + P * k:ZQ + P * k + P] for k in range(4)],
                       hT[:, 0:4, SEQ:])
            output_projection(l)
            stages_before = len(stages)
            run_half(l, FIRST_LOADS, 0)
            clear(half["sems"])
            half["held"].close()
            half["held"], half["sems"] = ExitStack(), []
            memory_kv(l)
            head_norm_stage("memk", l, zm[:, :, 0:256].rearrange("p t (h d) -> p t h d", h=XH), pr("xk"),
                            xsq[:, 0:512].rearrange("p (t h d) -> p t h d", t=MT, h=XH), lambda act: load_gain(act, l, 1))
            turn_stage("memT", l, MT, lambda t: [zm[:, t, P * e:P * e + P] for e in range(2)], kmT,
                       act_first=lambda act: store_memory(act, l))
            cross_queries(l)
            head_norm_stage("xprep", l, zx.rearrange("p t (h d) -> p t h d", h=XH), pr("xq"),
                            xsq.rearrange("p (t h d) -> p t h d", t=TT, h=XH), lambda act: load_gain(act, l, 3))
            turn_stage("xqT", l, TT, lambda t: [zx[:, t, P * e:P * e + P] for e in range(2)], qxT, QSC)
            tile_attention("xatt", l, 2, [
                (qxT[64 * g:64 * g + 64, e, t * P:t * P + P], kmT[64 * g:64 * g + 64, e, :], MEM, False,
                 [zm[:, i, 256 + 128 * e + 64 * g:320 + 128 * e + 64 * g] for i in range(MT)], None)
                for t in range(TP) for e in range(2) for g in range(2)],
                [oxT[:, e, t * P:t * P + P] for t in range(TP) for e in range(2)], False)
            cross_samples(l)
            cross_output(l)
            mlp_hidden(l, arena_stored)
            mlp_out(l)
            run_half(l, SECOND_LOADS, stages_before)
            clear(half["sems"] + layer_sems)

        with nc.Block() as block:
            @block.sync
            def _(sp):
                sp.dma_start(dout["y"], x[:, :, :]).then_inc(done, 16)
                sp.wait_ge(done, 16)
    return nc


def constants():
    c = np.zeros((P, NCST), np.float32)
    put = lambda n, a: c.__setitem__((slice(0, a.shape[0]), slice(*CST[n])), a)
    p = np.arange(P)
    put("id", np.eye(P, dtype=np.float32))
    put("causal", np.where(p[None, :] <= p[:, None], 0.0, NEG).astype(np.float32))
    put("tri", (p[:, None] <= p[None, :]).astype(np.float32))
    half = HD // 8
    freqs = np.float32(500000.0) ** (-np.arange(half, dtype=np.float32) / np.float32(half))
    pos = np.zeros((TT, P), np.float32)
    pos[:TP] = np.arange(SEQ).reshape(TP, P)
    pos[TP, :NS] = PAST + np.arange(NS) % DS
    ang = (pos[:, :, None] * freqs.astype(np.float32)).astype(np.float32)
    put("cos", np.cos(ang).transpose(1, 0, 2).reshape(P, -1))
    put("sin", np.sin(ang).transpose(1, 0, 2).reshape(P, -1))
    end = np.arange(NC_P) * STRIDE + CMP_LEN - 1
    seen = (end[None, None, :] <= (np.arange(TP)[None, :, None] * P + p[:, None, None]))
    put("cma", np.where(seen, 0.0, NEG).reshape(P, -1))
    put("cmm", seen.astype(np.float32).reshape(P, -1))
    tok = np.arange(NS)
    b4, t = p // 32, p % DS
    new = np.stack([((tok[None, :] // DS == 4 * hb + b4[:, None]) & (tok[None, :] % DS <= t[:, None])) for hb in range(2)], 1)
    put("new", np.where(new, 0.0, NEG).reshape(P, -1))
    put("low", np.where(np.arange(4)[None, :] >= t[:, None], 0.0, NEG))
    put("ms", ((tok[:, None] // DS == tok[None, :] // DS) & (tok[:, None] <= tok[None, :])).astype(np.float32))
    put("ohb", (tok[:, None] // DS == np.arange(DB)[None, :]).astype(np.float32))
    key = (p // 16) * DS + t
    put("grp", (key[:, None] == key[None, :]).astype(np.float32))
    put("one", np.ones((P, 1), np.float32))
    return c


def lay_out(x_prompt, x_sample, mem_prompt, cache_nsa_kv, cache_win_kv, cache_mem_kv, state_mlstm_C, state_mlstm_n,
            state_mlstm_m, state_conv, page_table, norm_mix_g, w_in, nsa_qn_g, nsa_kn_g, cmp_pos, cmp_w1, cmp_w2,
            ml_conv_w, ml_conv_b, ml_gate_b, ml_hn_g, w_out, norm_xa_g, norm_mem_g, xa_wq, xa_wkv, xa_qn_g, xa_kn_g,
            xa_wo, norm_mlp_g, mlp_w1, mlp_w2):
    L = DEPTH
    a = {}
    xs = np.zeros((P, D), np.float32)
    xs[:NS] = x_sample.reshape(NS, D)
    a["x"] = np.concatenate([x_prompt.reshape(TP, P, D), xs[None]]).transpose(1, 0, 2)
    a["mem"] = mem_prompt.reshape(MT, P, D).transpose(1, 0, 2)
    a["pages"] = page_table.reshape(1, DB * NPG)
    eighth = np.broadcast_to((np.arange(P) % 8)[:, None], (P, DB)).astype(page_table.dtype)
    a["gather"] = np.concatenate([np.repeat(page_table, 8, axis=1).T, eighth], 1)
    a["consts"] = constants()
    gains = np.stack([norm_mix_g, norm_xa_g, norm_mem_g, norm_mlp_g], 1).reshape(L * 4, 1, D)
    a["gains"] = np.broadcast_to(np.concatenate([gains, gains[:4]]), (L * 4 + 4, P, D))
    pm = np.zeros((L, P, NPRM), np.float32)

    def put(n, v, rows=P):
        pm[:, :rows, slice(*PRM[n])] = v
    put("qn", nsa_qn_g[:, None, :])
    put("kn", nsa_kn_g.reshape(L, 1, 192))
    put("hn", ml_hn_g[:, None, :])
    put("xq", xa_qn_g[:, None, :])
    put("xk", xa_kn_g[:, None, :])
    put("cw", ml_conv_w.reshape(L, 4, KT, P).transpose(0, 3, 2, 1).reshape(L, P, 32))
    put("cb", ml_conv_b.reshape(L, KT, P).transpose(0, 2, 1))
    put("bi", ml_gate_b[:, :MH, None], MH)
    put("bf", ml_gate_b[:, MH:, None], MH)
    put("w2", cmp_w2.transpose(0, 2, 1, 3).reshape(L, P, 128))
    put("pos", cmp_pos.reshape(L, 2, J, P).transpose(0, 3, 1, 2).reshape(L, P, 32))
    a["prm"] = np.concatenate([pm, pm[:1]])
    cols = lambda w, k: w.reshape(L, k, P, -1).transpose(0, 2, 1, 3)
    q, kv, g, qk, v, o, f = np.split(w_in, np.cumsum([512, 768, 24, 1024, 512, 512]).tolist(), axis=-1)
    q = q.reshape(L, D, G, HG, HD).transpose(0, 1, 3, 2, 4).reshape(L, D, 512)
    g = g.reshape(L, D, G, HG, 3).transpose(0, 1, 3, 2, 4).reshape(L, D, 24)
    wa = w_out[:, :512].reshape(L, G, HG, HD, D).transpose(0, 2, 1, 3, 4).reshape(L, 512, D)
    w_out = np.concatenate([wa, w_out[:, 512:]], 1)
    wi = cols(np.concatenate([q, kv, v, o, g, f], -1), KT)
    wqk, wo_, w1, w2 = cols(qk, KT), cols(w_out, KT), cols(mlp_w1, KT), cols(mlp_w2, FF // P)
    ch = {f"in{i}": wi[..., NZ * i:NZ * i + NZ] for i in range(5)}
    for i in range(2):
        ch[f"qk{i}"] = wqk[..., 512 * i:512 * i + 512]
        ch[f"w_out{i}"] = wo_[..., 512 * i:512 * i + 512]
    ch["cmpw"] = cmp_w1.reshape(L, 2, J, P, HID).transpose(0, 3, 1, 2, 4)
    ch["wkv"] = cols(xa_wkv, KT)
    ch["wqo"] = np.concatenate([cols(xa_wq, KT).reshape(L, P, -1), cols(xa_wo, 2).reshape(L, P, -1)], -1)
    for i in range(8):
        ch[f"w1_{i}"] = w1[..., 512 * i:512 * i + 512]
        ch[f"w2_{i}"] = w2[:, :, 8 * (i % 4):8 * (i % 4) + 8, 512 * (i // 4):512 * (i // 4) + 512]
    a["wst"] = np.concatenate([ch[n].reshape(L, -1) for n, _ in CHUNKS], 1)
    c = cache_nsa_kv.reshape(POOL, PAGE // 2, 2, L, 4, G, HD)
    a["cx"] = c[:, :, :, :, 0:2].transpose(3, 0, 2, 6, 1, 4, 5).reshape(L * POOL, P, 256)
    c = cache_nsa_kv.reshape(POOL * 8, 16, L, 4, P)
    a["kx"] = c[:, :, :, 2].transpose(2, 0, 1, 3).reshape(L * POOL * 8, 2048)
    a["vx"] = c[:, :, :, 3].transpose(2, 0, 1, 3).reshape(L * POOL * 8, 2048)
    w = cache_win_kv.reshape(L * DB, WIN, 2 * P)
    a["win"] = w
    a["winT"] = w[:, :, 0:P].transpose(0, 2, 1)
    m = cache_mem_kv.reshape(L, 2, 4, MEM, 2, 2, P)
    k_ = m[:, :, :, :, 0].transpose(0, 1, 5, 2, 4, 3)
    v_ = m[:, :, :, :, 1].reshape(L, 2, 4, MT, P, 2, P).transpose(0, 1, 4, 2, 3, 5, 6)
    a["mkv"] = np.concatenate([k_.reshape(L, 2, P, 4, 512), v_.reshape(L, 2, P, 4, 512)], -1).reshape(L * 2, P, 4096)
    a["cT"] = state_mlstm_C.transpose(0, 4, 2, 1, 3).reshape(L, P, 4096)
    a["nT"] = state_mlstm_n.transpose(0, 3, 2, 1).reshape(L, P, MH * DB)
    a["mT"] = state_mlstm_m.transpose(0, 2, 1)
    a["convT"] = state_conv.reshape(L, DB, 3, KT, P).transpose(0, 4, 3, 1, 2).reshape(L, P, KT * DB * 3)
    return {n: np.ascontiguousarray(v) for n, v in a.items()}


OUTS = {
    "y": (P, TT, D), "nsa_p": (DEPTH, P, TP, 512), "nsa_s": (DEPTH, NS, 512), "win_p": (DEPTH, P, TP, 256),
    "win_s": (DEPTH * DB, WIN, 256), "convT": (DEPTH, P, KT, NS + 3), "mT": (DEPTH, MH, TOK),
    "cT_p": (DEPTH, P, MH, 129), "cT_s": (DEPTH, P, 4096), "nT": (DEPTH, P, MH * DB), "mem": (DEPTH, P, MT, 512),
}


def kernel(**inputs):
    import concourse.bacc as _bacc
    from concourse.bass_utils import run_bass_kernel_spmd as _run

    arrays = lay_out(**{n: np.asarray(v) for n, v in inputs.items()})
    nc = _bacc.Bacc("TRN2", target_bir_lowering=False, num_devices=1)
    din = {n: nc.dram_tensor(f"in_{n}", v.shape, mybir.dt.from_np(v.dtype), kind="ExternalInput").ap()
           for n, v in arrays.items()}
    dout = {n: nc.dram_tensor(f"out_{n}", s, F32, kind="ExternalOutput").ap() for n, s in OUTS.items()}
    build(nc, din, dout)
    r = _run(nc, [{f"in_{n}": v for n, v in arrays.items()}], core_ids=[0])
    o = {n: np.asarray(r.results[0][f"out_{n}"]) for n in OUTS}
    L = DEPTH
    rows = o["y"].transpose(1, 0, 2)
    tok = lambda n, w: o[n].transpose(0, 2, 1, 3).reshape(L, SEQ, w)
    ct = o["cT_p"]
    cs_ = o["cT_s"].reshape(L, P, MH, DB, MD)
    cv = o["convT"]
    return (
        rows[:TP].reshape(1, SEQ, D), rows[TP, :NS].reshape(DB, DS, D),
        tok("nsa_p", 512).transpose(1, 0, 2).reshape(1, SEQ, L, 4, G, HD),
        o["nsa_s"].reshape(L, DB, DS, 4, G, HD).transpose(1, 2, 0, 3, 4, 5),
        tok("win_p", 256).reshape(L, 1, WIN, 2, G, HD),
        o["win_s"].reshape(L, DB, WIN, 2, G, HD),
        ct[..., 0:MD].transpose(0, 2, 3, 1).reshape(L, 1, MH, MD, MD),
        cs_.transpose(0, 3, 2, 4, 1),
        ct[..., MD].transpose(0, 2, 1).reshape(L, 1, MH, MD),
        o["nT"].reshape(L, MD, MH, DB).transpose(0, 3, 2, 1),
        o["mT"][:, :, SEQ - 1].reshape(L, 1, MH),
        o["mT"][:, :, SEQ + DS - 1::DS].transpose(0, 2, 1),
        cv[..., 0:3].transpose(0, 3, 2, 1).reshape(L, 1, 3, KT * P),
        cv[..., 3:].reshape(L, P, KT, DB, DS)[..., 1:].transpose(0, 3, 4, 2, 1).reshape(L, DB, 3, KT * P),
        o["mem"].transpose(0, 2, 1, 3).reshape(L, 1, MEM, 2, XH, HD),
    )
```
